# Optimizing a Trainium2 kernel written in Bass

```python
import math
import jax, jax.numpy as jnp
from jax import lax
import numpy as np
import jax
import jax.numpy as jnp

D_MODEL = 1024
BATCH = 1
SEQ = 256
DEPTH = 4

N_MIXERS = 3
EPS = 1e-6
D_FF = -(-8 * D_MODEL // (3 * 256)) * 256
FOURIER_GROUP = 128
N_FOURIER_GROUPS = D_MODEL // FOURIER_GROUP
S5_GROUP = 16
S5_GROUPS = D_MODEL // S5_GROUP
S5_STATE = 64
S5_DT_MIN = 1e-3
S5_DT_MAX = 1e-1
HEAD_DIM = 64
HEADS_PER_GROUP = D_MODEL // HEAD_DIM
DILATED_GROUPS = ((128, 1), (512, 4), (2048, 16))
N_ATTN_GROUPS = len(DILATED_GROUPS)
N_ATTN_HEADS = N_ATTN_GROUPS * HEADS_PER_GROUP
QKV_WIDTH = N_ATTN_GROUPS * 3 * HEADS_PER_GROUP * HEAD_DIM
ATTN_OUT = HEADS_PER_GROUP * HEAD_DIM
NUM_BUCKETS = 32
MAX_DISTANCE = 1024
N_LAYERS_A = (DEPTH + 2) // 3
N_LAYERS_B = (DEPTH + 1) // 3
N_LAYERS_C = DEPTH // 3


def rms_norm(x, g):
    xf = x.astype(jnp.float32)
    y = xf * lax.rsqrt(jnp.mean(xf * xf, axis=-1, keepdims=True) + EPS)
    return (y * g.astype(jnp.float32)).astype(x.dtype)

def swiglu(h, w_gate_up, w_down):
    gate, up = jnp.split(h @ w_gate_up, 2, axis=-1)
    return (jax.nn.silu(gate) * up) @ w_down

def fourier_mixer(h, w_out):
    b, s, d = h.shape
    hg = h.astype(jnp.float32).reshape(b, s, N_FOURIER_GROUPS, FOURIER_GROUP)
    f = jnp.fft.fft2(hg, axes=(1, 3), norm="ortho").real
    return f.reshape(b, s, d).astype(h.dtype) @ w_out

def _s5_direction(u, lam_re, lam_im, log_dt, b_re, b_im, c_re, c_im, reverse):
    f32 = jnp.float32
    lam = lax.complex(lam_re.astype(f32), lam_im.astype(f32))
    dt = jnp.exp(log_dt.astype(f32))[:, None]
    lam_bar = jnp.exp(lam * dt)
    b_bar = ((lam_bar - 1.0) / lam)[..., None] * lax.complex(b_re.astype(f32), b_im.astype(f32))
    bu = lax.complex(jnp.einsum('bsgp,gnp->bsgn', u, b_bar.real),
                     jnp.einsum('bsgp,gnp->bsgn', u, b_bar.imag))
    a = jnp.broadcast_to(lam_bar, bu.shape)

    def combine(e1, e2):
        a1, x1 = e1
        a2, x2 = e2
        return a1 * a2, a2 * x1 + x2

    _, hs = lax.associative_scan(combine, (a, bu), axis=1, reverse=reverse)
    c = lax.complex(c_re.astype(f32), c_im.astype(f32))
    return jnp.einsum('gpn,bsgn->bsgp', c, hs).real

def s5_mixer(h, lam_re, lam_im, log_dt, b_re, b_im, c_re, c_im, d_skip, w_glu):
    b, s, d = h.shape
    hf = h.astype(jnp.float32)
    u = hf.reshape(b, s, S5_GROUPS, S5_GROUP)
    y_fwd = _s5_direction(u, lam_re[0], lam_im[0], log_dt[0], b_re[0], b_im[0], c_re[0], c_im[0], False)
    y_bwd = _s5_direction(u, lam_re[1], lam_im[1], log_dt[1], b_re[1], b_im[1], c_re[1], c_im[1], True)
    y = (y_fwd + y_bwd).reshape(b, s, d) + d_skip.astype(jnp.float32) * hf
    g = jax.nn.gelu(y).astype(h.dtype)
    val, gate = jnp.split(g @ w_glu, 2, axis=-1)
    return val * jax.nn.sigmoid(gate)

def t5_bucket(rel):
    half = NUM_BUCKETS // 2
    max_exact = half // 2
    n = np.abs(rel)
    sign = (rel > 0).astype(np.int32) * half
    large = max_exact + (np.log(np.maximum(n, 1) / max_exact) / math.log(MAX_DISTANCE / max_exact)
                         * (half - max_exact)).astype(np.int32)
    large = np.minimum(large, half - 1)
    return (sign + np.where(n < max_exact, n, large)).astype(np.int32)

def head_rms_norm(t, g):
    tf = t.astype(jnp.float32)
    y = tf * lax.rsqrt(jnp.mean(tf * tf, axis=-1, keepdims=True) + EPS)
    return (y * g.astype(jnp.float32)).astype(t.dtype)

def dilated_group_attention(q, k, v, bias_g, dil, n_side):
    bsz, s, nh, e = q.shape
    seg = s // dil
    blk = n_side
    nb = -(-seg // blk)
    segp = nb * blk

    def res(t):
        return t.reshape(bsz, seg, dil, nh, e).transpose(0, 2, 1, 3, 4)

    qb = jnp.pad(res(q), ((0, 0), (0, 0), (0, segp - seg), (0, 0), (0, 0))).reshape(bsz, dil, nb, blk, nh, e)

    def kv_blocks(t):
        tp = jnp.pad(res(t), ((0, 0), (0, 0), (blk, segp - seg + blk), (0, 0), (0, 0)))
        tp = tp.reshape(bsz, dil, nb + 2, blk, nh, e)
        return jnp.concatenate([tp[:, :, :-2], tp[:, :, 1:-1], tp[:, :, 2:]], axis=3)

    kb = kv_blocks(k)
    vb = kv_blocks(v)
    qi = np.arange(blk)[:, None]
    ki = np.arange(3 * blk)[None, :]
    off = ki - blk - qi
    band = np.abs(off) <= n_side
    key_idx = np.arange(nb)[:, None] * blk + np.arange(3 * blk)[None, :] - blk
    in_range = (key_idx >= 0) & (key_idx < seg)
    allowed = band[None] & in_range[:, None, :]
    buckets = t5_bucket(off * dil)
    bias = jnp.transpose(bias_g.astype(jnp.float32)[buckets], (2, 0, 1))

    sc = jnp.einsum('brnqhe,brnkhe->brnhqk', qb, kb, preferred_element_type=jnp.float32) * (e ** -0.5)
    sc = jnp.where(allowed[None, None, :, None], sc + bias, -1e30)
    m = jnp.max(sc, axis=-1, keepdims=True)
    p = jnp.exp(sc - m)
    den = jnp.sum(p, axis=-1, keepdims=True)
    o = jnp.einsum('brnhqk,brnkhe->brnqhe', (p / den).astype(v.dtype), vb)
    lse = (m + jnp.log(den))[..., 0]
    o = o.reshape(bsz, dil, segp, nh, e)[:, :, :seg].transpose(0, 2, 1, 3, 4).reshape(bsz, s, nh, e)
    lse = lse.transpose(0, 1, 2, 4, 3).reshape(bsz, dil, segp, nh)[:, :, :seg]
    lse = lse.transpose(0, 2, 1, 3).reshape(bsz, s, nh)
    return o, lse

def dilated_attention_mixer(h, w_qkv, q_gain, k_gain, w_o, rel_bias):
    b, s, d = h.shape
    qkv = (h @ w_qkv).reshape(b, s, N_ATTN_GROUPS, 3, HEADS_PER_GROUP, HEAD_DIM)
    outs = []
    lses = []
    for g, (window, dil) in enumerate(DILATED_GROUPS):
        q = head_rms_norm(qkv[:, :, g, 0], q_gain[g])
        k = head_rms_norm(qkv[:, :, g, 1], k_gain[g])
        v = qkv[:, :, g, 2]
        bias_g = rel_bias[:, g * HEADS_PER_GROUP:(g + 1) * HEADS_PER_GROUP]
        o, l = dilated_group_attention(q, k, v, bias_g, dil, (window // 2) // dil)
        outs.append(o)
        lses.append(l)
    wts = jax.nn.softmax(jnp.stack(lses, axis=0), axis=0)
    o = jnp.einsum('gbsh,gbshe->bshe', wts, jnp.stack(outs, axis=0).astype(jnp.float32))
    return o.reshape(b, s, ATTN_OUT).astype(h.dtype) @ w_o

def first_inputs(seed: int = 0) -> dict:
    key = jax.random.key(seed)
    ks = jax.random.split(key, 24)
    f32 = jnp.float32
    d = D_MODEL

    def nrm(k, shape, scale):
        return jax.random.normal(k, shape, f32) * scale

    s5_shape = (N_LAYERS_B, 2, S5_GROUPS, S5_STATE)
    n_idx = jnp.arange(S5_STATE, dtype=f32)
    return {
        "x": nrm(ks[0], (BATCH, SEQ, d), 1.0),
        "norm_mix_g": 1.0 + nrm(ks[1], (DEPTH, d), 0.1),
        "norm_ffn_g": 1.0 + nrm(ks[2], (DEPTH, d), 0.1),
        "fnet_w_out": nrm(ks[3], (N_LAYERS_A, d, d), d ** -0.5),
        "s5_lambda_re": -0.5 + nrm(ks[4], s5_shape, 0.01),
        "s5_lambda_im": math.pi * n_idx + nrm(ks[5], s5_shape, 0.01),
        "s5_log_dt": jax.random.uniform(ks[6], (N_LAYERS_B, 2, S5_GROUPS), f32,
                                        math.log(S5_DT_MIN), math.log(S5_DT_MAX)),
        "s5_b_re": nrm(ks[7], (N_LAYERS_B, 2, S5_GROUPS, S5_STATE, S5_GROUP), (2 * S5_GROUP) ** -0.5),
        "s5_b_im": nrm(ks[8], (N_LAYERS_B, 2, S5_GROUPS, S5_STATE, S5_GROUP), (2 * S5_GROUP) ** -0.5),
        "s5_c_re": nrm(ks[9], (N_LAYERS_B, 2, S5_GROUPS, S5_GROUP, S5_STATE), S5_STATE ** -0.5),
        "s5_c_im": nrm(ks[10], (N_LAYERS_B, 2, S5_GROUPS, S5_GROUP, S5_STATE), S5_STATE ** -0.5),
        "s5_d": nrm(ks[11], (N_LAYERS_B, d), 1.0),
        "s5_w_glu": nrm(ks[12], (N_LAYERS_B, d, 2 * d), d ** -0.5),
        "attn_w_qkv": nrm(ks[13], (N_LAYERS_C, d, QKV_WIDTH), d ** -0.5),
        "attn_q_gain": 1.0 + nrm(ks[14], (N_LAYERS_C, N_ATTN_GROUPS, HEAD_DIM), 0.1),
        "attn_k_gain": 1.0 + nrm(ks[15], (N_LAYERS_C, N_ATTN_GROUPS, HEAD_DIM), 0.1),
        "attn_w_o": nrm(ks[16], (N_LAYERS_C, ATTN_OUT, d), ATTN_OUT ** -0.5),
        "rel_bias": nrm(ks[17], (NUM_BUCKETS, N_ATTN_HEADS), 0.5),
        "ffn_w_gate_up": nrm(ks[18], (DEPTH, d, 2 * D_FF), d ** -0.5),
        "ffn_w_down": nrm(ks[19], (DEPTH, D_FF, d), D_FF ** -0.5),
    }

def first_block(x, norm_mix_g, norm_ffn_g, fnet_w_out, s5_lambda_re, s5_lambda_im, s5_log_dt,
              s5_b_re, s5_b_im, s5_c_re, s5_c_im, s5_d, s5_w_glu, attn_w_qkv, attn_q_gain,
              attn_k_gain, attn_w_o, rel_bias, ffn_w_gate_up, ffn_w_down):
    counts = [0, 0, 0]
    for i in range(DEPTH):
        kind = i % N_MIXERS
        j = counts[kind]
        counts[kind] += 1
        h = rms_norm(x, norm_mix_g[i])
        if kind == 0:
            mix = fourier_mixer(h, fnet_w_out[j])
        elif kind == 1:
            mix = s5_mixer(h, s5_lambda_re[j], s5_lambda_im[j], s5_log_dt[j], s5_b_re[j], s5_b_im[j],
                           s5_c_re[j], s5_c_im[j], s5_d[j], s5_w_glu[j])
        else:
            mix = dilated_attention_mixer(h, attn_w_qkv[j], attn_q_gain[j], attn_k_gain[j],
                                          attn_w_o[j], rel_bias)
        x = x + mix.astype(x.dtype)
        h = rms_norm(x, norm_ffn_g[i])
        x = x + swiglu(h, ffn_w_gate_up[i], ffn_w_down[i]).astype(x.dtype)
    return x


DEPTH_2 = 2

N_EVEN = (DEPTH_2 + 1) // 2
N_ODD = DEPTH_2 // 2

NORM_EPS = 1e-6

RG_W = D_MODEL
RG_BLOCKS = 8
RG_BLOCK_W = RG_W // RG_BLOCKS
RG_C = 8.0
CONV_WIDTH = 4

MLA_HEADS = 8
MLA_NOPE = 128
MLA_ROPE = 64
MLA_V = 128
MLA_QK = MLA_NOPE + MLA_ROPE
Q_LORA = 512
KV_LORA = 256
ROPE_THETA = 10000.0
Q_BLOCK = 128

HY_SIZES = (RG_W, RG_W, Q_LORA, KV_LORA, MLA_ROPE)
HY_IN = RG_W + RG_W + Q_LORA + KV_LORA + MLA_ROPE
HY_SPLITS = [RG_W, 2 * RG_W, 2 * RG_W + Q_LORA, 2 * RG_W + Q_LORA + KV_LORA]
HY_MIX = RG_W + MLA_HEADS * MLA_V

GDN_K_HEADS = 8
GDN_V_HEADS = 16
GDN_HEAD_DIM = 128
GDN_QK_W = GDN_K_HEADS * GDN_HEAD_DIM
GDN_V_W = GDN_V_HEADS * GDN_HEAD_DIM
GDN_CONV_W = 2 * GDN_QK_W + GDN_V_W
GDN_IN = GDN_CONV_W + GDN_V_W + 2 * GDN_V_HEADS
GDN_SPLITS = [GDN_CONV_W, GDN_CONV_W + GDN_V_W, GDN_CONV_W + GDN_V_W + GDN_V_HEADS]
GDN_CHUNK = 64

FFN_HIDDEN = -(-8 * D_MODEL // (3 * 256)) * 256


def rms_norm_2(x, w):
    xf = x.astype(jnp.float32)
    y = xf * lax.rsqrt(jnp.mean(xf * xf, axis=-1, keepdims=True) + NORM_EPS)
    return (y * w.astype(jnp.float32)).astype(x.dtype)

def l2_norm(x):
    xf = x.astype(jnp.float32)
    return xf * lax.rsqrt(jnp.sum(xf * xf, axis=-1, keepdims=True) + NORM_EPS)

def causal_depthwise_conv(x, w):
    width, chans = w.shape
    return lax.conv_general_dilated(
        x, w[:, None, :].astype(x.dtype), window_strides=(1,),
        padding=((width - 1, 0),), dimension_numbers=("NWC", "WIO", "NWC"),
        feature_group_count=chans)

def rope_tables(positions):
    inv_freq = 1.0 / (ROPE_THETA ** (jnp.arange(0, MLA_ROPE, 2, dtype=jnp.float32) / MLA_ROPE))
    ang = positions.astype(jnp.float32)[..., None] * inv_freq
    return jnp.cos(ang), jnp.sin(ang)

def apply_rope(x, cos, sin):
    half = x.shape[-1] // 2
    c = cos[:, :, None, :].astype(x.dtype)
    s = sin[:, :, None, :].astype(x.dtype)
    x1, x2 = x[..., :half], x[..., half:]
    return jnp.concatenate([x1 * c - x2 * s, x2 * c + x1 * s], axis=-1)

def causal_block_attention(q, k, v, scale):
    T = q.shape[1]
    outs = []
    for start in range(0, T, Q_BLOCK):
        end = min(start + Q_BLOCK, T)
        qb, kb, vb = q[:, start:end], k[:, :end], v[:, :end]
        s = jnp.einsum('bqhd,bkhd->bhqk', qb, kb).astype(jnp.float32) * scale
        mask = (start + jnp.arange(end - start))[:, None] >= jnp.arange(end)[None, :]
        p = jax.nn.softmax(jnp.where(mask, s, -jnp.inf), axis=-1).astype(v.dtype)
        outs.append(jnp.einsum('bhqk,bkhd->bqhd', p, vb))
    return jnp.concatenate(outs, axis=1)

def _lru_combine(e1, e2):
    a1, b1 = e1
    a2, b2 = e2
    return a1 * a2, a2 * b1 + b2

def rglru_branch(x_r, gate_r, conv_w, conv_b, gate_a_w, gate_a_b, gate_x_w, gate_x_b, lam):
    B, T, _ = x_r.shape
    xc = causal_depthwise_conv(x_r, conv_w) + conv_b.astype(x_r.dtype)
    xb = xc.reshape(B, T, RG_BLOCKS, RG_BLOCK_W)
    r = jax.nn.sigmoid((jnp.einsum('btni,nij->btnj', xb, gate_a_w).reshape(B, T, RG_W)
                        + gate_a_b).astype(jnp.float32))
    i = jax.nn.sigmoid((jnp.einsum('btni,nij->btnj', xb, gate_x_w).reshape(B, T, RG_W)
                        + gate_x_b).astype(jnp.float32))
    log_a = -RG_C * r * jax.nn.softplus(-lam.astype(jnp.float32))
    a = jnp.exp(log_a)
    b = jnp.sqrt(-jnp.expm1(2.0 * log_a)) * (i * xc.astype(jnp.float32))
    _, h = lax.associative_scan(_lru_combine, (a, b), axis=1)
    return h.astype(x_r.dtype) * jax.nn.gelu(gate_r)

def mla_branch(c_q, c_kv, k_pe, cos, sin, q_norm, w_uq, kv_norm, w_ukv):
    B, T, _ = c_q.shape
    q = (rms_norm_2(c_q, q_norm) @ w_uq).reshape(B, T, MLA_HEADS, MLA_QK)
    q = jnp.concatenate([q[..., :MLA_NOPE], apply_rope(q[..., MLA_NOPE:], cos, sin)], axis=-1)
    kv = (rms_norm_2(c_kv, kv_norm) @ w_ukv).reshape(B, T, MLA_HEADS, MLA_NOPE + MLA_V)
    k_nope, v = kv[..., :MLA_NOPE], kv[..., MLA_NOPE:]
    k_rope = apply_rope(k_pe[:, :, None, :], cos, sin)
    k = jnp.concatenate([k_nope, jnp.broadcast_to(k_rope, (B, T, MLA_HEADS, MLA_ROPE))], axis=-1)
    o = causal_block_attention(q, k, v, MLA_QK ** -0.5)
    return o.reshape(B, T, MLA_HEADS * MLA_V)

def hybrid_rglru_mla(h, cos, sin, w_in, conv_w, conv_b, gate_a_w, gate_a_b, gate_x_w,
                     gate_x_b, lam, q_norm, w_uq, kv_norm, w_ukv, w_out):
    proj = h @ w_in
    x_r, gate_r, c_q, c_kv, k_pe = jnp.split(proj, HY_SPLITS, axis=-1)
    y_a = rglru_branch(x_r, gate_r, conv_w, conv_b, gate_a_w, gate_a_b, gate_x_w, gate_x_b, lam)
    y_b = mla_branch(c_q, c_kv, k_pe, cos, sin, q_norm, w_uq, kv_norm, w_ukv)
    return jnp.concatenate([y_a, y_b], axis=-1) @ w_out

def chunk_gated_delta_rule(q, k, v, g, beta):
    B, T, H, DK = q.shape
    DV = v.shape[-1]
    N = T // GDN_CHUNK
    f32 = jnp.float32

    def chunks(t):
        return t.astype(f32).reshape(B, N, GDN_CHUNK, H, -1).transpose(0, 1, 3, 2, 4)

    qc, kc, vc = chunks(q), chunks(k), chunks(v)
    gch = chunks(g[..., None])[..., 0]
    bch = chunks(beta[..., None])[..., 0]
    gc = jnp.cumsum(gch, axis=-1)
    idx = jnp.arange(GDN_CHUNK)
    causal = idx[:, None] >= idx[None, :]
    strict = idx[:, None] > idx[None, :]
    decay = jnp.exp(jnp.where(causal, gc[..., :, None] - gc[..., None, :], -jnp.inf))
    k_beta = kc * bch[..., None]
    a_strict = jnp.where(strict, jnp.einsum('bnhid,bnhjd->bnhij', k_beta, kc) * decay, 0.0)
    lhs = a_strict + jnp.eye(GDN_CHUNK, dtype=f32)
    u = lax.linalg.triangular_solve(lhs, vc * bch[..., None], left_side=True,
                                    lower=True, unit_diagonal=True)
    w = lax.linalg.triangular_solve(lhs, k_beta * jnp.exp(gc)[..., None], left_side=True,
                                    lower=True, unit_diagonal=True)
    qk = jnp.einsum('bnhid,bnhjd->bnhij', qc, kc) * decay
    q_dec = qc * jnp.exp(gc)[..., None]
    k_dec = kc * jnp.exp(gc[..., -1:] - gc)[..., None]
    chunk_decay = jnp.exp(gc[..., -1])

    def step(S, xs):
        u_n, w_n, qk_n, q_n, k_n, d_n = xs
        v_new = u_n - jnp.einsum('bhck,bhkv->bhcv', w_n, S)
        o_n = jnp.einsum('bhck,bhkv->bhcv', q_n, S) + jnp.einsum('bhij,bhjv->bhiv', qk_n, v_new)
        S = S * d_n[..., None, None] + jnp.einsum('bhck,bhcv->bhkv', k_n, v_new)
        return S, o_n

    xs = tuple(jnp.moveaxis(t, 1, 0) for t in (u, w, qk, q_dec, k_dec, chunk_decay))
    S0 = jnp.zeros((B, H, DK, DV), f32)
    _, o = lax.scan(step, S0, xs)
    return o.transpose(1, 0, 3, 2, 4).reshape(B, T, H, DV).astype(v.dtype)

def gated_delta_net(h, w_in, conv_w, a_log, dt_bias, norm_w, w_out):
    B, T, _ = h.shape
    proj = h @ w_in
    qkv, z, b, a = jnp.split(proj, GDN_SPLITS, axis=-1)
    qkv = jax.nn.silu(causal_depthwise_conv(qkv, conv_w))
    q, k, v = jnp.split(qkv, [GDN_QK_W, 2 * GDN_QK_W], axis=-1)
    rep = GDN_V_HEADS // GDN_K_HEADS
    q = l2_norm(q.reshape(B, T, GDN_K_HEADS, GDN_HEAD_DIM)) * GDN_HEAD_DIM ** -0.5
    k = l2_norm(k.reshape(B, T, GDN_K_HEADS, GDN_HEAD_DIM))
    q = jnp.repeat(q, rep, axis=2)
    k = jnp.repeat(k, rep, axis=2)
    v = v.reshape(B, T, GDN_V_HEADS, GDN_HEAD_DIM)
    beta = jax.nn.sigmoid(b.astype(jnp.float32))
    g = -jnp.exp(a_log.astype(jnp.float32)) * jax.nn.softplus(
        a.astype(jnp.float32) + dt_bias.astype(jnp.float32))
    o = chunk_gated_delta_rule(q, k, v, g, beta)
    o = rms_norm_2(o, norm_w) * jax.nn.silu(z.reshape(B, T, GDN_V_HEADS, GDN_HEAD_DIM))
    return o.reshape(B, T, GDN_V_W) @ w_out

def swiglu_2(h, w_gate, w_up, w_down):
    return (jax.nn.silu(h @ w_gate) * (h @ w_up)) @ w_down

def second_inputs(seed: int = 0) -> dict:
    key = jax.random.key(seed)
    ks = list(jax.random.split(key, 32))
    f32 = jnp.float32

    def normal(k, shape, fan_in):
        return jax.random.normal(k, shape, f32) * fan_in ** -0.5

    def gain(k, shape):
        return 1.0 + 0.02 * jax.random.normal(k, shape, f32)

    def bias(k, shape):
        return 0.01 * jax.random.normal(k, shape, f32)

    x = jax.random.normal(ks[0], (BATCH, SEQ, D_MODEL), f32)
    offset = jax.random.randint(ks[1], (BATCH, 1), 0, 4096, dtype=jnp.int32)
    positions = offset + jnp.arange(SEQ, dtype=jnp.int32)[None, :]

    a_c = jax.random.uniform(ks[12], (N_EVEN, RG_W), f32, 0.9, 0.999)
    s = a_c ** (1.0 / RG_C)
    rg_lambda = jnp.log(s) - jnp.log1p(-s)

    a_log = jnp.log(jax.random.uniform(ks[20], (N_ODD, GDN_V_HEADS), f32, 1.0, 16.0))
    dt = jnp.exp(jax.random.uniform(ks[21], (N_ODD, GDN_V_HEADS), f32,
                                    math.log(1e-3), math.log(1e-1)))
    dt_bias = dt + jnp.log(-jnp.expm1(-dt))

    return {
        "x": x,
        "positions": positions,
        "norm_mix_pre": gain(ks[2], (DEPTH_2, D_MODEL)),
        "norm_mix_post": gain(ks[3], (DEPTH_2, D_MODEL)),
        "norm_ffn_pre": gain(ks[4], (DEPTH_2, D_MODEL)),
        "norm_ffn_post": gain(ks[5], (DEPTH_2, D_MODEL)),
        "hy_w_in": normal(ks[6], (N_EVEN, D_MODEL, HY_IN), D_MODEL),
        "rg_conv_w": normal(ks[7], (N_EVEN, CONV_WIDTH, RG_W), CONV_WIDTH),
        "rg_conv_b": bias(ks[8], (N_EVEN, RG_W)),
        "rg_gate_a_w": normal(ks[9], (N_EVEN, RG_BLOCKS, RG_BLOCK_W, RG_BLOCK_W), RG_BLOCK_W),
        "rg_gate_a_b": bias(ks[10], (N_EVEN, RG_W)),
        "rg_gate_x_w": normal(ks[11], (N_EVEN, RG_BLOCKS, RG_BLOCK_W, RG_BLOCK_W), RG_BLOCK_W),
        "rg_gate_x_b": bias(ks[13], (N_EVEN, RG_W)),
        "rg_lambda": rg_lambda,
        "mla_q_norm": gain(ks[14], (N_EVEN, Q_LORA)),
        "mla_w_uq": normal(ks[15], (N_EVEN, Q_LORA, MLA_HEADS * MLA_QK), Q_LORA),
        "mla_kv_norm": gain(ks[16], (N_EVEN, KV_LORA)),
        "mla_w_ukv": normal(ks[17], (N_EVEN, KV_LORA, MLA_HEADS * (MLA_NOPE + MLA_V)), KV_LORA),
        "hy_w_out": normal(ks[18], (N_EVEN, HY_MIX, D_MODEL), HY_MIX),
        "gdn_w_in": normal(ks[19], (N_ODD, D_MODEL, GDN_IN), D_MODEL),
        "gdn_conv_w": normal(ks[22], (N_ODD, CONV_WIDTH, GDN_CONV_W), CONV_WIDTH),
        "gdn_a_log": a_log,
        "gdn_dt_bias": dt_bias,
        "gdn_norm": gain(ks[23], (N_ODD, GDN_HEAD_DIM)),
        "gdn_w_out": normal(ks[24], (N_ODD, GDN_V_W, D_MODEL), GDN_V_W),
        "ffn_w_gate": normal(ks[25], (DEPTH_2, D_MODEL, FFN_HIDDEN), D_MODEL),
        "ffn_w_up": normal(ks[26], (DEPTH_2, D_MODEL, FFN_HIDDEN), D_MODEL),
        "ffn_w_down": normal(ks[27], (DEPTH_2, FFN_HIDDEN, D_MODEL), FFN_HIDDEN),
    }

def second_block(x, positions, norm_mix_pre, norm_mix_post, norm_ffn_pre, norm_ffn_post,
              hy_w_in, rg_conv_w, rg_conv_b, rg_gate_a_w, rg_gate_a_b, rg_gate_x_w,
              rg_gate_x_b, rg_lambda, mla_q_norm, mla_w_uq, mla_kv_norm, mla_w_ukv, hy_w_out,
              gdn_w_in, gdn_conv_w, gdn_a_log, gdn_dt_bias, gdn_norm, gdn_w_out,
              ffn_w_gate, ffn_w_up, ffn_w_down):
    cos, sin = rope_tables(positions)
    for layer in range(DEPTH_2):
        i = layer // 2
        h = rms_norm_2(x, norm_mix_pre[layer])
        if layer % 2 == 0:
            m = hybrid_rglru_mla(h, cos, sin, hy_w_in[i], rg_conv_w[i], rg_conv_b[i],
                                 rg_gate_a_w[i], rg_gate_a_b[i], rg_gate_x_w[i], rg_gate_x_b[i],
                                 rg_lambda[i], mla_q_norm[i], mla_w_uq[i], mla_kv_norm[i],
                                 mla_w_ukv[i], hy_w_out[i])
        else:
            m = gated_delta_net(h, gdn_w_in[i], gdn_conv_w[i], gdn_a_log[i], gdn_dt_bias[i],
                                gdn_norm[i], gdn_w_out[i])
        x = x + rms_norm_2(m, norm_mix_post[layer])
        h = rms_norm_2(x, norm_ffn_pre[layer])
        x = x + rms_norm_2(swiglu_2(h, ffn_w_gate[layer], ffn_w_up[layer], ffn_w_down[layer]),
                         norm_ffn_post[layer])
    return x


def setup_inputs(seed=0):
    out = dict(first_inputs(seed))
    for name, value in second_inputs(seed + 1).items():
        if name != "x":
            out[name + "_2"] = value
    return out


def reference(
    x, norm_mix_g, norm_ffn_g, fnet_w_out, s5_lambda_re, s5_lambda_im, s5_log_dt, s5_b_re,
    s5_b_im, s5_c_re, s5_c_im, s5_d, s5_w_glu, attn_w_qkv, attn_q_gain, attn_k_gain, attn_w_o,
    rel_bias, ffn_w_gate_up, ffn_w_down, positions_2, norm_mix_pre_2, norm_mix_post_2,
    norm_ffn_pre_2, norm_ffn_post_2, hy_w_in_2, rg_conv_w_2, rg_conv_b_2, rg_gate_a_w_2,
    rg_gate_a_b_2, rg_gate_x_w_2, rg_gate_x_b_2, rg_lambda_2, mla_q_norm_2, mla_w_uq_2,
    mla_kv_norm_2, mla_w_ukv_2, hy_w_out_2, gdn_w_in_2, gdn_conv_w_2, gdn_a_log_2,
    gdn_dt_bias_2, gdn_norm_2, gdn_w_out_2, ffn_w_gate_2, ffn_w_up_2, ffn_w_down_2,
):
    x = first_block(
        x, norm_mix_g, norm_ffn_g, fnet_w_out, s5_lambda_re, s5_lambda_im, s5_log_dt, s5_b_re,
        s5_b_im, s5_c_re, s5_c_im, s5_d, s5_w_glu, attn_w_qkv, attn_q_gain, attn_k_gain,
        attn_w_o, rel_bias, ffn_w_gate_up, ffn_w_down,
    )
    return second_block(
        x, positions_2, norm_mix_pre_2, norm_mix_post_2, norm_ffn_pre_2, norm_ffn_post_2,
        hy_w_in_2, rg_conv_w_2, rg_conv_b_2, rg_gate_a_w_2, rg_gate_a_b_2, rg_gate_x_w_2,
        rg_gate_x_b_2, rg_lambda_2, mla_q_norm_2, mla_w_uq_2, mla_kv_norm_2, mla_w_ukv_2,
        hy_w_out_2, gdn_w_in_2, gdn_conv_w_2, gdn_a_log_2, gdn_dt_bias_2, gdn_norm_2,
        gdn_w_out_2, ffn_w_gate_2, ffn_w_up_2, ffn_w_down_2,
    )


_drawn_inputs = setup_inputs


def setup_inputs(seed=0):
    import zlib

    import numpy as np

    out = dict(_drawn_inputs(seed))
    spreads = {}
    factors = {'s5_lambda_re': 200.0,
     'attn_q_gain': 4.298,
     'attn_k_gain': 4.552,
     'norm_mix_post_2': 3.776,
     'norm_ffn_pre_2': 3.037,
     'norm_ffn_post_2': 4.602,
     'rg_gate_a_b_2': 200.0,
     'rg_gate_x_b_2': 64.0,
     'mla_q_norm_2': 8.0,
     'mla_kv_norm_2': 6.646,
     'gdn_norm_2': 184.38,
     'rg_conv_b_2': 8.0}
    for name, (base, spread) in spreads.items():
        noise = np.random.default_rng([zlib.crc32(name.encode()), seed]).standard_normal(out[name].shape)
        drawn = base * np.exp(spread * noise) if base else spread * noise
        out[name] = jnp.asarray(drawn.astype(out[name].dtype))
    for name, factor in factors.items():
        out[name] = (out[name] * factor).astype(out[name].dtype)
    return out
```

```python
import math
from contextlib import ExitStack

import numpy as np
import concourse.bass as bass
from concourse import mybir

F32 = mybir.dt.float32
F32R = mybir.dt.float32r
I32 = mybir.dt.int32
ALU = mybir.AluOpType
ACT = mybir.ActivationFunctionType
AX = mybir.AxisListType

P = 128
T = 256
D = 1024
KT = D // P
FF = 2816
FT = FF // P
RAW = 6
CUT = 4
ROUND_ITEMS = 12
START = 12
ITEM = 8
EPS = 1e-6
ROUND = 1.5 * 2.0 ** 23
TWO_PI = 6.283185

VECTORS = [
    ("norm_mix_g", 32), ("norm_ffn_g", 32), ("s5_d", 8),
    ("norm_mix_pre_2", 16), ("norm_mix_post_2", 16), ("norm_ffn_pre_2", 16), ("norm_ffn_post_2", 16),
    ("mla_q_norm_2", 4), ("mla_kv_norm_2", 2), ("rg_conv_w_2", 32), ("rg_conv_b_2", 8),
    ("rg_gate_a_b_2", 8), ("rg_gate_x_b_2", 8), ("rg_lambda_2", 8), ("gdn_conv_w_2", 128),
    ("gdn_norm_2", 1), ("attn_q_gain", 3), ("attn_k_gain", 3),
]
VEC_AT = {}
_at = 0
for _name, _n in VECTORS:
    VEC_AT[_name] = _at
    _at += _n
NVEC = _at


class Space:
    pass


class Signal:

    def __init__(self, s, n):
        self.s, self.n = s, n


def tile_of(t3, n):
    if isinstance(n, int):
        return t3[:, n, :]
    return t3[:, bass.ds(n, 1), :].rearrange("p a n -> p (a n)")


def loads(k, sp, first, count):
    first = first + CUT + RAW
    count = max(min(count, k.items - first), 0)
    rounds = count // ROUND_ITEMS if count >= 2 * ROUND_ITEMS else 0
    if rounds:
        with sp.Fori(0, rounds) as i:
            for s in range(ROUND_ITEMS):
                at = sp.snap(i * ROUND_ITEMS + (first - START + s))
                sp.wait_ge(k.item_cut, i * ROUND_ITEMS + (first + s - RAW + 1))
                sp.dma_start(k.raw[:, (first + s) % RAW, :], k.weights[bass.ds(at, 1), :, :].rearrange("a p n -> p (a n)"))\
                  .then_inc(k.item_here[(first + s) % RAW], 16)
    for s in range(rounds * ROUND_ITEMS, count):
        sp.wait_ge(k.item_cut, first + s - RAW + 1)
        sp.dma_start(k.raw[:, (first + s) % RAW, :], k.weights[first - START + s, :, :])\
          .then_inc(k.item_here[(first + s) % RAW], 16)


def round_item(k, act, used, i=0):
    item = used + CUT
    if isinstance(i, int) and item >= k.items:
        return
    act.wait_ge(k.item_here[item % RAW], i * (16 * ROUND_ITEMS // RAW) + 16 * ((item - START) // RAW + 1))
    act.wait_ge(k.item_used, i * ROUND_ITEMS + (used + 1))
    act.activation(k.hi[:, item % CUT, :], k.raw[:, item % RAW, :], ACT.Copy).then_inc(k.item_rounded, 1)


def cut_item(k, engine, used, i=0):
    item = used + CUT
    if isinstance(i, int) and item >= k.items:
        return
    engine.wait_ge(k.item_rounded, i * ROUND_ITEMS + (item + 1))
    engine.tensor_tensor(k.lo[:, item % CUT, :], k.raw[:, item % RAW, :], k.hi[:, item % CUT, :].bitcast(F32), ALU.subtract)\
          .then_inc(k.item_cut, 1)


class Weights:

    def __init__(self, k, pe, first, i=0):
        self.k, self.pe, self.first, self.i = k, pe, first, i

    def tile(self, t, cols=P):
        item = self.first + t // ITEM
        if t % ITEM == 0:
            self.pe.wait_ge(self.k.item_cut, self.i * ROUND_ITEMS + (item + 1))
        at = slice(t % ITEM * P, t % ITEM * P + cols)
        return self.k.hi[:, item % CUT, at], self.k.lo[:, item % CUT, at]


def product(pe, out, w, x, start, stop, **more):
    (wh, wl), (xh, xl) = w, x
    pe.matmul(out, wh, xh, start=start, stop=False, **more)
    pe.matmul(out, wh, xl, start=False, stop=False, **more)
    return pe.matmul(out, wl, xh, start=False, stop=stop, **more)


def pair_tile(pair, j, cols=slice(None)):
    return pair[0][:, j, cols], pair[1][:, j, cols]


def cut(k, src, pair, kt):
    b_r = k.cut_round.n
    with k.nc.Block() as block:
        @block.scalar
        def _(act):
            for j in range(kt):
                act.activation(pair[0][:, j, :], src[:, j, :], ACT.Copy).then_inc(k.cut_round.s, 1)

        def low(engine, mine):
            for j in mine:
                engine.wait_ge(k.cut_round.s, b_r + j + 1)
                engine.tensor_tensor(pair[1][:, j, :], src[:, j, :], pair[0][:, j, :].bitcast(F32), ALU.subtract)

        @block.vector
        def _(dve):
            low(dve, [j for j in range(kt) if j % 3])

        @block.gpsimd
        def _(pool):
            low(pool, [j for j in range(kt) if j % 3 == 0])
    k.cut_round.n += kt


def norm(k, src, kt, gain_col, dst, width, times=1.0, pair=None):
    nc = k.nc
    tag = f"{k.norm_done.n}"
    eps = k.eps if times == 1.0 else k.eps192
    with nc.sbuf_tensor("norm_sq" + tag, [P, kt, T], F32) as sq, nc.sbuf_tensor("norm_rs" + tag, [P, 2, T], F32) as rs, \
            nc.Block() as block:
        b_sq, b_sum, b_root, b_inv, b_n, b_r = (k.sq_done.n, k.sum_done.n, k.root_done.n, k.norm_done.n, k.norm_out.n,
                                                k.cut_round.n)

        @block.scalar
        def _(act):
            for j in range(kt):
                act.activation(sq[:, j, :], src[:, j, :], ACT.Square).then_inc(k.sq_done.s, 1)
            act.wait_ge(k.sum_done.s, b_sum + 1)
            act.activation(rs[:, 0, :], k.ps[:, 0, 0:T], ACT.Sqrt, scale=times / width,
                           bias=eps[:, 0:1]).then_inc(k.root_done.s, 1)
            if pair:
                for j in range(kt):
                    act.wait_ge(k.norm_out.s, b_n + j + 1)
                    act.activation(pair[0][:, j, :], dst[:, j, :], ACT.Copy).then_inc(k.cut_round.s, 1)

        @block.tensor
        def _(pe):
            for j in range(kt):
                pe.wait_ge(k.sq_done.s, b_sq + j + 1)
                mm = pe.matmul(k.ps[:, 0, 0:T], k.ones[:, :], sq[:, j, :], start=(j == 0), stop=(j == kt - 1))
            mm.then_inc(k.sum_done.s, 1)

        @block.vector
        def _(dve):
            dve.wait_ge(k.root_done.s, b_root + 1)
            dve.reciprocal(rs[:, 1, :], rs[:, 0, :]).then_inc(k.norm_done.s, 1)
            dve.wait_ge(k.norm_done.s, b_inv + 1)
            for j in range(kt):
                dve.scalar_tensor_tensor(dst[:, j, :], src[:, j, :], k.vec[:, gain_col + j:gain_col + j + 1],
                                         rs[:, 1, :], ALU.mult, ALU.mult).then_inc(k.norm_out.s, 1)
            if pair:
                for j in range(kt):
                    if j % 2 == 0:
                        dve.wait_ge(k.cut_round.s, b_r + j + 1)
                        dve.tensor_tensor(pair[1][:, j, :], dst[:, j, :], pair[0][:, j, :].bitcast(F32), ALU.subtract)

        if pair:
            @block.gpsimd
            def _(pool):
                for j in range(1, kt, 2):
                    pool.wait_ge(k.cut_round.s, b_r + j + 1)
                    pool.tensor_tensor(pair[1][:, j, :], dst[:, j, :], pair[0][:, j, :].bitcast(F32), ALU.subtract)
            k.cut_round.n += kt
        k.norm_out.n += kt
        k.sq_done.n += kt
        k.sum_done.n += 1
        k.root_done.n += 1
        k.norm_done.n += 1


def linear(k, src, kt, nt, dve_out=None, act_out=None):
    first = k.used
    items = nt * kt // ITEM
    banks = 2 if kt > ITEM else 4
    per = ITEM * ROUND_ITEMS // kt
    rounds = nt // per if nt >= 2 * per else 0
    b_out = k.out_done.n

    def walk(engine, step):
        if rounds:
            with engine.Fori(0, rounds) as i:
                for b in range(per):
                    step(i, b)
        for n in range(rounds * per, nt):
            step(0, n)

    def computed(i, b):
        return i * ROUND_ITEMS + (first + -(-(b + 1) * kt // ITEM))

    def items_of(b):
        return range(b * kt // ITEM, (b + 1) * kt // ITEM)

    with k.nc.Block() as block:
        @block.sync
        def _(sp):
            loads(k, sp, first, items)

        @block.tensor
        def _(pe):
            def step(i, b):
                w = Weights(k, pe, first, i)
                pe.wait_ge(k.out_done.s, i * per + (b + b_out - banks + 1))
                for j in range(kt):
                    mm = product(pe, k.ps[:, b % banks, 0:T], w.tile(b * kt + j), pair_tile(src, j),
                                 start=(j == 0), stop=(j == kt - 1))
                    if (b * kt + j) % ITEM == ITEM - 1:
                        mm.then_inc(k.item_used, 1)
            walk(pe, step)

        @block.scalar
        def _(act):
            def step(i, b):
                if act_out:
                    act.wait_ge(k.item_used, computed(i, b))
                    act_out(act, i * per + b, k.ps[:, b % banks, 0:T]).then_inc(k.out_done.s, 1)
                for item in items_of(b):
                    round_item(k, act, first + item, i)
            walk(act, step)

        @block.vector
        def _(dve):
            def step(i, b):
                if dve_out:
                    dve.wait_ge(k.item_used, computed(i, b))
                    dve_out(dve, i * per + b, k.ps[:, b % banks, 0:T]).then_inc(k.out_done.s, 1)
                for item in items_of(b):
                    cut_item(k, dve, first + item, i)
            walk(dve, step)
    k.used += items
    k.out_done.n += nt


def swiglu(k, src, out):
    first = k.used
    items = 3 * FT
    per = ROUND_ITEMS // 3
    rounds = (FT - 2) // per
    b_silu, b_hid, b_prod = k.silu_done.n, k.hidden_done.n, k.mul_done.n

    def walk(engine, step):
        with engine.Fori(0, rounds) as i:
            for b in range(per):
                step(i, b)
        for j in range(rounds * per, FT):
            step(0, j)

    with k.nc.sbuf_tensor(f"silu{first}", [P, 2, T], F32) as silu, k.nc.sbuf_tensor(f"hidden{first}", [P, 2, T], F32) as hidden, \
            k.nc.sbuf_tensor(f"hidden_h{first}", [P, 2, T], F32R) as hid_h, \
            k.nc.sbuf_tensor(f"hidden_l{first}", [P, 2, T], F32R) as hid_l, \
            k.nc.Block() as block:
        @block.sync
        def _(sp):
            loads(k, sp, first, items)

        @block.tensor
        def _(pe):
            def gate_up(i, b):
                w = Weights(k, pe, first, i)
                at = 0 if (isinstance(i, int) and b == 0) else 2 + 3 * (b - 1)
                for half in range(2):
                    for j in range(KT):
                        mm = product(pe, k.ps[:, 4 + b % 2, half * T:(half + 1) * T], w.tile((at + half) * ITEM + j),
                                     pair_tile(src, j), start=(j == 0), stop=(j == KT - 1))
                    mm.then_inc(k.item_used, 1)

            def down(i, b):
                w = Weights(k, pe, first, i)
                at = 4 + 3 * b if not (isinstance(i, int) and b == FT - 1) else items - 1
                pe.wait_ge(k.hidden_done.s, i * per + (b + b_hid + 1))
                for n in range(KT):
                    mm = product(pe, k.ps[:, n // 2, n % 2 * T:(n % 2 + 1) * T], w.tile(at * ITEM + n),
                                 pair_tile((hid_h, hid_l), b % 2), start=False, stop=False, skip_group_check=True)
                mm.then_inc(k.item_used, 1)

            for n in range(KT // 2):
                pe.matmul(k.ps[:, n, :], k.zeros[:, 0:P], k.zeros[:, :], start=True, stop=False, skip_group_check=True)
            gate_up(0, 0)

            def step(i, b):
                if not (isinstance(i, int) and b == FT - 1):
                    gate_up(i, b + 1)
                down(i, b)
            walk(pe, step)

        def beside(engine, part, i, b):
            for item in range(3 * b, 3 * b + 3):
                part(k, engine, first + item, i)

        @block.scalar
        def _(act):
            def step(i, b):
                act.wait_ge(k.item_used, i * ROUND_ITEMS + (first + 3 * b + (2 if b == 0 else 1)))
                act.wait_ge(k.hidden_done.s, i * per + (b + b_hid - 1))
                act.activation(silu[:, b % 2, :], k.ps[:, 4 + b % 2, 0:T], ACT.Silu).then_inc(k.silu_done.s, 1)
                beside(act, round_item, i, b)
            walk(act, step)

        @block.vector
        def _(dve):
            def step(i, b):
                dve.wait_ge(k.silu_done.s, i * per + (b + b_silu + 1))
                dve.wait_ge(k.item_used, i * ROUND_ITEMS + (first + 3 * b - 1))
                dve.tensor_tensor(hid_h[:, b % 2, :], silu[:, b % 2, :], k.ps[:, 4 + b % 2, T:2 * T], ALU.mult)
                dve.tensor_tensor(hidden[:, b % 2, :], silu[:, b % 2, :], k.ps[:, 4 + b % 2, T:2 * T], ALU.mult)\
                   .then_inc(k.mul_done.s, 1)
                dve.wait_ge(k.mul_done.s, i * per + (b + b_prod + 1))
                dve.tensor_tensor(hid_l[:, b % 2, :], hidden[:, b % 2, :], hid_h[:, b % 2, :].bitcast(F32), ALU.subtract)\
                   .then_inc(k.hidden_done.s, 1)
                beside(dve, cut_item, i, b)
            walk(dve, step)
            dve.wait_ge(k.item_used, first + items)
            for n in range(KT):
                out(dve, n, k.ps[:, n // 2, n % 2 * T:(n % 2 + 1) * T])
    k.used += items
    k.silu_done.n += FT
    k.mul_done.n += FT
    k.hidden_done.n += FT



def fourier(k):
    nc = k.nc
    with nc.sbuf_tensor(f"dft_hf{k.used}", [P, 2, 2, 2 * P], F32) as hf, \
            nc.sbuf_tensor(f"dft_h{k.used}", [P, KT, T], F32R) as f_h, nc.sbuf_tensor(f"dft_l{k.used}", [P, KT, T], F32R) as f_l:
        dft = const(k, "dft_feature")
        cs = const(k, "dft_cos").rearrange("p (a n) -> p a n", a=2)
        ns = const(k, "dft_nsin").rearrange("p (a n) -> p a n", a=2)
        b_f, b_c, b_s, b_o, b_l = k.dft1_done.n, k.dft1_out.n, k.dft2_done.n, k.dft2_out.n, k.dft2_low.n
        with nc.Block() as block:
            @block.tensor
            def _(pe):
                def over_features(g):
                    if g >= 2:
                        pe.wait_ge(k.dft1_out.s, b_c + g - 1)
                    for a in range(2):
                        mm = pe.matmul(k.ps[:, g % 2, a * T:(a + 1) * T], k.h[:, g, a * P:(a + 1) * P], dft,
                                       start=True, stop=True)
                    mm.then_inc(k.dft1_done.s, 1)

                over_features(0)
                for g in range(KT):
                    if g + 1 < KT:
                        over_features(g + 1)
                    pe.wait_ge(k.dft1_out.s, b_c + g + 1)
                    if g >= 2:
                        pe.wait_ge(k.dft2_low.s, b_l + g - 1)
                    for a in range(2):
                        pe.matmul(k.ps[:, 2 + g % 2, 0:T], hf[:, g % 2, a, 0:P], cs[:, a, :], start=(a == 0), stop=False)
                        mm = pe.matmul(k.ps[:, 2 + g % 2, 0:T], hf[:, g % 2, a, P:2 * P], ns[:, a, :], start=False,
                                       stop=(a == 1))
                    mm.then_inc(k.dft2_done.s, 1)

            def low(dve, g):
                dve.wait_ge(k.dft2_out.s, b_o + g + 1)
                dve.tensor_tensor(f_l[:, g, :], k.ps[:, 2 + g % 2, 0:T], f_h[:, g, :].bitcast(F32), ALU.subtract)\
                   .then_inc(k.dft2_low.s, 1)

            @block.vector
            def _(dve):
                for g in range(KT):
                    dve.wait_ge(k.dft1_done.s, b_f + g + 1)
                    if g >= 2:
                        dve.wait_ge(k.dft2_done.s, b_s + g - 1)
                    dve.tensor_copy(hf[:, g % 2, :, :], k.ps[:, g % 2, :].rearrange("p (a n) -> p a n", a=2))\
                       .then_inc(k.dft1_out.s, 1)
                    if g:
                        low(dve, g - 1)
                low(dve, KT - 1)

            @block.scalar
            def _(act):
                for g in range(KT):
                    act.wait_ge(k.dft2_done.s, b_s + g + 1)
                    act.activation(f_h[:, g, :], k.ps[:, 2 + g % 2, 0:T], ACT.Copy).then_inc(k.dft2_out.s, 1)
        for s in (k.dft1_done, k.dft1_out, k.dft2_done, k.dft2_out, k.dft2_low):
            s.n += KT
        linear(k, (f_h, f_l), KT, KT, dve_out=residual(k))


SG, SP_, SN = 64, 16, 64
ST = 2 * SG // 2


def s5(k):
    nc = k.nc
    with ExitStack() as ctx:
        def sb(name, shape, dt=F32):
            return ctx.enter_context(nc.sbuf_tensor(name, shape, dt))
        lam = sb("lam", [P, 3, ST])
        w = sb("s5_w", [P, 12, ST])
        dt_, r, y, th, sn, cs_, ar, ai, m2, cr, ci, t0 = (w[:, j, :] for j in range(12))
        bT = sb("s5_bT", [P, 2, 2, KT, 2, SN])
        cT = sb("s5_cT", [P, 3, ST, 2, SP_])
        yd = sb("s5_yd", [P, KT, T])
        even_odd = const(k, "b_half")
        c_half = const(k, "c_half")
        V = k.s5v
        A = k.s5a
        with nc.sbuf_tensor("s5_b_raw", [P, 2, 2, KT, SN], F32) as b_raw, \
                nc.sbuf_tensor("s5_c_raw", [P, 2, ST, SP_], F32) as c_raw, \
                nc.sbuf_tensor("s5_c_w", [P, 4, ST, SP_], F32) as c_w, nc.Block() as block:
            @block.sync
            def _(sp):
                sp.dma_start(lam[:, :, :], k.ins["s5_lam"]).then_inc(k.side_here.s, 16)
                sp.dma_start(b_raw[:, :, :, :, :].rearrange("p a b c d -> p (a b c d)"), k.ins["s5_b"]).then_inc(k.side_here.s, 16)
                sp.dma_start(c_raw[:, :, :, :].rearrange("p a b c -> p (a b c)"), k.ins["s5_c"]).then_inc(k.side_here.s, 16)

            b0, v0, a0 = k.side_here.n, V.n, A.n

            @block.scalar
            def _(act):
                act.wait_ge(k.side_here.s, b0 + 48)
                act.activation(dt_, lam[:, 2, :], ACT.Exp).then_inc(A.s, 1)
                act.wait_ge(V.s, v0 + 1)
                act.activation(r, ar, ACT.Exp).then_inc(A.s, 1)
                act.wait_ge(V.s, v0 + 4)
                act.activation(sn, y, ACT.Sin, scale=TWO_PI).then_inc(A.s, 1)
                act.activation(t0, y, ACT.Abs).then_inc(A.s, 1)
                act.wait_ge(A.s, a0 + 4)
                act.activation(cs_, t0, ACT.Sin, scale=-TWO_PI, bias=k.half_pi[:, 0:1]).then_inc(A.s, 1)

            @block.vector
            def _(dve):
                n = [v0]

                def tick(ins):
                    n[0] += 1
                    ins.then_inc(V.s, 1)
                    dve.wait_ge(V.s, n[0])
                dve.wait_ge(A.s, a0 + 1)
                tick(dve.tensor_tensor(ar, lam[:, 0, :], dt_, ALU.mult))
                tick(dve.scalar_tensor_tensor(th, lam[:, 1, :], 1.0 / (2 * math.pi), dt_, ALU.mult, ALU.mult))
                tick(dve.tensor_scalar(m2, th, ROUND, -ROUND, ALU.add, ALU.add))
                tick(dve.tensor_tensor(y, th, m2, ALU.subtract))
                dve.wait_ge(A.s, a0 + 5)
                tick(dve.tensor_tensor(ar, r, cs_, ALU.mult))
                tick(dve.tensor_scalar(ar, ar, -1.0, None, ALU.add))
                tick(dve.tensor_tensor(ai, r, sn, ALU.mult))
                tick(dve.tensor_tensor(m2, lam[:, 0, :], lam[:, 0, :], ALU.mult))
                tick(dve.tensor_tensor(t0, lam[:, 1, :], lam[:, 1, :], ALU.mult))
                tick(dve.tensor_tensor(m2, m2, t0, ALU.add))
                tick(dve.reciprocal(m2, m2))
                tick(dve.tensor_tensor(cr, ar, lam[:, 0, :], ALU.mult))
                tick(dve.tensor_tensor(t0, ai, lam[:, 1, :], ALU.mult))
                tick(dve.tensor_tensor(cr, cr, t0, ALU.add))
                tick(dve.tensor_tensor(cr, cr, m2, ALU.mult))
                tick(dve.tensor_tensor(ci, ai, lam[:, 0, :], ALU.mult))
                tick(dve.tensor_tensor(t0, ar, lam[:, 1, :], ALU.mult))
                tick(dve.tensor_tensor(ci, ci, t0, ALU.subtract))
                tick(dve.tensor_tensor(ci, ci, m2, ALU.mult))
                crb = spread(cr.rearrange("p (c o) -> p c o", o=1), 2, SP_)
                cib = spread(ci.rearrange("p (c o) -> p c o", o=1), 2, SP_)
                tick(dve.tensor_tensor(c_w[:, 0, :, :], c_raw[:, 0, :, :], crb, ALU.mult))
                tick(dve.tensor_tensor(c_w[:, 1, :, :], c_raw[:, 1, :, :], cib, ALU.mult))
                tick(dve.tensor_tensor(c_w[:, 0, :, :], c_w[:, 0, :, :], c_w[:, 1, :, :], ALU.subtract))
                tick(dve.tensor_tensor(c_w[:, 2, :, :], c_raw[:, 0, :, :], cib, ALU.mult))
                tick(dve.tensor_tensor(c_w[:, 3, :, :], c_raw[:, 1, :, :], crb, ALU.mult))
                tick(dve.tensor_tensor(c_w[:, 2, :, :], c_w[:, 2, :, :], c_w[:, 3, :, :], ALU.add))
                for half in range(2):
                    for j, (src, sign) in enumerate(((0, 1.0), (0, -1.0), (2, -1.0))):
                        tick(dve.tensor_scalar(cT[:, j, :, half, :], c_w[:, src, :, :], c_half[:, half:half + 1], sign,
                                               ALU.mult, ALU.mult))
                    for a in range(2):
                        tick(dve.tensor_scalar(bT[:, a, :, :, half, :].rearrange("p a b n -> p (a b) n"),
                                               b_raw[:, a, :, :, :].rearrange("p a b n -> p (a b) n"),
                                               even_odd[:, half:half + 1], None, ALU.mult))
                tick(dve.tensor_scalar(y[:, ST // 2:ST], y[:, ST // 2:ST], -1.0, None, ALU.mult))
                k.s5_ticks = n[0] - v0
            k.side_here.n += 48
            V.n += k.s5_ticks
            A.n += 5

        with nc.sbuf_tensor([P, 2, 2, T], F32) as ph, nc.sbuf_tensor([P, 2, 3, T], F32) as ang, \
                nc.sbuf_tensor([P, 2, 2, T], F32) as tab, nc.sbuf_tensor([P, 2, 2, 2, T], F32) as mod, \
                nc.sbuf_tensor([P, 2, 2, T], F32) as bm, nc.sbuf_tensor([P, 2, 2, T], F32) as g, \
                nc.sbuf_tensor([P, 2, 2, 2, T], F32) as prod, nc.Block() as block:
            order = [(kt, j, d) for kt in range(KT) for j in range(4) for d in range(2)]
            s_bu, s_y, s_ang, s_phase, s_tab = k.s5_bu, k.s5_y, k.s5_ang, k.s5_phase, k.s5_tab
            s_abs, s_bm = k.s5_abs, k.s5_bm
            s_free, s_scan, s_prod, s_out = k.s5_free, k.s5_scan, k.s5_prod, k.s5_out
            tvec = const(k, "time")
            v1 = V.n

            def cidx(kt, j, d):
                return d * (ST // 2) + kt * 4 + j

            @block.tensor
            def _(pe):
                def drive(q):
                    kt, j, d = order[q]
                    if q >= 2:
                        pe.wait_ge(s_free.s, q - 1)
                    for a in range(2):
                        mm = pe.matmul(k.ps[:, q % 2, a * T:(a + 1) * T],
                                       bT[32 * j:32 * j + 32, a, d, kt, :, :].rearrange("p a b -> p (a b)"),
                                       k.h[32 * j:32 * j + 32, kt, :], start=True, stop=True, tile_position=(32 * j, 0))
                    mm.then_inc(s_bu.s, 1)
                drive(0)
                for q, (kt, j, d) in enumerate(order):
                    if q + 1 < ST:
                        drive(q + 1)
                    if j == 0 and d == 0 and kt >= 2:
                        pe.wait_ge(s_out.s, kt - 1)
                    pe.wait_ge(s_prod.s, q + 1)
                    c = cidx(kt, j, d)
                    for m, (a, b, which) in enumerate(((0, 0, 0), (1, 1, 1), (0, 1, 2), (1, 0, 2))):
                        mm = pe.matmul(k.ps[32 * j:32 * j + 32, 2 + kt % 2, 0:T],
                                       cT[:, which, c, :, :].rearrange("p a b -> p (a b)"), prod[:, q % 2, a, b, :],
                                       start=(d == 0 and m == 0), stop=(d == 1 and m == 3), tile_position=(0, 32 * j))
                    mm.then_inc(s_y.s, 1)

            @block.scalar
            def _(act):
                act.wait_ge(V.s, v1)
                for q, (kt, j, d) in enumerate(order):
                    c = cidx(kt, j, d)
                    if q >= 2:
                        act.wait_ge(s_ang.s, q - 1)
                    act.activation(ph[:, q % 2, 0, :], tvec, ACT.Identity, scale=y[:, c:c + 1], bias=k.round_c[:, 0:1])
                    act.activation(ph[:, q % 2, 1, :], tvec, ACT.Copy, scale=y[:, c:c + 1]).then_inc(s_phase.s, 1)
                    act.wait_ge(s_ang.s, q + 1)
                    if q >= 2:
                        act.wait_ge(s_prod.s, q - 1)
                    act.activation(tab[:, q % 2, 1, :], ang[:, q % 2, 0, :], ACT.Sin, scale=-TWO_PI)
                    act.activation(ang[:, q % 2, 1, :], ang[:, q % 2, 0, :], ACT.Abs).then_inc(s_abs.s, 1)
                    act.wait_ge(s_abs.s, q + 1)
                    act.activation(tab[:, q % 2, 0, :], ang[:, q % 2, 1, :], ACT.Sin, scale=-TWO_PI,
                                   bias=k.half_pi[:, 0:1]).then_inc(s_tab.s, 1)

            def y_out(dve, kt):
                dve.wait_ge(s_y.s, 8 * (kt + 1))
                dve.scalar_tensor_tensor(yd[:, kt, :], k.h[:, kt, :], k.vec[:, VEC_AT["s5_d"] + kt:VEC_AT["s5_d"] + kt + 1],
                                         k.ps[:, 2 + kt % 2, 0:T], ALU.mult, ALU.add).then_inc(s_out.s, 1)

            @block.vector
            def _(dve):
                def angle(q):
                    dve.wait_ge(s_phase.s, q + 1)
                    if q >= 2:
                        dve.wait_ge(s_tab.s, q - 1)
                    dve.scalar_tensor_tensor(ang[:, q % 2, 0, :], ph[:, q % 2, 0, :], -ROUND, ph[:, q % 2, 1, :],
                                             ALU.add, ALU.subtract).then_inc(s_ang.s, 1)
                angle(0)
                for q, (kt, j, d) in enumerate(order):
                    c = cidx(kt, j, d)
                    if q + 1 < ST:
                        angle(q + 1)
                    s = q % 2
                    cosb = spread(tab[:, s, 0:1, :], 1, 2)
                    sinb = spread(tab[:, s, 1:2, :], 1, 2)
                    bu = k.ps[:, s, :].rearrange("p (a n) -> p a n", a=2)
                    dve.wait_ge(s_bu.s, q + 1)
                    dve.wait_ge(s_tab.s, q + 1)
                    dve.tensor_tensor(mod[:, s, 0, :, :], bu, cosb, ALU.mult)
                    dve.tensor_tensor(mod[:, s, 1, :, :], bu, sinb, ALU.mult).then_inc(s_free.s, 1)
                    dve.wait_ge(s_free.s, q + 1)
                    dve.tensor_tensor(bm[:, s, 0, :], mod[:, s, 0, 0, :], mod[:, s, 1, 1, :], ALU.add)
                    dve.tensor_tensor(bm[:, s, 1, :], mod[:, s, 0, 1, :], mod[:, s, 1, 0, :], ALU.subtract).then_inc(s_bm.s, 1)
                    dve.wait_ge(s_bm.s, q + 1)
                    if q >= 2:
                        dve.wait_ge(s_prod.s, q - 1)
                    rb = spread(r[:, c:c + 1], 1, T)
                    for a in range(2):
                        if d == 0:
                            mm = dve.tensor_tensor_scan(g[:, s, a, :], rb, bm[:, s, a, :], 0.0, ALU.mult, ALU.add)
                        else:
                            mm = dve.tensor_tensor_scan(g[:, s, a, ::-1], rb, bm[:, s, a, ::-1], 0.0, ALU.mult, ALU.add)
                    mm.then_inc(s_scan.s, 1)
                    if j == 3 and d == 1:
                        if kt > 0:
                            y_out(dve, kt - 1)
                y_out(dve, KT - 1)

            @block.gpsimd
            def _(pool):
                for q, (kt, j, d) in enumerate(order):
                    s = q % 2
                    pool.wait_ge(s_scan.s, q + 1)
                    if q >= 2:
                        pool.wait_ge(s_y.s, q - 1)
                    for a in range(2):
                        mm = pool.tensor_tensor(prod[:, s, a, :, :], spread(g[:, s, a:a + 1, :], 1, 2), tab[:, s, :, :], ALU.mult)
                    mm.then_inc(s_prod.s, 1)

        with nc.Block() as block:
            @block.scalar
            def _(act):
                for n in range(KT):
                    act.activation(yd[:, n, :], yd[:, n, :], ACT.Gelu_apprx_tanh)
        cut(k, yd, k.hp, KT)

        with nc.sbuf_tensor([P, 2, T], F32) as sg, nc.sbuf_tensor([P, 2, T], F32) as pr:
            glu(k, k.hp, sg, pr)


def spread(ap, axis, n):
    shape = list(ap.shape)
    shape[axis] = n
    return ap.broadcast_to(shape)


def glu(k, src, sg, pr):
    first = k.used
    b_sig, b_out, b_mul = k.act_done.n, k.out_done.n, k.mul_done.n
    with k.nc.Block() as block:
        @block.sync
        def _(sp):
            loads(k, sp, first, 2 * KT)

        @block.tensor
        def _(pe):
            w = Weights(k, pe, first)
            for n in range(KT):
                if n >= 2:
                    pe.wait_ge(k.mul_done.s, b_mul + n - 1)
                for half in range(2):
                    for j in range(KT):
                        mm = product(pe, k.ps[:, n % 2, half * T:(half + 1) * T], w.tile((2 * n + half) * ITEM + j),
                                     pair_tile(src, j), start=(j == 0), stop=(j == KT - 1))
                    mm.then_inc(k.item_used, 1)

        @block.scalar
        def _(act):
            for n in range(KT):
                act.wait_ge(k.item_used, first + 2 * n + 2)
                if n >= 2:
                    act.wait_ge(k.mul_done.s, b_mul + n - 1)
                act.activation(sg[:, n % 2, :], k.ps[:, n % 2, 0:T], ACT.Sigmoid).then_inc(k.act_done.s, 1)
                for half in range(2):
                    round_item(k, act, first + 2 * n + half)

        @block.vector
        def _(dve):
            for n in range(KT):
                dve.wait_ge(k.act_done.s, b_sig + n + 1)
                dve.tensor_tensor(pr[:, n % 2, :], sg[:, n % 2, :], k.ps[:, n % 2, T:2 * T], ALU.mult)\
                   .then_inc(k.mul_done.s, 1)
                dve.wait_ge(k.mul_done.s, b_mul + n + 1)
                dve.tensor_tensor(k.x[:, n, :], k.x[:, n, :], pr[:, n % 2, :], ALU.add)
                for half in range(2):
                    cut_item(k, dve, first + 2 * n + half)
    k.used += 2 * KT
    k.act_done.n += KT
    k.mul_done.n += KT



AH = 16
GROUPS = 3
NEG = -1e30


def token_major(k, src, out3, kt=KT):
    first = k.used
    with k.nc.Block() as block:
        @block.sync
        def _(sp):
            loads(k, sp, first, kt)

        @block.tensor
        def _(pe):
            w = Weights(k, pe, first)
            for j in range(kt):
                wh, wl = w.tile(j * ITEM, ITEM * P)
                for a in range(2):
                    for c in range(2):
                        half = slice(c * 512, (c + 1) * 512)
                        mm = product(pe, k.ps[:, 2 * a + c, :], pair_tile(src, j, slice(a * P, (a + 1) * P)),
                                     (wh[:, half], wl[:, half]), start=(j == 0), stop=(j == kt - 1))
                mm.then_inc(k.item_used, 1)

        @block.scalar
        def _(act):
            for j in range(kt):
                round_item(k, act, first + j)
            act.wait_ge(k.item_used, first + kt)
            for c in range(2):
                act.activation(out3[:, 0, c * 512:(c + 1) * 512], k.ps[:, c, :], ACT.Copy)

        @block.vector
        def _(dve):
            for j in range(kt):
                cut_item(k, dve, first + j)
            dve.wait_ge(k.item_used, first + kt)
            for c in range(2):
                dve.tensor_copy(out3[:, 1, c * 512:(c + 1) * 512], k.ps[:, 2 + c, :])
    k.used += kt


def attention_bias(k, tab0, tab12):
    nc = k.nc
    with nc.sbuf_tensor("ab_onehot", [32, 3, 512], F32) as onehot, nc.sbuf_tensor("ab_mask", [AH, 3, 512], F32) as mask, \
            nc.sbuf_tensor("ab_rel", [32, GROUPS * AH], F32) as rel, \
            nc.sbuf_tensor("ab_tab", [AH, 3, 512], F32) as tab, nc.Block() as block:
        b_in, b_p, b_t, b_w = k.side_here.n, k.bias_ps.n, k.bias_tab.n, k.bias_written.n

        @block.sync
        def _(sp):
            sp.dma_start(onehot[:, :, :], k.ins["bias_onehot"]).then_inc(k.side_here.s, 16)
            sp.dma_start(mask[:, :, :], k.ins["bias_mask"]).then_inc(k.side_here.s, 16)
            sp.dma_start(rel[:, :], k.ins["rel_bias"]).then_inc(k.side_here.s, 16)
            sp.wait_ge(k.bias_tab.s, b_t + 1)
            sp.dma_start(tab0, tab[:, 0, :]).then_inc(k.bias_written.s, 16)
            sp.dma_start(tab12, tab[:, 1:3, 0:P]).then_inc(k.bias_written.s, 16)
            sp.wait_ge(k.bias_written.s, b_w + 32)

        @block.tensor
        def _(pe):
            pe.wait_ge(k.side_here.s, b_in + 48)
            for g in range(GROUPS):
                mm = pe.matmul(k.ps[0:AH, g, :], rel[:, g * AH:(g + 1) * AH], onehot[:, g, :], start=True, stop=True)
            mm.then_inc(k.bias_ps.s, 1)

        @block.vector
        def _(dve):
            dve.wait_ge(k.bias_ps.s, b_p + 1)
            dve.tensor_tensor(tab[:, :, :], k.ps[0:AH, 0:3, :], mask[:, :, :], ALU.add).then_inc(k.bias_tab.s, 1)
        k.side_here.n += 48
        k.bias_ps.n += 1
        k.bias_tab.n += 1
        k.bias_written.n += 32


def attention(k):
    nc = k.nc
    with ExitStack() as ctx:
        def sb(name, shape, dt=F32):
            return ctx.enter_context(nc.sbuf_tensor(name, shape, dt))
        tab0 = nc.dram_tensor("bias_group0", (AH, 512), F32, kind="Internal").ap()
        tab12 = nc.dram_tensor("bias_groups12", (AH, 2, P), F32, kind="Internal").ap()
        attention_bias(k, tab0, tab12)
        qT = sb("at_q", [P, 24, T])
        kT = sb("at_k", [P, 24, T])
        v = sb("at_v", [P, GROUPS, 2, D])
        with nc.sbuf_tensor("at_ph", [P, KT, T], F32R) as ph, nc.sbuf_tensor("at_pl", [P, KT, T], F32R) as pl:
            sort_tokens(k, (ph, pl), falling=True)
            for g in range(GROUPS):
                project_heads(k, (ph, pl), g, VEC_AT["attn_q_gain"] + g, qT, 8 * g, scaled=True)
            sort_tokens(k, (ph, pl), falling=False)
            for g in range(GROUPS):
                src = (ph, pl) if g else k.hp
                project_heads(k, src, g, VEC_AT["attn_k_gain"] + g, kT, 8 * g, scaled=False)
                token_major(k, src, v[:, g, :, :])
        oT = k.h
        attend(k, tab0, tab12, qT, kT, v, oT)
        advance([k.at_sc, k.at_max, k.at_neg, k.at_exp, k.at_rd, k.at_diag, k.at_tr, k.at_cp, k.at_pv], 2 * AH)
        advance([k.at_o], AH // 2)
        cut(k, oT, k.hp, KT)
        linear(k, k.hp, KT, KT, dve_out=residual(k))


def sort_tokens(k, dst, falling):
    with k.nc.Block() as block:
        def part(a, j):
            by_class = k.hp[a][:, j, :].rearrange("p (m c) -> p c m", c=4).bitcast(F32)
            return dst[a][:, j, :].rearrange("p (c m) -> p c m", c=4), by_class[:, :, ::-1] if falling else by_class

        @block.vector
        def _(dve):
            for j in range(KT):
                dve.tensor_copy(*part(0, j))

        @block.scalar
        def _(act):
            for j in range(KT):
                out, src = part(1, j)
                act.activation(out, src, ACT.Copy)


def advance(signals, n):
    for s in signals:
        s.n += n


def project_heads(k, src, g, gain_col, dst, at, scaled):
    nc = k.nc
    first = k.used
    b_sq, b_ss, b_rt, b_inv, b_out = k.sq_done.n, k.sum_done.n, k.root_done.n, k.norm_done.n, k.out_done.n
    with nc.sbuf_tensor(f"ph_sq{first}", [P, 2, T], F32) as sq, nc.sbuf_tensor(f"ph_rt{first}", [P, 2, T], F32) as rt, \
            nc.sbuf_tensor(f"ph_inv{first}", [P, 2, T], F32) as inv, nc.Block() as block:
        @block.sync
        def _(sp):
            loads(k, sp, first, KT)

        @block.tensor
        def _(pe):
            w = Weights(k, pe, first)

            def project(n):
                if n >= 4:
                    pe.wait_ge(k.out_done.s, b_out + n - 3)
                for j in range(KT):
                    mm = product(pe, k.ps[:, n % 4, 0:T], w.tile(n * ITEM + j), pair_tile(src, j), start=(j == 0), stop=(j == KT - 1))
                mm.then_inc(k.item_used, 1)
            project(0)
            for n in range(KT):
                if n + 1 < KT:
                    project(n + 1)
                pe.wait_ge(k.sq_done.s, b_sq + n + 1)
                if n >= 2:
                    pe.wait_ge(k.root_done.s, b_rt + n - 1)
                pe.matmul(k.ps[:, 4 + n % 2, 0:T], const(k, "two_heads"), sq[:, n % 2, :], start=True, stop=True)\
                  .then_inc(k.sum_done.s, 1)

        @block.scalar
        def _(act):
            for n in range(KT):
                act.wait_ge(k.item_used, first + n + 1)
                if n >= 2:
                    act.wait_ge(k.sum_done.s, b_ss + n - 1)
                act.activation(sq[:, n % 2, :], k.ps[:, n % 4, 0:T], ACT.Square).then_inc(k.sq_done.s, 1)
                act.wait_ge(k.sum_done.s, b_ss + n + 1)
                if n >= 2:
                    act.wait_ge(k.norm_done.s, b_inv + n - 1)
                act.activation(rt[:, n % 2, :], k.ps[:, 4 + n % 2, 0:T], ACT.Sqrt, scale=1.0 if scaled else 1.0 / 64,
                               bias=k.eps64[:, 0:1] if scaled else k.eps[:, 0:1]).then_inc(k.root_done.s, 1)
                round_item(k, act, first + n)

        @block.gpsimd
        def _(pool):
            for n in range(KT):
                cut_item(k, pool, first + n)

        @block.vector
        def _(dve):
            for n in range(KT):
                dve.wait_ge(k.root_done.s, b_rt + n + 1)
                dve.reciprocal(inv[:, n % 2, :], rt[:, n % 2, :]).then_inc(k.norm_done.s, 1)
                dve.wait_ge(k.norm_done.s, b_inv + n + 1)
                dve.scalar_tensor_tensor(dst[:, at + n, :], k.ps[:, n % 4, 0:T], k.vec[:, gain_col:gain_col + 1],
                                         inv[:, n % 2, :], ALU.mult, ALU.mult).then_inc(k.out_done.s, 1)
    k.used += KT
    for s in (k.sq_done, k.sum_done, k.root_done, k.norm_done, k.out_done):
        s.n += KT


def attend(k, tab0, tab12, qT, kT, v, oT):
    nc = k.nc
    HG = 2
    with ExitStack() as ctx:
        def sb(name, shape, dt=F32):
            return ctx.enter_context(nc.sbuf_tensor(name, shape, dt))
        bias0 = sb("at_bias0", [P, 2, HG, 2, T])
        bias12 = sb("at_bias12", [P, 2, HG, 2, P])
        sc = sb("at_scores", [P, 2, 512])
        pr = sb("at_probs", [P, 2, 512])
        pt = sb("at_probs_t", [P, 2, 512])
        st = sb("at_stats", [P, 2, 4])
        dg = sb("at_diag", [P, 2, P])
        steps = [(h, a) for h in range(AH) for a in range(2)]
        N = len(steps)
        ident = const(k, "ident")
        s_bias, s_fill = k.at_bias, k.at_fill
        s_sc, s_max, s_neg, s_exp, s_rd, s_diag, s_tr, s_cp, s_pv, s_o = (
            k.at_sc, k.at_max, k.at_neg, k.at_exp, k.at_rd, k.at_diag, k.at_tr, k.at_cp, k.at_pv, k.at_o)
        block = ctx.enter_context(nc.Block())

        @block.sync
        def _(sp):
            sp.wait_ge(s_fill.s, 1)
            for hg in range(AH // HG):
                if hg >= 2:
                    sp.wait_ge(s_max.s, 2 * HG * (hg - 1))
                for c in range(2):
                    rows = slice(64 * c, 64 * c + 64)
                    for hh in range(HG):
                        h = hg * HG + hh
                        for a in range(2):
                            src = bass.AP(tab0.tensor, h * 512 + 3 - (2 * a + c), [[4, 64], [1, T]])
                            sp.dma_start(bias0[rows, hg % 2, hh, a, :], src).then_inc(s_bias[hg % 2].s, 16)
                    src = bass.AP(tab12.tensor, hg * HG * 2 * P, [[1, 64], [P, 2 * HG], [1, 64]])
                    sp.dma_start(bias12[rows, hg % 2, :, :, 64 * c:64 * c + 64].rearrange("p h g n -> p (h g) n"), src)\
                      .then_inc(s_bias[hg % 2].s, 16)

        @block.gpsimd
        def _(pool):
            pool.memset(bias12[:, :, :, :, :], NEG).then_inc(s_fill.s, 1)

        @block.tensor
        def _(pe):
            def scores(q):
                h, a = steps[q]
                p0, n = 64 * (h % 2), h // 2
                if q >= 2:
                    pe.wait_ge(s_max.s, q - 1)
                for g in range(GROUPS):
                    keys = slice(0, T) if g == 0 else slice(a * P, (a + 1) * P)
                    col = 0 if g == 0 else T + (g - 1) * P
                    mm = pe.matmul(k.ps[:, q % 2, col:col + (T if g == 0 else P)], qT[p0:p0 + 64, 8 * g + n, a * P:(a + 1) * P],
                                   kT[p0:p0 + 64, 8 * g + n, keys], start=True, stop=True, tile_position=(p0, 0))
                mm.then_inc(s_sc.s, 1)

            def transposed(q):
                pe.wait_ge(s_diag.s, q + 1)
                if q >= 2:
                    pe.wait_ge(s_cp.s, q - 1)
                for j in range(4):
                    mm = pe.matmul(k.ps[:, 2 + q % 2, j * P:(j + 1) * P], pr[:, q % 2, j * P:(j + 1) * P], dg[:, q % 2, :],
                                   start=True, stop=True)
                mm.then_inc(s_tr.s, 1)

            def values(q):
                h, a = steps[q]
                p0, n = 64 * (h % 2), h // 2
                pe.wait_ge(s_cp.s, q + 1)
                if q % 4 == 0 and n >= 2:
                    pe.wait_ge(s_o.s, n - 1)
                vs = [v[:, 0, 0, :], v[:, 0, 1, :], v[:, 1, a, :], v[:, 2, a, :]]
                for j in range(4):
                    mm = pe.matmul(k.ps[p0:p0 + 64, 4 + n % 2, a * P:(a + 1) * P], vs[j][:, h * 64:(h + 1) * 64],
                                   pt[:, q % 2, j * P:(j + 1) * P], start=(j == 0), stop=(j == 3), tile_position=(0, p0))
                mm.then_inc(s_pv.s, 1)
            scores(0)
            scores(1)
            for q in range(N):
                transposed(q)
                if q + 2 < N:
                    scores(q + 2)
                values(q)

        def head_pair_out(dve, n):
            dve.wait_ge(s_pv.s, 4 * (n + 1))
            dst = oT[:, n, :].rearrange("p (m c) -> p c m", c=4)
            dve.tensor_copy(dst[:, :, ::-1], k.ps[:, 4 + n % 2, 0:T].rearrange("p (c m) -> p c m", c=4))\
               .then_inc(s_o.s, 1)

        @block.vector
        def _(dve):
            def masked(q):
                h, a = steps[q]
                hg, hh = h // HG, h % HG
                dve.wait_ge(s_sc.s, q + 1)
                if a == 0 and hh == 0:
                    dve.wait_ge(s_bias[hg % 2].s, 16 * (4 * HG // 2 * 2 + 2) * (hg // 2 + 1))
                if q >= 2:
                    dve.wait_ge(s_exp.s, q - 1)
                b12 = bias12[:, hg % 2, hh, :, :].rearrange("p g n -> p (g n)")
                dve.tensor_tensor(sc[:, q % 2, 0:T], k.ps[:, q % 2, 0:T], bias0[:, hg % 2, hh, a, :], ALU.add)
                dve.tensor_tensor(sc[:, q % 2, T:512], k.ps[:, q % 2, T:512], b12, ALU.add).then_inc(s_max.s, 1)
                dve.wait_ge(s_max.s, q + 1)
                dve.tensor_reduce(st[:, q % 2, 1:2], sc[:, q % 2, :], op=ALU.max, axis=AX.X, negate=True).then_inc(s_neg.s, 1)
            masked(0)
            for q in range(N):
                if q + 1 < N:
                    masked(q + 1)
                dve.wait_ge(s_exp.s, q + 1)
                dve.reciprocal(st[:, q % 2, 3:4], st[:, q % 2, 2:3]).then_inc(s_rd.s, 1)
                dve.wait_ge(s_rd.s, q + 1)
                if q >= 2:
                    dve.wait_ge(s_tr.s, q - 1)
                dve.tensor_scalar(dg[:, q % 2, :], ident, st[:, q % 2, 3:4], None, ALU.mult).then_inc(s_diag.s, 1)
                h, a = steps[q]
                if h % 2 == 0 and a == 0 and h > 0:
                    head_pair_out(dve, h // 2 - 1)
            head_pair_out(dve, AH // 2 - 1)

        @block.scalar
        def _(act):
            def copied(q):
                act.wait_ge(s_tr.s, q + 1)
                if q >= 2:
                    act.wait_ge(s_pv.s, q - 1)
                act.activation(pt[:, q % 2, :], k.ps[:, 2 + q % 2, :], ACT.Copy).then_inc(s_cp.s, 1)
            for q in range(N):
                act.wait_ge(s_neg.s, q + 1)
                if q >= 2:
                    act.wait_ge(s_tr.s, q - 1)
                    act.wait_ge(s_rd.s, q - 1)
                act.activation(pr[:, q % 2, :], sc[:, q % 2, :], ACT.Exp, bias=st[:, q % 2, 1:2],
                               accum_out=st[:, q % 2, 2:3]).then_inc(s_exp.s, 1)
                if q > 0:
                    copied(q - 1)
            copied(N - 1)



def post_norm(k, m, gain_col):
    norm(k, m, KT, gain_col, k.h, D)
    with k.nc.Block() as block:
        @block.vector
        def _(dve):
            for j in range(KT // 2):
                dve.tensor_tensor(k.x[:, j, :], k.x[:, j, :], k.h[:, j, :], ALU.add)

        @block.gpsimd
        def _(pool):
            for j in range(KT // 2, KT):
                pool.tensor_tensor(k.x[:, j, :], k.x[:, j, :], k.h[:, j, :], ALU.add)


def store_to(dst):
    def out(dve, n, ps):
        return dve.tensor_copy(tile_of(dst, n), ps)
    return out


def ffn_second(k, layer):
    norm(k, k.x, KT, VEC_AT["norm_ffn_pre_2"] + KT * layer, k.h, D, pair=k.hp)
    with k.nc.sbuf_tensor(f"ffn_m{layer}", [P, KT, T], F32) as m:
        swiglu(k, k.hp, store_to(m))
        post_norm(k, m, VEC_AT["norm_ffn_post_2"] + KT * layer)


QL, KVL = 4, 2
MH = 8
MLA_SCALE = 192.0


def hybrid(k):
    nc = k.nc
    with ExitStack() as ctx:
        def sb(name, shape, dt=F32):
            return ctx.enter_context(nc.sbuf_tensor(name, shape, dt))
        norm(k, k.x, KT, VEC_AT["norm_mix_pre_2"], k.h, D, pair=k.hp)
        y = sb("hy_y", [P, 2 * KT, T])
        cq = sb("hy_cq", [P, QL, T])
        ckv = sb("hy_ckv", [P, KVL, T])
        kpe = sb("hy_kpe", [P, T])
        with nc.sbuf_tensor("rg_x", [P, KT, T + 3], F32) as xr, nc.sbuf_tensor("rg_gate", [P, KT, T], F32) as gate:
            with nc.Block() as block:
                @block.gpsimd
                def _(pool):
                    pool.memset(xr[:, :, 0:3], 0.0)

            def project_out(act, n, ps):
                if n < KT:
                    return act.activation(xr[:, n, 3:3 + T], ps, ACT.Copy)
                if n < 2 * KT:
                    return act.activation(gate[:, n - KT, :], ps, ACT.Gelu_apprx_tanh)
                if n < 2 * KT + QL:
                    return act.activation(cq[:, n - 2 * KT, :], ps, ACT.Copy)
                if n < 2 * KT + QL + KVL:
                    return act.activation(ckv[:, n - 2 * KT - QL, :], ps, ACT.Copy)
                return act.activation(kpe[:, :], ps, ACT.Copy)
            linear(k, k.hp, KT, 2 * KT + QL + KVL + 1, act_out=project_out)
            rg_lru(k, xr, gate, y)
        mla(k, cq, ckv, kpe, y)
        with nc.sbuf_tensor("hy_m", [P, KT, T], F32) as m, nc.sbuf_tensor("hy_yh", [P, 2 * KT, T], F32R) as yh, \
                nc.sbuf_tensor("hy_yl", [P, 2 * KT, T], F32R) as yl:
            cut(k, y, (yh, yl), 2 * KT)
            linear(k, (yh, yl), 2 * KT, KT, dve_out=store_to(m))
            post_norm(k, m, VEC_AT["norm_mix_post_2"])


def rg_lru(k, xr, gate, y):
    nc = k.nc
    first = k.used
    V, A = k.s5v, k.s5a
    lam = VEC_AT["rg_lambda_2"]
    with ExitStack() as ctx:
        def sb(name, shape, dt=F32):
            return ctx.enter_context(nc.sbuf_tensor(name, shape, dt))
        col = sb("rg_col", [P, 6, KT])
        xc = sb("rg_xc", [P, KT, T])
        xch, xcl = sb("rg_xch", [P, KT, T], F32R), sb("rg_xcl", [P, KT, T], F32R)
        r = sb("rg_r", [P, 2, T])
        i_ = sb("rg_i", [P, 2, T])
        a_ = sb("rg_a", [P, 2, T])
        th = sb("rg_t", [P, 2, T])
        rc = sb("rg_rc", [P, 2, 2, T])
        cf = sb("rg_cf", [P, 2, T])
        b = sb("rg_b", [P, 2, 2, T])
        hs = sb("rg_h", [P, 2, T])
        v0, a0 = V.n, A.n
        b_cr, b_cl = k.cut_round.n, k.cut_low.n
        s_xc, s_gate, s_sig, s_at, s_q, s_root, s_fin = (k.rg_xc, k.rg_gate, k.rg_sig, k.rg_at, k.rg_q, k.rg_root, k.rg_fin)
        block = ctx.enter_context(nc.Block())
        lcol = k.vec[:, lam:lam + KT]

        @block.sync
        def _(sp):
            loads(k, sp, first, 2)

        @block.gpsimd
        def _(pool):
            for n in range(KT):
                pool.wait_ge(k.cut_round.s, b_cr + n + 1)
                pool.tensor_tensor(xcl[:, n, :], xc[:, n, :], xch[:, n, :].bitcast(F32), ALU.subtract).then_inc(k.cut_low.s, 1)
            for item in range(2):
                cut_item(k, pool, first + item)

        @block.tensor
        def _(pe):
            w = Weights(k, pe, first)
            for n in range(KT):
                pe.wait_ge(k.cut_low.s, b_cl + n + 1)
                if n >= 2:
                    pe.wait_ge(s_sig.s, n - 1)
                for half in range(2):
                    mm = product(pe, k.ps[:, n % 2, half * T:(half + 1) * T], w.tile(2 * n + half), (xch[:, n, :], xcl[:, n, :]),
                                 start=True, stop=True)
                if n % 4 == 3:
                    mm.then_inc(k.item_used, 1)
                else:
                    mm.then_inc(s_gate.s, 1)

        def gates_ready(n):
            return (k.item_used, first + n // 4 + 1) if n % 4 == 3 else (s_gate.s, 3 * (n // 4) + n % 4 + 1)

        @block.scalar
        def _(act):
            act.activation(col[:, 0, :], lcol, ACT.Abs).then_inc(A.s, 1)
            act.wait_ge(A.s, a0 + 1)
            act.activation(col[:, 1, :], col[:, 0, :], ACT.Exp, scale=-1.0).then_inc(A.s, 1)
            act.wait_ge(A.s, a0 + 2)
            act.activation(col[:, 2, :], col[:, 1, :], ACT.Ln, bias=k.one_c[:, 0:1]).then_inc(A.s, 1)
            for n in range(KT):
                act.wait_ge(s_xc.s, n + 1)
                act.activation(xch[:, n, :], xc[:, n, :], ACT.Copy).then_inc(k.cut_round.s, 1)
            act.wait_ge(V.s, v0 + 3)
            for n in range(KT):
                act.wait_ge(*gates_ready(n))
                if n >= 2:
                    act.wait_ge(s_fin.s, n - 1)
                ba, bx = VEC_AT["rg_gate_a_b_2"] + n, VEC_AT["rg_gate_x_b_2"] + n
                act.activation(r[:, n % 2, :], k.ps[:, n % 2, 0:T], ACT.Sigmoid, bias=k.vec[:, ba:ba + 1])
                act.activation(i_[:, n % 2, :], k.ps[:, n % 2, T:2 * T], ACT.Sigmoid, bias=k.vec[:, bx:bx + 1]).then_inc(s_sig.s, 1)
                act.wait_ge(s_sig.s, n + 1)
                act.activation(th[:, n % 2, :], r[:, n % 2, :], ACT.Tanh, scale=col[:, 5, n:n + 1])
                act.activation(a_[:, n % 2, :], r[:, n % 2, :], ACT.Exp, scale=col[:, 4, n:n + 1]).then_inc(s_at.s, 1)
                act.wait_ge(s_q.s, n + 1)
                act.activation(cf[:, n % 2, :], rc[:, n % 2, 1, :], ACT.Sqrt, scale=2.0).then_inc(s_root.s, 1)
                if n % 4 == 3:
                    round_item(k, act, first + n // 4)

        @block.vector
        def _(dve):
            cnt = [v0]

            def tick(ins):
                cnt[0] += 1
                ins.then_inc(V.s, 1)
                dve.wait_ge(V.s, cnt[0])
            dve.wait_ge(A.s, a0 + 3)
            tick(dve.tensor_scalar(col[:, 3, :], lcol, -1.0, 0.0, ALU.mult, ALU.max))
            dve.tensor_tensor(col[:, 3, :], col[:, 3, :], col[:, 2, :], ALU.add).then_inc(V.s, 1)
            cnt[0] += 1
            dve.wait_ge(V.s, cnt[0])
            dve.tensor_scalar(col[:, 5, :], col[:, 3, :], 8.0, None, ALU.mult)
            tick(dve.tensor_scalar(col[:, 4, :], col[:, 3, :], -8.0, None, ALU.mult))
            for n in range(KT):
                for j in range(4):
                    wc = VEC_AT["rg_conv_w_2"] + KT * j + n
                    bc = VEC_AT["rg_conv_b_2"] + n
                    if j == 0:
                        tick(dve.tensor_scalar(xc[:, n, :], xr[:, n, 0:T], k.vec[:, wc:wc + 1], k.vec[:, bc:bc + 1], ALU.mult, ALU.add))
                    else:
                        ins = dve.scalar_tensor_tensor(xc[:, n, :], xr[:, n, j:j + T], k.vec[:, wc:wc + 1], xc[:, n, :], ALU.mult, ALU.add)
                        if j < 3:
                            tick(ins)
                        else:
                            ins.then_inc(s_xc.s, 1)
            dve.wait_ge(s_xc.s, KT)
            for n in range(KT):
                s = n % 2
                dve.wait_ge(s_at.s, n + 1)
                tick(dve.tensor_scalar(rc[:, s, 0, :], th[:, s, :], 1.0, None, ALU.add))
                tick(dve.reciprocal(rc[:, s, 1, :], rc[:, s, 0, :]))
                dve.tensor_tensor(rc[:, s, 1, :], rc[:, s, 1, :], th[:, s, :], ALU.mult).then_inc(s_q.s, 1)
                tick(dve.tensor_tensor(b[:, s, 0, :], i_[:, s, :], xc[:, n, :], ALU.mult))
                dve.wait_ge(s_root.s, n + 1)
                tick(dve.tensor_tensor(b[:, s, 1, :], b[:, s, 0, :], cf[:, s, :], ALU.mult))
                tick(dve.tensor_tensor_scan(hs[:, s, :], a_[:, s, :], b[:, s, 1, :], 0.0, ALU.mult, ALU.add))
                dve.tensor_tensor(y[:, n, :], hs[:, s, :], gate[:, n, :], ALU.mult).then_inc(s_fin.s, 1)
            V.n = cnt[0]
    A.n += 3
    k.cut_round.n += KT
    k.cut_low.n += KT
    k.used += 2


def mla(k, cq, ckv, kpe, y):
    nc = k.nc
    with ExitStack() as ctx:
        def sb(name, shape, dt=F32):
            return ctx.enter_context(nc.sbuf_tensor(name, shape, dt))
        q = sb("mla_q", [P, MH + MH // 2, T])
        kn = sb("mla_k", [P, MH, T])
        v = sb("mla_v", [P, 2, D])
        kr = sb("mla_kr", [P, T])
        cs = sb("mla_cs", [P, 2, T])
        cn = sb("mla_cn", [P, QL, T])
        kvn = sb("mla_kvn", [P, KVL, T])
        cnp = sb("mla_cnh", [P, QL, T], F32R), sb("mla_cnl", [P, QL, T], F32R)
        kvp = sb("mla_kvh", [P, KVL, T], F32R), sb("mla_kvl", [P, KVL, T], F32R)
        norm(k, cq, QL, VEC_AT["mla_q_norm_2"], cn, QL * P, times=MLA_SCALE, pair=cnp)
        norm(k, ckv, KVL, VEC_AT["mla_kv_norm_2"], kvn, KVL * P, pair=kvp)
        linear(k, cnp, QL, MH + MH // 2, dve_out=store_to(q))
        linear(k, kvp, KVL, MH, dve_out=store_to(kn))
        token_major(k, kvp, v, KVL)
        rope(k, q, kpe, kr, cs)
        mla_attend(k, q, kn, kr, v, y)


def rope(k, q, kpe, kr, cs):
    nc = k.nc
    C1 = 6.28125
    C2 = 2 * math.pi - C1
    V, A = k.s5v, k.s5a
    with ExitStack() as ctx:
        def sb(name, shape, dt=F32):
            return ctx.enter_context(nc.sbuf_tensor(name, shape, dt))
        posi = sb("rope_pos", [P, T], I32)
        w = sb("rope_w", [P, 5, T])
        pr = sb("rope_pr", [P, 2, 2, T])
        v0, a0, i0 = V.n, A.n, k.side_here.n
        block = ctx.enter_context(nc.Block())
        tiles_ = [(q[:, MH + j, :], q[:, MH + j, :]) for j in range(MH // 2)] + [(kpe[:, :], kr[:, :])]

        @block.sync
        def _(sp):
            sp.dma_start(posi[:, :], k.ins["positions"].broadcast_to([P, T])).then_inc(k.side_here.s, 16)

        @block.tensor
        def _(pe):
            for j, (x, _) in enumerate(tiles_):
                if j >= 2:
                    pe.wait_ge(k.rope_out.s, j - 1)
                pe.matmul(k.ps[:, j % 2, 0:T], const(k, "rope_swap"), x, start=True, stop=True).then_inc(k.rope_sw.s, 1)

        @block.scalar
        def _(act):
            act.wait_ge(V.s, v0 + 7)
            act.activation(w[:, 3, :], w[:, 2, :], ACT.Abs).then_inc(A.s, 1)
            act.activation(cs[:, 1, :], w[:, 2, :], ACT.Sin).then_inc(A.s, 1)
            act.wait_ge(A.s, a0 + 1)
            act.activation(cs[:, 0, :], w[:, 3, :], ACT.Sin, scale=-1.0, bias=k.half_pi[:, 0:1]).then_inc(A.s, 1)

        @block.vector
        def _(dve):
            cnt = [v0]

            def tick(ins):
                cnt[0] += 1
                ins.then_inc(V.s, 1)
                dve.wait_ge(V.s, cnt[0])
            dve.wait_ge(k.side_here.s, i0 + 16)
            tick(dve.tensor_copy(w[:, 0, :], posi[:, :]))
            tick(dve.tensor_scalar(w[:, 1, :], w[:, 0, :], const(k, "inv_freq"), None, ALU.mult))
            tick(dve.tensor_scalar(w[:, 2, :], w[:, 1, :], 1.0 / (2 * math.pi), ROUND, ALU.mult, ALU.add))
            tick(dve.tensor_scalar(w[:, 4, :], w[:, 2, :], -ROUND, None, ALU.add))
            tick(dve.scalar_tensor_tensor(w[:, 0, :], w[:, 4, :], -C1, w[:, 1, :], ALU.mult, ALU.add))
            tick(dve.scalar_tensor_tensor(w[:, 1, :], w[:, 4, :], -C2, w[:, 0, :], ALU.mult, ALU.add))
            tick(dve.tensor_scalar(w[:, 2, :], w[:, 1, :], 3.1415925, -3.1415925, ALU.min, ALU.max))
            dve.wait_ge(A.s, a0 + 3)
            for j, (x, out) in enumerate(tiles_):
                dve.wait_ge(k.rope_sw.s, j + 1)
                dve.tensor_tensor(pr[:, j % 2, 0, :], x, cs[:, 0, :], ALU.mult)
                dve.tensor_tensor(pr[:, j % 2, 1, :], k.ps[:, j % 2, 0:T], cs[:, 1, :], ALU.mult).then_inc(k.rope_out.s, 1)
                dve.wait_ge(k.rope_out.s, j + 1)
                dve.tensor_tensor(out, pr[:, j % 2, 0, :], pr[:, j % 2, 1, :], ALU.add)
            V.n = cnt[0]
        A.n += 3
        k.side_here.n += 16


def mla_attend(k, q, kn, kr, v, y):
    nc = k.nc
    with ExitStack() as ctx:
        def sb(name, shape, dt=F32):
            return ctx.enter_context(nc.sbuf_tensor(name, shape, dt))
        sc = sb("ma_scores", [P, 2, T])
        pr = sb("ma_probs", [P, 2, T])
        pt = sb("ma_probs_t", [P, 2, T])
        st = sb("ma_stats", [P, 2, 4])
        dg = sb("ma_diag", [P, 2, P])
        steps = [(h, a) for h in range(MH) for a in range(2)]
        N = len(steps)
        at = {"sc": k.at_sc, "max": k.at_max, "neg": k.at_neg, "exp": k.at_exp, "rd": k.at_rd, "diag": k.at_diag,
              "tr": k.at_tr, "cp": k.at_cp, "pv": k.at_pv, "o": k.at_o}
        s_ = {name: one.s for name, one in at.items()}
        b_ = {name: one.n for name, one in at.items()}
        block = ctx.enter_context(nc.Block())

        @block.tensor
        def _(pe):
            def scores(i):
                h, a = steps[i]
                p0, n = 64 * (h % 2), (a + 1) * P
                if i >= 2:
                    pe.wait_ge(s_["max"], b_["max"] + i - 1)
                pe.matmul(k.ps[:, i % 2, 0:n], q[:, h, a * P:(a + 1) * P], kn[:, h, 0:n], start=True, stop=False)
                pe.matmul(k.ps[:, i % 2, 0:n], q[p0:p0 + 64, MH + h // 2, a * P:(a + 1) * P], kr[p0:p0 + 64, 0:n],
                          start=False, stop=True, tile_position=(p0, 0)).then_inc(s_["sc"], 1)

            def transposed(i):
                h, a = steps[i]
                pe.wait_ge(s_["diag"], b_["diag"] + i + 1)
                if i >= 2:
                    pe.wait_ge(s_["cp"], b_["cp"] + i - 1)
                for j in range(a + 1):
                    mm = pe.matmul(k.ps[:, 2 + i % 2, j * P:(j + 1) * P], pr[:, i % 2, j * P:(j + 1) * P], dg[:, i % 2, :],
                                   start=True, stop=True)
                mm.then_inc(s_["tr"], 1)

            def values(i):
                h, a = steps[i]
                pe.wait_ge(s_["cp"], b_["cp"] + i + 1)
                if a == 0 and h >= 2:
                    pe.wait_ge(s_["o"], b_["o"] + h - 1)
                for j in range(a + 1):
                    mm = pe.matmul(k.ps[:, 4 + h % 2, a * P:(a + 1) * P], v[:, j, h * P:(h + 1) * P],
                                   pt[:, i % 2, j * P:(j + 1) * P], start=(j == 0), stop=(j == a))
                mm.then_inc(s_["pv"], 1)
            scores(0)
            scores(1)
            for i in range(N):
                transposed(i)
                if i + 2 < N:
                    scores(i + 2)
                values(i)

        @block.vector
        def _(dve):
            mask = const(k, "causal")

            def masked(i):
                h, a = steps[i]
                n = (a + 1) * P
                dve.wait_ge(s_["sc"], b_["sc"] + i + 1)
                if i >= 2:
                    dve.wait_ge(s_["exp"], b_["exp"] + i - 1)
                dve.tensor_tensor(sc[:, i % 2, 0:n], k.ps[:, i % 2, 0:n], mask[:, T - n:T], ALU.add).then_inc(s_["max"], 1)
                dve.wait_ge(s_["max"], b_["max"] + i + 1)
                dve.tensor_reduce(st[:, i % 2, 1:2], sc[:, i % 2, 0:n], op=ALU.max, axis=AX.X, negate=True).then_inc(s_["neg"], 1)

            def head_out(h):
                dve.wait_ge(s_["pv"], b_["pv"] + 2 * (h + 1))
                dve.tensor_copy(y[:, KT + h, :], k.ps[:, 4 + h % 2, 0:T]).then_inc(s_["o"], 1)
            masked(0)
            for i in range(N):
                if i + 1 < N:
                    masked(i + 1)
                dve.wait_ge(s_["exp"], b_["exp"] + i + 1)
                dve.reciprocal(st[:, i % 2, 3:4], st[:, i % 2, 2:3]).then_inc(s_["rd"], 1)
                dve.wait_ge(s_["rd"], b_["rd"] + i + 1)
                if i >= 2:
                    dve.wait_ge(s_["tr"], b_["tr"] + i - 1)
                dve.tensor_scalar(dg[:, i % 2, :], const(k, "ident"), st[:, i % 2, 3:4], None, ALU.mult).then_inc(s_["diag"], 1)
                h, a = steps[i]
                if a == 0 and h > 0:
                    head_out(h - 1)
            head_out(MH - 1)

        @block.scalar
        def _(act):
            def copied(i):
                n = (steps[i][1] + 1) * P
                act.wait_ge(s_["tr"], b_["tr"] + i + 1)
                if i >= 2:
                    act.wait_ge(s_["pv"], b_["pv"] + i - 1)
                act.activation(pt[:, i % 2, 0:n], k.ps[:, 2 + i % 2, 0:n], ACT.Copy).then_inc(s_["cp"], 1)
            for i in range(N):
                n = (steps[i][1] + 1) * P
                act.wait_ge(s_["neg"], b_["neg"] + i + 1)
                if i >= 2:
                    act.wait_ge(s_["tr"], b_["tr"] + i - 1)
                    act.wait_ge(s_["rd"], b_["rd"] + i - 1)
                act.activation(pr[:, i % 2, 0:n], sc[:, i % 2, 0:n], ACT.Exp, bias=st[:, i % 2, 1:2],
                               accum_out=st[:, i % 2, 2:3]).then_inc(s_["exp"], 1)
                if i > 0:
                    copied(i - 1)
            copied(N - 1)



GH = 16
GC = 64
LEVELS = 6


def gdn(k):
    nc = k.nc
    with ExitStack() as ctx:
        def sb(name, shape, dt=F32):
            return ctx.enter_context(nc.sbuf_tensor(name, shape, dt))
        norm(k, k.x, KT, VEC_AT["norm_mix_pre_2"] + KT, k.h, D, pair=k.hp)
        col = sb("gdn_col", [P, 2, 6, GH])
        qk = sb("gdn_qk", [P, GH, T])
        v = sb("gdn_v", [P, GH, T])
        z = sb("gdn_z", [P, GH, T])
        gdn_gates(k, col)
        conv_silu(k, qk, v)

        def silu_out(act, n, ps):
            return act.activation(tile_of(z, n), ps, ACT.Silu)
        linear(k, k.hp, KT, GH, act_out=silu_out)
        l2_norms(k, qk)
        delta_rule(k, col, qk, v)
        head_norms(k, v, z)
        with nc.sbuf_tensor("gdn_m", [P, KT, T], F32) as m, nc.sbuf_tensor("gdn_vh", [P, 2 * KT, T], F32R) as vh, \
                nc.sbuf_tensor("gdn_vl", [P, 2 * KT, T], F32R) as vl:
            cut(k, v, (vh, vl), 2 * KT)
            linear(k, (vh, vl), 2 * KT, KT, dve_out=store_to(m))
            post_norm(k, m, VEC_AT["norm_mix_post_2"] + KT)


def gdn_gates(k, col):
    nc = k.nc
    V, A = k.s5v, k.s5a
    with ExitStack() as ctx:
        def sb(name, shape, dt=F32):
            return ctx.enter_context(nc.sbuf_tensor(name, shape, dt))
        wba = sb("gg_w", [P, KT, 2 * GH])
        par = sb("gg_par", [P, 2, GH])
        zz = sb("gg_z", [P, 2, 2, GH])
        e = sb("gg_e", [P, 4, 2, 2, GH])
        ea = sb("gg_ea", [P, GH])
        t0 = sb("gg_t", [P, 2, 2, GH])
        v0, a0, i0 = V.n, A.n, k.side_here.n
        block = ctx.enter_context(nc.Block())

        @block.sync
        def _(sp):
            sp.dma_start(wba[:, :, :].rearrange("p k n -> p (k n)"), k.ins["gdn_ba"]).then_inc(k.side_here.s, 16)
            sp.dma_start(par[:, 0, :], k.ins["gdn_a_log"].broadcast_to([P, GH])).then_inc(k.side_here.s, 16)
            sp.dma_start(par[:, 1, :], k.ins["gdn_dt_bias"].broadcast_to([P, GH])).then_inc(k.side_here.s, 16)

        @block.tensor
        def _(pe):
            pe.wait_ge(k.side_here.s, i0 + 48)
            for a in range(2):
                for j in range(KT):
                    mm = pe.matmul(k.ps[:, a, 0:2 * GH], k.h[:, j, a * P:(a + 1) * P], wba[:, j, :], start=(j == 0), stop=(j == KT - 1))
            mm.then_inc(k.gg_ba.s, 1)
            pe.wait_ge(k.gg_g.s, 1)
            for a in range(2):
                pe.matmul(k.ps[:, 2 + a, 0:GH], const(k, "cumulate")[:, 0:P], col[:, a, 4, :], start=True, stop=True)
                mm = pe.matmul(k.ps[:, 4 + a, 0:GH], const(k, "chunk_sum"), col[:, a, 4, :], start=True, stop=True)
            mm.then_inc(k.gg_gc.s, 1)

        @block.scalar
        def _(act):
            act.wait_ge(k.side_here.s, i0 + 48)
            act.activation(ea[:, :], par[:, 0, :], ACT.Exp).then_inc(A.s, 1)
            act.wait_ge(V.s, v0 + 4)
            act.activation(e[:, 0, :, :, :], zz[:, :, :, :], ACT.Abs).then_inc(A.s, 1)
            act.wait_ge(A.s, a0 + 2)
            act.activation(e[:, 1, :, :, :], e[:, 0, :, :, :], ACT.Exp, scale=-1.0).then_inc(A.s, 1)
            act.wait_ge(A.s, a0 + 3)
            act.activation(e[:, 2, :, :, :], e[:, 1, :, :, :], ACT.Ln, bias=k.one_c[:, 0:1]).then_inc(A.s, 1)
            act.wait_ge(V.s, v0 + 9)
            act.activation(col[:, :, 0, :], col[:, :, 5, :], ACT.Exp).then_inc(A.s, 1)
            act.wait_ge(V.s, v0 + 12)
            act.activation(col[:, :, 2, :], t0[:, :, 0, :], ACT.Exp)
            act.activation(col[:, :, 3, :], t0[:, :, 1, :], ACT.Exp)

        @block.vector
        def _(dve):
            cnt = [v0]

            def tick(ins):
                cnt[0] += 1
                ins.then_inc(V.s, 1)
                dve.wait_ge(V.s, cnt[0])
            dve.wait_ge(k.gg_ba.s, 1)
            for a in range(2):
                tick(dve.tensor_scalar(zz[:, a, 0, :], k.ps[:, a, 0:GH], -1.0, None, ALU.mult))
                tick(dve.tensor_tensor(zz[:, a, 1, :], k.ps[:, a, GH:2 * GH], par[:, 1, :], ALU.add))
            tick(dve.tensor_scalar(e[:, 3, :, :, :], zz[:, :, :, :], 0.0, None, ALU.max))
            dve.wait_ge(A.s, a0 + 4)
            tick(dve.tensor_tensor(e[:, 0, :, :, :], e[:, 3, :, :, :], e[:, 2, :, :, :], ALU.add))
            for a in range(2):
                dve.scalar_tensor_tensor(col[:, a, 4, :], e[:, 0, a, 1, :], -1.0, ea[:, :], ALU.mult, ALU.mult)\
                   .then_inc(V.s, 1)
                cnt[0] += 1
            tick(dve.tensor_scalar(col[:, :, 5, :], e[:, 0, :, 0, :], -1.0, None, ALU.mult))
            dve.sem_inc(k.gg_g.s, 1)
            dve.wait_ge(k.gg_gc.s, 1)
            tick(dve.tensor_scalar(col[:, :, 1, :], k.ps[:, 2:4, 0:GH], -1.0, None, ALU.mult))
            tick(dve.tensor_tensor(t0[:, :, 0, :], col[:, :, 5, :], col[:, :, 1, :], ALU.subtract))
            tick(dve.tensor_tensor(t0[:, :, 1, :], k.ps[:, 4:6, 0:GH], col[:, :, 1, :], ALU.add))
            V.n = cnt[0]
        A.n += 5
        k.side_here.n += 48


def conv_silu(k, qk, v):
    first = k.used
    nt = 2 * GH
    V = k.s5v
    with k.nc.sbuf_tensor("conv_acc", [P, 2, T], F32) as acc, k.nc.Block() as block:
        v0 = V.n

        @block.sync
        def _(sp):
            loads(k, sp, first, nt)

        @block.tensor
        def _(pe):
            w = Weights(k, pe, first)
            for n in range(nt):
                if n >= 4:
                    pe.wait_ge(V.s, v0 + 4 * (n - 3))
                for j in range(KT):
                    mm = product(pe, k.ps[:, n % 4, 0:T], w.tile(n * ITEM + j), pair_tile(k.hp, j), start=(j == 0), stop=(j == KT - 1))
                mm.then_inc(k.item_used, 1)

        @block.vector
        def _(dve):
            for n in range(nt):
                dve.wait_ge(k.item_used, first + n + 1)
                if n >= 2:
                    dve.wait_ge(k.cv_silu.s, n - 1)
                for s in range(4):
                    c = VEC_AT["gdn_conv_w_2"] + nt * (3 - s) + n
                    wc = k.vec[:, c:c + 1]
                    if s == 0:
                        ins = dve.tensor_scalar(acc[:, n % 2, :], k.ps[:, n % 4, 0:T], wc, None, ALU.mult)
                    else:
                        ins = dve.scalar_tensor_tensor(acc[:, n % 2, s:T], k.ps[:, n % 4, 0:T - s], wc, acc[:, n % 2, s:T],
                                                       ALU.mult, ALU.add)
                    ins.then_inc(V.s, 1)
                    if s < 3:
                        dve.wait_ge(V.s, v0 + 4 * n + s + 1)

        @block.scalar
        def _(act):
            for n in range(nt):
                act.wait_ge(V.s, v0 + 4 * (n + 1))
                dst = qk[:, n, :] if n < GH else v[:, n - GH, :]
                act.activation(dst, acc[:, n % 2, :], ACT.Silu).then_inc(k.cv_silu.s, 1)
                round_item(k, act, first + n)

        @block.gpsimd
        def _(pool):
            for n in range(nt):
                cut_item(k, pool, first + n)
    V.n += 4 * nt
    k.used += nt


def l2_norms(k, qk):
    with k.nc.sbuf_tensor("l2_sq", [P, 2, 2 * T], F32) as sq, k.nc.sbuf_tensor("l2_rt", [P, 2, 2 * T], F32) as rt, \
            k.nc.sbuf_tensor("l2_inv", [P, 2, 2 * T], F32) as inv, k.nc.Block() as block:
        b_sq, b_ss, b_rt, b_inv, b_m = k.sq_done.n, k.sum_done.n, k.root_done.n, k.norm_done.n, k.mul_done.n

        def pair(t3, n):
            return t3[:, 2 * n:2 * n + 2, :].rearrange("p a n -> p (a n)")

        @block.tensor
        def _(pe):
            for n in range(KT):
                pe.wait_ge(k.sq_done.s, b_sq + n + 1)
                if n >= 2:
                    pe.wait_ge(k.root_done.s, b_rt + n - 1)
                pe.matmul(k.ps[:, n % 2, :], k.ones[:, :], sq[:, n % 2, :], start=True, stop=True).then_inc(k.sum_done.s, 1)

        @block.scalar
        def _(act):
            def square(n):
                if n >= 2:
                    act.wait_ge(k.sum_done.s, b_ss + n - 1)
                act.activation(sq[:, n % 2, :], pair(qk, n), ACT.Square).then_inc(k.sq_done.s, 1)
            square(0)
            for n in range(KT):
                if n + 1 < KT:
                    square(n + 1)
                act.wait_ge(k.sum_done.s, b_ss + n + 1)
                if n >= 2:
                    act.wait_ge(k.norm_done.s, b_inv + n - 1)
                query = n < KT // 2
                act.activation(rt[:, n % 2, :], k.ps[:, n % 2, :], ACT.Sqrt, scale=float(P) if query else 1.0,
                               bias=(k.eps128 if query else k.eps)[:, 0:1]).then_inc(k.root_done.s, 1)

        @block.vector
        def _(dve):
            for n in range(KT):
                dve.wait_ge(k.root_done.s, b_rt + n + 1)
                if n >= 2:
                    dve.wait_ge(k.mul_done.s, b_m + n - 1)
                dve.reciprocal(inv[:, n % 2, :], rt[:, n % 2, :]).then_inc(k.norm_done.s, 1)

        @block.gpsimd
        def _(pool):
            for n in range(KT):
                pool.wait_ge(k.norm_done.s, b_inv + n + 1)
                pool.tensor_tensor(pair(qk, n), pair(qk, n), inv[:, n % 2, :], ALU.mult).then_inc(k.mul_done.s, 1)
    for s in (k.sq_done, k.sum_done, k.root_done, k.norm_done, k.mul_done):
        s.n += KT


def head_norms(k, o, z):
    with k.nc.sbuf_tensor("hn_sq", [P, 2, 2 * T], F32) as sq, k.nc.sbuf_tensor("hn_rt", [P, 2, 2 * T], F32) as rt, \
            k.nc.sbuf_tensor("hn_inv", [P, 2, 2 * T], F32) as inv, k.nc.Block() as block:
        b_sq, b_ss, b_rt, b_inv, b_m = k.sq_done.n, k.sum_done.n, k.root_done.n, k.norm_done.n, k.mul_done.n
        gain = k.vec[:, VEC_AT["gdn_norm_2"]:VEC_AT["gdn_norm_2"] + 1]

        def pair(t3, n):
            return t3[:, 2 * n:2 * n + 2, :].rearrange("p a n -> p (a n)")

        @block.tensor
        def _(pe):
            for n in range(KT):
                pe.wait_ge(k.sq_done.s, b_sq + n + 1)
                if n >= 2:
                    pe.wait_ge(k.root_done.s, b_rt + n - 1)
                pe.matmul(k.ps[:, n % 2, :], k.ones[:, :], sq[:, n % 2, :], start=True, stop=True).then_inc(k.sum_done.s, 1)

        @block.scalar
        def _(act):
            def square(n):
                if n >= 2:
                    act.wait_ge(k.sum_done.s, b_ss + n - 1)
                act.activation(sq[:, n % 2, :], pair(o, n), ACT.Square).then_inc(k.sq_done.s, 1)
            square(0)
            for n in range(KT):
                if n + 1 < KT:
                    square(n + 1)
                act.wait_ge(k.sum_done.s, b_ss + n + 1)
                if n >= 2:
                    act.wait_ge(k.norm_done.s, b_inv + n - 1)
                act.activation(rt[:, n % 2, :], k.ps[:, n % 2, :], ACT.Sqrt, scale=1.0 / P, bias=k.eps[:, 0:1])\
                   .then_inc(k.root_done.s, 1)

        @block.vector
        def _(dve):
            for n in range(KT):
                dve.wait_ge(k.root_done.s, b_rt + n + 1)
                if n >= 2:
                    dve.wait_ge(k.mul_done.s, b_m + n - 1)
                dve.reciprocal(inv[:, n % 2, :], rt[:, n % 2, :]).then_inc(k.hn_inv.s, 1)
                dve.wait_ge(k.hn_inv.s, n + 1)
                dve.scalar_tensor_tensor(inv[:, n % 2, :], pair(z, n), gain, inv[:, n % 2, :], ALU.mult, ALU.mult)\
                   .then_inc(k.norm_done.s, 1)

        @block.gpsimd
        def _(pool):
            for n in range(KT):
                pool.wait_ge(k.norm_done.s, b_inv + n + 1)
                pool.tensor_tensor(pair(o, n), pair(o, n), inv[:, n % 2, :], ALU.mult).then_inc(k.mul_done.s, 1)
    for s in (k.sq_done, k.sum_done, k.root_done, k.norm_done, k.mul_done):
        s.n += KT


def delta_rule(k, col, qk, v):
    nc = k.nc
    HG = 4
    NG = GH // HG
    with ExitStack() as ctx:
        def sb(name, shape, dt=F32):
            return ctx.enter_context(nc.sbuf_tensor(name, shape, dt))
        ktok = sb("dr_ktok", [P, 2, 2, P])
        bv = sb("dr_bv", [P, 2, HG, P])
        E = sb("dr_e", [P, 2, HG, 2, P])
        kbg, kdec = E[:, :, :, 0, :], E[:, :, :, 1, :]
        AQ = sb("dr_aq", [P, 2, HG, 2, P])
        MT = sb("dr_mt", [P, 2, HG, P])
        X = sb("dr_x", [P, 2, HG, P])
        XT = sb("dr_xt", [P, 2, HG, P])
        Ps = sb("dr_ps", [P, 2, HG, P])
        u = sb("dr_u", [P, 2, HG, P])
        wT = sb("dr_wt", [P, 2, HG, P])
        qd = k.h[:, 0:HG, :]
        rx = k.h[:, HG:2 * HG, :]
        S = sb("dr_s", [P, 2, HG, P])
        Sd = sb("dr_sd", [P, HG, P])
        g = Space()
        g.vt = k.sem("gdn_values_transposed")
        g.kt = k.sem("gdn_keys_transposed")
        g.gq = k.sem("gdn_products_and_rows")
        g.vc = k.sem("gdn_beta_values")
        g.kc = k.sem("gdn_keys_copied")
        g.re = k.sem("gdn_row_exp")
        g.t = k.sem("gdn_rows_masked")
        g.e = k.sem("gdn_decays")
        g.aq = k.sem("gdn_a_and_q")
        g.qd = k.sem("gdn_queries_decayed")
        g.kb = k.sem("gdn_keys_scaled")
        g.mt = k.sem("gdn_level_part")
        g.p = k.sem("gdn_m_x")
        g.pc = k.sem("gdn_m_x_copied")
        g.px = k.sem("gdn_x_m_x")
        g.x = k.sem("gdn_x_updated")
        g.u = k.sem("gdn_u_in_psum")
        g.w = k.sem("gdn_w_in_psum")
        g.uc = k.sem("gdn_u_copied")
        g.wc = k.sem("gdn_w_copied")
        g.ws = k.sem("gdn_w_state")
        g.vn = k.sem("gdn_u_corrected")
        g.kv = k.sem("gdn_keys_u")
        g.o = k.sem("gdn_chunk_output")
        g.oc = k.sem("gdn_output_copied")
        g.s = k.sem("gdn_state")
        g.sd = k.sem("gdn_state_decayed")
        block = ctx.enter_context(nc.Block())
        ident, cum = const(k, "ident"), const(k, "cumulate")
        lmask = const(k, "levels").rearrange("p (l n) -> p l n", l=LEVELS)
        dmask = const(k, "decay_mask")
        levels = range(1, LEVELS + 1)

        def four(bank):
            return k.ps[:, bank, :].rearrange("p (h n) -> p h n", h=HG)

        def q_of(hg, kh):
            return qk[:, 2 * hg + kh, :]

        def k_of(hg, kh):
            return qk[:, KT + 2 * hg + kh, :]

        @block.tensor
        def _(pe):
            for hg in range(NG):
                U = 2 * hg
                for a in range(2):
                    rows = slice(a * P, (a + 1) * P)
                    if a == 1:
                        pe.wait_ge(g.vc, U + 1)
                        pe.wait_ge(g.kc, U + 1)
                    elif hg:
                        pe.wait_ge(g.uc, U)
                        pe.wait_ge(g.wc, U)
                        pe.wait_ge(g.oc, 4 * hg)
                    for hh in range(HG):
                        mm = pe.transpose(k.ps[:, 6, hh * P:(hh + 1) * P], v[:, HG * hg + hh, rows], ident)
                    mm.then_inc(g.vt, 1)
                    for kh in range(2):
                        mm = pe.transpose(k.ps[:, 7, kh * P:(kh + 1) * P], k_of(hg, kh)[:, rows], ident)
                    mm.then_inc(g.kt, 1)
                    for kh in range(2):
                        for half, rhs in enumerate((k_of(hg, kh), q_of(hg, kh))):
                            pe.matmul(k.ps[:, a, (2 * kh + half) * P:(2 * kh + half + 1) * P], k_of(hg, kh)[:, rows], rhs[:, rows],
                                      start=True, stop=True)
                    for hh in range(HG):
                        h = HG * hg + hh
                        bank, c = 2 + 2 * a + hh // 2, hh % 2 * 2 * P
                        pe.matmul(k.ps[:, bank, c:c + 2 * P], spread(col[:, a, 4, h:h + 1], 1, P), cum, start=True, stop=True)
                        mm = pe.matmul(k.ps[:, bank, c:c + P], spread(col[:, a, 5, h:h + 1], 1, P), ident, start=False, stop=True,
                                       skip_group_check=True)
                    mm.then_inc(g.gq, 1)
                for l in levels:
                    for a in range(2):
                        pe.wait_ge(g.mt, 12 * hg + 2 * (l - 1) + a + 1)
                        if l > 1:
                            pe.wait_ge(g.x, 12 * hg + 2 * (l - 2) + a + 1)
                        for hh in range(HG):
                            mm = pe.matmul(k.ps[:, a, hh * P:(hh + 1) * P], MT[:, a, hh, :], ident if l == 1 else X[:, a, hh, :],
                                           start=True, stop=True)
                        mm.then_inc(g.p, 1)
                    if l > 1:
                        for a in range(2):
                            pe.wait_ge(g.pc, 10 * hg + 2 * (l - 2) + a + 1)
                            for hh in range(HG):
                                cols = slice(hh * P, (hh + 1) * P)
                                if l < LEVELS:
                                    pe.matmul(k.ps[:, 2 + 2 * a, cols], XT[:, a, hh, :], Ps[:, a, hh, :], start=True, stop=True)
                                mm = pe.matmul(k.ps[:, 3 + 2 * a, cols], Ps[:, a, hh, :], XT[:, a, hh, :], start=True, stop=True)
                            mm.then_inc(g.px, 1)
                for a in range(2):
                    pe.wait_ge(g.x, 12 * hg + 2 * (LEVELS - 1) + a + 1)
                    pe.wait_ge(g.kb, U + a + 1)
                    if a == 0:
                        pe.wait_ge(g.vc, U + 2)
                        pe.wait_ge(g.kc, U + 2)
                    else:
                        pe.wait_ge(g.uc, U + 1)
                        pe.wait_ge(g.wc, U + 1)
                    for hh in range(HG):
                        mm = pe.matmul(k.ps[:, 6, hh * P:(hh + 1) * P], XT[:, a, hh, :], bv[:, a, hh, :], start=True, stop=True)
                    mm.then_inc(g.u, 1)
                    for hh in range(HG):
                        mm = pe.matmul(k.ps[:, 7, hh * P:(hh + 1) * P], kbg[:, a, hh, :], XT[:, a, hh, :], start=True, stop=True)
                    mm.then_inc(g.w, 1)
                for n in range(4):
                    a, p0 = n // 2, GC * (n % 2)
                    part = slice(p0, p0 + GC)
                    if n == 0:
                        pe.wait_ge(g.uc, U + 2)
                        pe.wait_ge(g.wc, U + 2)
                        pe.wait_ge(g.qd, U + 2)
                    else:
                        pe.wait_ge(g.s, 3 * hg + n)
                        for hh in range(HG):
                            mm = pe.matmul(k.ps[part, n % 2, hh * P:(hh + 1) * P], wT[:, a, hh, part], S[:, n % 2, hh, :],
                                           start=True, stop=True, tile_position=(0, p0))
                        mm.then_inc(g.ws, 1)
                        pe.wait_ge(g.vn, 3 * hg + n)
                    if n < 3:
                        for hh in range(HG):
                            mm = pe.matmul(k.ps[:, 4 + n % 2, hh * P:(hh + 1) * P], kdec[part, a, hh, :], u[part, a, hh, :],
                                           start=True, stop=True, tile_position=(p0, 0))
                        mm.then_inc(g.kv, 1)
                    if n >= 2:
                        pe.wait_ge(g.oc, 4 * hg + n - 1)
                    for hh in range(HG):
                        out = k.ps[:, 2 + n % 2, hh * GC:(hh + 1) * GC]
                        if n:
                            pe.matmul(out, S[:, n % 2, hh, :], qd[:, hh, n * GC:(n + 1) * GC], start=True, stop=False)
                        mm = pe.matmul(out, u[part, a, hh, :], AQ[part, a, hh, 1, part], start=(n == 0), stop=True,
                                       tile_position=(p0, 0))
                    mm.then_inc(g.o, 1)

        @block.scalar
        def _(act):
            for hg in range(NG):
                U = 2 * hg
                for a in range(2):
                    rows = slice(a * P, (a + 1) * P)
                    act.wait_ge(g.vt, U + a + 1)
                    if hg:
                        act.wait_ge(g.u, U - 1 + a)
                    for hh in range(HG):
                        h = HG * hg + hh
                        ins = act.activation(bv[:, a, hh, :], k.ps[:, 6, hh * P:(hh + 1) * P], ACT.Copy, scale=col[:, a, 0, h:h + 1])
                    ins.then_inc(g.vc, 1)
                    act.wait_ge(g.kt, U + a + 1)
                    if hg:
                        act.wait_ge(g.kb, U - 1 + a)
                    act.activation(ktok[:, a, :, :], k.ps[:, 7, 0:2 * P].rearrange("p (h n) -> p h n", h=2), ACT.Copy).then_inc(g.kc, 1)
                    act.wait_ge(g.t, U + a + 1)
                    if hg:
                        act.wait_ge(g.qd, U)
                        act.wait_ge(g.sd, 2 * hg)
                    for b in range(2):
                        rows4 = k.ps[:, 2 + 2 * a + b, :].rearrange("p (h c n) -> p h c n", h=2, c=2)
                        ins = act.activation(rx[:, 2 * b:2 * b + 2, rows], rows4[:, :, 1, :], ACT.Exp)
                    ins.then_inc(g.re, 1)
                    for hh in range(HG):
                        h = HG * hg + hh
                        ins = act.activation(E[:, a, hh, :, :], E[:, a, hh, :, :], ACT.Exp, bias=col[:, a, 1, h:h + 1])
                    ins.then_inc(g.e, 1)
                for l in levels:
                    if l > 1:
                        for a in range(2):
                            act.wait_ge(g.p, 12 * hg + 2 * (l - 1) + a + 1)
                            if l > 2 or hg:
                                act.wait_ge(g.px, 10 * hg + 2 * (l - 3) + a + 1)
                            act.activation(Ps[:, a, :, :], four(a), ACT.Copy).then_inc(g.pc, 1)
                for a in range(2):
                    act.wait_ge(g.w, U + a + 1)
                    act.activation(wT[:, a, :, :], four(7), ACT.Copy).then_inc(g.wc, 1)
                for n in range(4):
                    act.wait_ge(g.o, 4 * hg + n + 1)
                    act.activation(v[:, HG * hg:HG * (hg + 1), n * GC:(n + 1) * GC],
                                   k.ps[:, 2 + n % 2, 0:HG * GC].rearrange("p (h n) -> p h n", h=HG), ACT.Copy).then_inc(g.oc, 1)

        @block.vector
        def _(dve):
            for hg in range(NG):
                U = 2 * hg
                for a in range(2):
                    dve.wait_ge(g.gq, U + a + 1)
                    if hg:
                        dve.wait_ge(g.o, 4 * hg)
                    for b in range(2):
                        ins = dve.tensor_tensor(E[:, a, 2 * b:2 * b + 2, :, :].rearrange("p h c n -> p h (c n)"),
                                                k.ps[:, 2 + 2 * a + b, :].rearrange("p (h n) -> p h n", h=2),
                                                spread(dmask.rearrange("p (o n) -> p o n", o=1), 1, 2), ALU.add)
                    ins.then_inc(g.t, 1)
                for a in range(2):
                    dve.wait_ge(g.e, U + a + 1)
                    if hg:
                        dve.wait_ge(g.o, 4 * hg)
                    for kh in range(2):
                        ins = dve.tensor_tensor(AQ[:, a, 2 * kh:2 * kh + 2, :, :].rearrange("p h c n -> p h (c n)"),
                                                E[:, a, 2 * kh:2 * kh + 2, :, :].rearrange("p h c n -> p h (c n)"),
                                                spread(k.ps[:, a, 2 * kh * P:(2 * kh + 2) * P].rearrange("p (o n) -> p o n", o=1), 1, 2),
                                                ALU.mult)
                    ins.then_inc(g.aq, 1)
                idb = spread(ident.rearrange("p (o n) -> p o n", o=1), 1, HG)
                for l in levels:
                    for a in range(2):
                        if l == 1:
                            dve.wait_ge(g.p, 12 * hg + a + 1)
                            dve.tensor_tensor(X[:, a, :, :], idb, four(a), ALU.subtract)
                            dve.tensor_tensor(XT[:, a, :, :], idb, MT[:, a, :, :], ALU.subtract).then_inc(g.x, 1)
                        else:
                            dve.wait_ge(g.px, 10 * hg + 2 * (l - 2) + a + 1)
                            if l < LEVELS:
                                dve.tensor_tensor(X[:, a, :, :], X[:, a, :, :], four(2 + 2 * a), ALU.subtract)
                            dve.tensor_tensor(XT[:, a, :, :], XT[:, a, :, :], four(3 + 2 * a), ALU.subtract).then_inc(g.x, 1)
                for a in range(2):
                    dve.wait_ge(g.u, U + a + 1)
                    dve.tensor_copy(u[:, a, :, :], four(6)).then_inc(g.uc, 1)
                for n in range(4):
                    a, p0 = n // 2, GC * (n % 2)
                    part = slice(p0, p0 + GC)
                    if n:
                        dve.wait_ge(g.ws, 3 * hg + n)
                        dve.tensor_tensor(u[part, a, :, :], u[part, a, :, :], four(n % 2)[part, :, :], ALU.subtract).then_inc(g.vn, 1)
                    if n < 3:
                        dve.wait_ge(g.kv, 3 * hg + n + 1)
                        if n == 0:
                            if hg:
                                dve.wait_ge(g.o, 4 * hg)
                            dve.tensor_copy(S[:, 1, :, :], four(4)).then_inc(g.s, 1)
                        else:
                            dve.wait_ge(g.sd, 2 * hg + n)
                            if n == 2:
                                dve.wait_ge(g.o, 4 * hg + 2)
                            dve.tensor_tensor(S[:, (n + 1) % 2, :, :], Sd[:, :, :], four(4 + n % 2), ALU.add).then_inc(g.s, 1)

        @block.gpsimd
        def _(pool):
            for hg in range(NG):
                U = 2 * hg
                for a in range(2):
                    rows = slice(a * P, (a + 1) * P)
                    pool.wait_ge(g.aq, U + a + 1)
                    pool.tensor_tensor(MT[:, a, :, :], AQ[:, a, :, 0, :], spread(lmask[:, 0:1, :], 1, HG), ALU.mult).then_inc(g.mt, 1)
                for a in range(2):
                    rows = slice(a * P, (a + 1) * P)
                    pool.wait_ge(g.kc, U + a + 1)
                    if hg:
                        pool.wait_ge(g.o, 4 * hg)
                    for hh in range(HG):
                        h = HG * hg + hh
                        pool.tensor_scalar(kbg[:, a, hh, :], ktok[:, a, hh // 2, :], col[:, a, 2, h:h + 1], None, ALU.mult)
                        ins = pool.tensor_scalar(kdec[:, a, hh, :], ktok[:, a, hh // 2, :], col[:, a, 3, h:h + 1], None, ALU.mult)
                    ins.then_inc(g.kb, 1)
                    pool.wait_ge(g.re, U + a + 1)
                    for kh in range(2):
                        ins = pool.tensor_tensor(qd[:, 2 * kh:2 * kh + 2, rows], rx[:, 2 * kh:2 * kh + 2, rows],
                                                 spread(q_of(hg, kh)[:, rows].rearrange("p (o n) -> p o n", o=1), 1, 2), ALU.mult)
                    ins.then_inc(g.qd, 1)
                for l in levels:
                    if l == 1:
                        continue
                    for a in range(2):
                        pool.wait_ge(g.p, 12 * hg + 2 * (l - 2) + a + 1)
                        if l == 2:
                            pool.wait_ge(g.x, 12 * hg + a + 1)
                        pool.tensor_tensor(MT[:, a, :, :], AQ[:, a, :, 0, :], spread(lmask[:, l - 1:l, :], 1, HG), ALU.mult)\
                            .then_inc(g.mt, 1)
                for n in (1, 2):
                    pool.wait_ge(g.s, 3 * hg + n)
                    end = (n + 1) * GC
                    pool.tensor_tensor(Sd[:, :, :], S[:, n % 2, :, :], spread(rx[:, :, end - 1:end], 2, P), ALU.mult).then_inc(g.sd, 1)






def build(nc, ins, x_in, out, plan, n_items):
    k = Space()
    k.nc, k.ins, k.weights = nc, ins, ins["weights"]
    k.items = START + n_items
    k.used = START
    with ExitStack() as ctx:
        k.ctx = ctx

        def sb(name, shape, dt=F32):
            return ctx.enter_context(nc.sbuf_tensor(name, shape, dt))

        def sem(name):
            return ctx.enter_context(nc.semaphore(name))

        def counted(name, n=0):
            return Signal(sem(name), n)

        k.sem = sem
        k.ps = ctx.enter_context(nc.psum_tensor("ps", [P, 8, 512], F32))
        k.raw = sb("raw", [P, RAW, ITEM * P])
        k.hi = sb("hi", [P, CUT, ITEM * P], F32R)
        k.lo = sb("lo", [P, CUT, ITEM * P], F32R)
        k.x = sb("x", [P, KT, T])
        k.h = sb("h", [P, KT, T])
        k.hp = sb("h_high", [P, KT, T], F32R), sb("h_low", [P, KT, T], F32R)
        k.vec = sb("vec", [P, NVEC])
        k.consts = sb("consts", [P, ins["consts"].shape[1]])
        k.ones = sb("ones", [P, P])
        k.eps = sb("eps", [P, 1])
        k.zeros = sb("zeros", [P, 512], mybir.dt.bfloat16)
        k.item_here = [sem(f"item_here_{s}") for s in range(RAW)]
        k.item_rounded = sem("item_rounded")
        k.item_cut = sem("item_cut")
        k.item_used = sem("item_used")
        k.input_here = sem("input_here")
        k.setup_done = sem("setup_done")
        k.stored = sem("stored")
        k.sq_done = counted("squares_done")
        k.sum_done = counted("square_sum_done")
        k.root_done = counted("root_done")
        k.norm_done = counted("norm_done")
        k.act_done = counted("scalar_part_done")
        k.norm_out = counted("norm_tile")
        k.cut_round = counted("high_part")
        k.cut_low = counted("low_part")
        k.dft2_low = counted("token_dft_low_part")
        k.silu_done = counted("silu_done")
        k.mul_done = counted("product_done")
        k.side_here = counted("side_inputs_here")
        k.dft1_done = counted("feature_dft_done")
        k.dft1_out = counted("feature_dft_copied")
        k.dft2_done = counted("token_dft_done")
        k.dft2_out = counted("token_dft_copied")
        k.s5v = counted("s5_vector_steps")
        k.s5a = counted("s5_scalar_steps")
        k.s5_bu = counted("s5_drive_in_psum")
        k.s5_y = counted("s5_output_terms")
        k.s5_ang = counted("s5_fraction_of_turn")
        k.s5_phase = counted("s5_angle_in_turns")
        k.s5_tab = counted("s5_cos_sin_done")
        k.s5_abs = counted("s5_fraction_abs")
        k.s5_free = counted("s5_drive_read")
        k.s5_bm = counted("s5_drive_turned")
        k.s5_scan = counted("s5_scans_done")
        k.s5_prod = counted("s5_products_done")
        k.s5_out = counted("s5_output_tile")
        k.at_sc = counted("attention_scores")
        k.at_max = counted("attention_scores_masked")
        k.at_neg = counted("attention_row_maximum")
        k.at_exp = counted("attention_probabilities")
        k.at_rd = counted("attention_inverse_sum")
        k.at_diag = counted("attention_inverse_sum_diagonal")
        k.at_tr = counted("attention_probabilities_transposed")
        k.at_cp = counted("attention_transposed_copied")
        k.at_pv = counted("attention_values_mixed")
        k.at_o = counted("attention_heads_out")
        k.at_fill = counted("attention_bias_filled")
        k.at_bias = [counted("attention_bias_0"), counted("attention_bias_1")]
        k.bias_ps = counted("bias_in_psum")
        k.bias_tab = counted("bias_table")
        k.bias_written = counted("bias_written")
        k.rg_xc = counted("rg_convolved")
        k.rg_gate = counted("rg_gates_in_psum")
        k.rg_sig = counted("rg_sigmoids")
        k.rg_at = counted("rg_decay")
        k.rg_q = counted("rg_quotient")
        k.rg_root = counted("rg_root")
        k.rg_fin = counted("rg_tile_done")
        k.rope_sw = counted("rope_halves_swapped")
        k.rope_out = counted("rope_products")
        k.gg_ba = counted("gdn_b_a_in_psum")
        k.gg_g = counted("gdn_g_done")
        k.gg_gc = counted("gdn_cumulated")
        k.cv_silu = counted("conv_silu_done")
        k.hn_inv = counted("head_norm_inverse")
        k.eps128 = sb("eps128", [P, 1])
        k.eps192 = sb("eps192", [P, 1])
        k.one_c = sb("one_c", [P, 1])
        k.eps64 = sb("eps64", [P, 1])
        k.half_pi = sb("half_pi", [P, 1])
        k.round_c = sb("round_c", [P, 1])
        k.out_done = counted("output_done", 8)
        k.hidden_done = counted("hidden_done", 8)

        with nc.Block() as block:
            @block.sync
            def _(sp):
                sp.dma_start(k.x[:, :, :], x_in).then_inc(k.input_here, 16)
                sp.dma_start(k.vec[:, :], ins["vec"]).then_inc(k.input_here, 16)
                sp.dma_start(k.consts[:, :], ins["consts"]).then_inc(k.input_here, 16)
                for s in range(RAW):
                    sp.dma_start(k.raw[:, s, :], k.weights[s, :, :]).then_inc(k.item_here[s], 16)
                loads(k, sp, START - CUT, CUT)
                sp.wait_ge(k.input_here, 48)

            @block.vector
            def _(dve):
                dve.memset(k.ones[:, :], 1.0)
                dve.memset(k.zeros[:, :], 0.0)
                dve.memset(k.eps[:, :], EPS)
                dve.memset(k.eps128[:, :], P * EPS)
                dve.memset(k.eps192[:, :], MLA_SCALE * EPS)
                dve.memset(k.one_c[:, :], 1.0)
                dve.memset(k.eps64[:, :], 64 * EPS)
                dve.memset(k.half_pi[:, :], math.pi / 2)
                dve.memset(k.round_c[:, :], ROUND)
                dve.sem_inc(k.out_done.s, 8)
                dve.sem_inc(k.hidden_done.s, 8)
                dve.sem_inc(k.item_used, START)
                dve.sem_inc(k.item_rounded, START)
                dve.sem_inc(k.item_cut, START)
                for s in range(CUT):
                    cut_item(k, dve, START - CUT + s)

            @block.scalar
            def _(act):
                for s in range(CUT):
                    round_item(k, act, START - CUT + s)
        plan(k)
        assert k.used == k.items, (k.used, k.items)
        with nc.Block() as block:
            @block.sync
            def _(sp):
                sp.dma_start(out, k.x[:, :, :]).then_inc(k.stored, 16)
                sp.wait_ge(k.stored, 16)


def residual(k):
    def out(dve, n, ps):
        return dve.tensor_tensor(tile_of(k.x, n), tile_of(k.x, n), ps, ALU.add)
    return out


def ffn_first(k, layer):
    norm(k, k.x, KT, VEC_AT["norm_ffn_g"] + KT * layer, k.h, D, pair=k.hp)
    swiglu(k, k.hp, residual(k))


def tiles(w):
    kk, n = w.shape
    return w.reshape(kk // P, P, n // P, P).transpose(0, 2, 1, 3)


def as_items(t):
    return t.reshape(-1, ITEM, P, P).transpose(0, 2, 1, 3).reshape(-1, P, ITEM * P)


def by_output(w):
    t = tiles(w).transpose(1, 0, 2, 3)
    return as_items(t.reshape(-1, P, P))


def by_input(w):
    return as_items(tiles(w).reshape(-1, P, P))


def ffn_items(gate, up, down):
    g, u, d = by_output(gate), by_output(up), by_input(down)
    out = [g[0], u[0]]
    for j in range(FT):
        if j + 1 < FT:
            out += [g[j + 1], u[j + 1]]
        out.append(d[j])
    return np.stack(out)


def vectors(inp):
    cols = []
    for name, n in VECTORS:
        a = np.asarray(inp[name])
        if name in ("attn_q_gain", "attn_k_gain"):
            a = np.concatenate([a.reshape(3, 64), a.reshape(3, 64)], axis=1)
        cols.append(a.reshape(n, P))
    return np.ascontiguousarray(np.concatenate(cols).T)


def qkv_items(w):
    w = w.reshape(D, GROUPS, 3, D)
    parts = [by_output(w[:, g, 0]) for g in range(GROUPS)]
    for g in range(GROUPS):
        parts += [by_output(w[:, g, 1]), by_input(w[:, g, 2])]
    return np.concatenate(parts)


def t5_bucket(rel):
    half, max_exact = 16, 8
    n = np.abs(rel)
    sign = (rel > 0).astype(np.int32) * half
    large = max_exact + (np.log(np.maximum(n, 1) / max_exact) / math.log(1024 / max_exact)
                         * (half - max_exact)).astype(np.int32)
    large = np.minimum(large, half - 1)
    return (sign + np.where(n < max_exact, n, large)).astype(np.int32)


def bias_tables():
    onehot = np.zeros((32, GROUPS, 512), np.float32)
    mask = np.full((AH, GROUPS, 512), NEG, np.float32)
    rel = np.arange(-255, 256)
    onehot[t5_bucket(rel), 0, np.arange(511)] = 1
    mask[:, 0, :511][:, np.abs(rel) <= 64] = 0
    step = np.arange(-63, 64)
    for g, stride in ((1, 1), (2, 4)):
        onehot[t5_bucket(4 * step), g, np.arange(127)] = 1
        mask[:, g, :127][:, step % stride == 0] = 0
    return onehot, mask


def hybrid_items(inp):
    w_in = inp["hy_w_in_2"][0]
    w_in = np.concatenate([w_in, w_in[:, -64:]], 1)
    gates = np.stack([inp["rg_gate_a_w_2"][0], inp["rg_gate_x_w_2"][0]], 1).reshape(-1, P, P)
    uq = inp["mla_w_uq_2"][0].reshape(QL * P, MH, 192)
    uq = np.concatenate([uq[:, :, :P].reshape(QL * P, -1), uq[:, :, P:].reshape(QL * P, -1)], 1)
    ukv = inp["mla_w_ukv_2"][0].reshape(KVL * P, MH, 2, P)
    return np.concatenate([by_output(w_in), as_items(gates), by_output(uq),
                           by_output(np.ascontiguousarray(ukv[:, :, 0]).reshape(KVL * P, D)),
                           by_input(np.ascontiguousarray(ukv[:, :, 1]).reshape(KVL * P, D)),
                           by_output(inp["hy_w_out_2"][0])])


def gdn_items(inp):
    w = inp["gdn_w_in_2"][0]
    return np.concatenate([by_output(w[:, :6 * D]), by_output(inp["gdn_w_out_2"][0])])


def gdn_ba(inp):
    return np.ascontiguousarray(inp["gdn_w_in_2"][0][:, 6 * D:].reshape(KT, P, 2 * GH).transpose(1, 0, 2).reshape(P, -1))


def s5_lam(inp):
    def lay(a):
        return a.reshape(2, SG // 2, 2, SN).transpose(2, 3, 0, 1).reshape(P, ST)
    dt = np.repeat(np.asarray(inp["s5_log_dt"])[0][:, :, None], SN, 2)
    return np.ascontiguousarray(np.stack([lay(inp["s5_lambda_re"][0]), lay(inp["s5_lambda_im"][0]), lay(dt)], 1))


def s5_b(inp):
    def lay(a):
        return a[0].reshape(2, KT, KT, SN, SP_).transpose(2, 4, 0, 1, 3).reshape(P, 2 * KT * SN)
    return np.ascontiguousarray(np.concatenate([lay(inp["s5_b_re"]), lay(inp["s5_b_im"])], 1))


def s5_c(inp):
    def lay(a):
        return a[0].reshape(2, SG // 2, 2, SP_, SN).transpose(2, 4, 0, 1, 3).reshape(P, ST * SP_)
    return np.ascontiguousarray(np.concatenate([lay(inp["s5_c_re"]), lay(inp["s5_c_im"])], 1))


def glu_items(w):
    v, g = by_output(w[:, :D]), by_output(w[:, D:])
    return np.stack([g, v], 1).reshape(-1, P, ITEM * P)


def constants():
    i = np.arange(P)
    parts = {}
    parts["ident"] = np.eye(P)
    ang = 2 * np.pi * np.outer(i, i) / P
    parts["dft_feature"] = np.concatenate([np.cos(ang), np.sin(ang)], 1) / math.sqrt(T * P)
    s = np.arange(T)
    angt = 2 * np.pi * (np.outer(s, s) % T) / T
    parts["dft_cos"] = np.cos(angt).reshape(2, P, T).transpose(1, 0, 2).reshape(P, 2 * T)
    parts["dft_nsin"] = -np.sin(angt).reshape(2, P, T).transpose(1, 0, 2).reshape(P, 2 * T)
    parts["time"] = np.broadcast_to(s, (P, T))
    parts["two_heads"] = i[:, None] // 64 == i[None, :] // 64
    parts["rope_swap"] = np.where(i[:, None] == (i[None, :] ^ 32), np.where(i[None, :] % 64 < 32, -1.0, 1.0), 0.0)
    inv = 1.0 / (np.float32(10000.0) ** (np.arange(0, 64, 2, dtype=np.float32) / np.float32(64)))
    parts["inv_freq"] = np.tile(inv.astype(np.float32), 4)[:, None]
    parts["causal"] = np.concatenate([np.zeros((P, P)), np.where(i[None, :] <= i[:, None], 0.0, NEG)], 1)
    chunk = i[:, None] // GC == i[None, :] // GC
    later = i[None, :] >= i[:, None]
    parts["cumulate"] = np.tile(chunk & later, (1, 2))
    parts["chunk_sum"] = chunk
    parts["decay_mask"] = np.where(np.concatenate([chunk & (i[None, :] > i[:, None]), chunk & later], 1), 0.0, NEG)
    parts["levels"] = np.concatenate([(i[:, None] >> l == i[None, :] >> l) & (i[:, None] >> (l - 1) != i[None, :] >> (l - 1))
                                      for l in range(1, LEVELS + 1)], 1)
    parts["b_half"] = np.stack([(i // SP_) % 2 == 0, (i // SP_) % 2 == 1], 1)
    parts["c_half"] = np.stack([i < SN, i >= SN], 1)
    return parts


CONST_AT = {}
_at = 0
for _name, _a in constants().items():
    CONST_AT[_name] = (_at, _at + _a.shape[1])
    _at += _a.shape[1]


def const(k, name):
    a, b = CONST_AT[name]
    return k.consts[:, a:b]


def whole_program(k):
    for layer in range(4):
        if layer in (0, 3):
            norm(k, k.x, KT, VEC_AT["norm_mix_g"] + KT * layer, k.h, D)
            fourier(k)
        elif layer == 1:
            norm(k, k.x, KT, VEC_AT["norm_mix_g"] + KT * layer, k.h, D)
            s5(k)
        else:
            norm(k, k.x, KT, VEC_AT["norm_mix_g"] + KT * layer, k.h, D, pair=k.hp)
            attention(k)
        ffn_first(k, layer)
    hybrid(k)
    ffn_second(k, 0)
    gdn(k)
    ffn_second(k, 1)


def all_items(inp):
    def first(layer):
        gu = inp["ffn_w_gate_up"][layer]
        return ffn_items(gu[:, :FF], gu[:, FF:], inp["ffn_w_down"][layer])

    def second(layer):
        return ffn_items(inp["ffn_w_gate_2"][layer], inp["ffn_w_up_2"][layer], inp["ffn_w_down_2"][layer])
    return np.concatenate([
        by_output(inp["fnet_w_out"][0]), first(0),
        glu_items(inp["s5_w_glu"][0]), first(1),
        qkv_items(inp["attn_w_qkv"][0]), by_output(inp["attn_w_o"][0]), first(2),
        by_output(inp["fnet_w_out"][1]), first(3),
        hybrid_items(inp), second(0),
        gdn_items(inp), second(1),
    ])


def kernel(**inputs):
    import concourse.bacc as bacc
    from concourse.bass_utils import run_bass_kernel_spmd

    inp = {name: np.asarray(a) for name, a in inputs.items()}
    onehot, mask = bias_tables()
    arrays = {
        "in_x": np.ascontiguousarray(inp["x"].reshape(T, KT, P).transpose(2, 1, 0)),
        "in_weights": all_items(inp),
        "in_vec": vectors(inp),
        "in_consts": np.concatenate(list(constants().values()), 1).astype(np.float32),
        "in_s5_lam": s5_lam(inp), "in_s5_b": s5_b(inp), "in_s5_c": s5_c(inp),
        "in_bias_onehot": onehot, "in_bias_mask": mask, "in_rel_bias": np.ascontiguousarray(inp["rel_bias"]),
        "in_positions": np.ascontiguousarray(inp["positions_2"]),
        "in_gdn_ba": gdn_ba(inp),
        "in_gdn_a_log": np.ascontiguousarray(inp["gdn_a_log_2"]),
        "in_gdn_dt_bias": np.ascontiguousarray(inp["gdn_dt_bias_2"]),
    }
    nc = bacc.Bacc("TRN2", target_bir_lowering=False, num_devices=1)
    ins = {name[3:]: nc.dram_tensor(name, a.shape, mybir.dt.from_np(a.dtype), kind="ExternalInput").ap()
           for name, a in arrays.items()}
    out = nc.dram_tensor("out", (P, KT, T), F32, kind="ExternalOutput").ap()
    build(nc, ins, ins["x"], out, whole_program, arrays["in_weights"].shape[0])
    r = run_bass_kernel_spmd(nc, [arrays], core_ids=[0])
    return np.ascontiguousarray(r.results[0]["out"].transpose(2, 1, 0)).reshape(1, T, D)
```

```python
import math
from contextlib import ExitStack

import numpy as np
import concourse.bass as bass
from concourse import mybir

F32 = mybir.dt.float32
F32R = mybir.dt.float32r
I32 = mybir.dt.int32
ALU = mybir.AluOpType
ACT = mybir.ActivationFunctionType
AX = mybir.AxisListType

P = 128
T = 256
D = 1024
KT = D // P
FF = 2816
FT = FF // P
RAW = 6
CUT = 4
ROUND_ITEMS = 12
START = 12
ITEM = 8
EPS = 1e-6
ROUND = 1.5 * 2.0 ** 23
TWO_PI = 6.283185

VECTORS = [
    ("norm_mix_g", 32), ("norm_ffn_g", 32), ("s5_d", 8),
    ("norm_mix_pre_2", 16), ("norm_mix_post_2", 16), ("norm_ffn_pre_2", 16), ("norm_ffn_post_2", 16),
    ("mla_q_norm_2", 4), ("mla_kv_norm_2", 2), ("rg_conv_w_2", 32), ("rg_conv_b_2", 8),
    ("rg_gate_a_b_2", 8), ("rg_gate_x_b_2", 8), ("rg_lambda_2", 8), ("gdn_conv_w_2", 128),
    ("gdn_norm_2", 1), ("attn_q_gain", 3), ("attn_k_gain", 3),
]
VEC_AT = {}
_at = 0
for _name, _n in VECTORS:
    VEC_AT[_name] = _at
    _at += _n
NVEC = _at


class Space:
    pass


class Signal:

    def __init__(self, s, n):
        self.s, self.n = s, n


def tile_of(t3, n):
    if isinstance(n, int):
        return t3[:, n, :]
    return t3[:, bass.ds(n, 1), :].rearrange("p a n -> p (a n)")


def loads(k, sp, first, count):
    first = first + CUT + RAW
    count = max(min(count, k.items - first), 0)
    rounds = count // ROUND_ITEMS if count >= 2 * ROUND_ITEMS else 0
    if rounds:
        with sp.Fori(0, rounds) as i:
            for s in range(ROUND_ITEMS):
                at = sp.snap(i * ROUND_ITEMS + (first - START + s))
                sp.wait_ge(k.item_cut, i * ROUND_ITEMS + (first + s - RAW + 1))
                sp.dma_start(k.raw[:, (first + s) % RAW, :], k.weights[bass.ds(at, 1), :, :].rearrange("a p n -> p (a n)"))\
                  .then_inc(k.item_here[(first + s) % RAW], 16)
    for s in range(rounds * ROUND_ITEMS, count):
        sp.wait_ge(k.item_cut, first + s - RAW + 1)
        sp.dma_start(k.raw[:, (first + s) % RAW, :], k.weights[first - START + s, :, :])\
          .then_inc(k.item_here[(first + s) % RAW], 16)


def round_item(k, act, used, i=0):
    item = used + CUT
    if isinstance(i, int) and item >= k.items:
        return
    act.wait_ge(k.item_here[item % RAW], i * (16 * ROUND_ITEMS // RAW) + 16 * ((item - START) // RAW + 1))
    act.wait_ge(k.item_used, i * ROUND_ITEMS + (used + 1))
    act.activation(k.hi[:, item % CUT, :], k.raw[:, item % RAW, :], ACT.Copy).then_inc(k.item_rounded, 1)


def cut_item(k, engine, used, i=0):
    item = used + CUT
    if isinstance(i, int) and item >= k.items:
        return
    engine.wait_ge(k.item_rounded, i * ROUND_ITEMS + (item + 1))
    engine.tensor_tensor(k.lo[:, item % CUT, :], k.raw[:, item % RAW, :], k.hi[:, item % CUT, :].bitcast(F32), ALU.subtract)\
          .then_inc(k.item_cut, 1)


class Weights:

    def __init__(self, k, pe, first, i=0):
        self.k, self.pe, self.first, self.i = k, pe, first, i

    def tile(self, t, cols=P):
        item = self.first + t // ITEM
        if t % ITEM == 0:
            self.pe.wait_ge(self.k.item_cut, self.i * ROUND_ITEMS + (item + 1))
        at = slice(t % ITEM * P, t % ITEM * P + cols)
        return self.k.hi[:, item % CUT, at], self.k.lo[:, item % CUT, at]


def product(pe, out, w, x, start, stop, **more):
    (wh, wl), (xh, xl) = w, x
    pe.matmul(out, wh, xh, start=start, stop=False, **more)
    pe.matmul(out, wh, xl, start=False, stop=False, **more)
    return pe.matmul(out, wl, xh, start=False, stop=stop, **more)


def pair_tile(pair, j, cols=slice(None)):
    return pair[0][:, j, cols], pair[1][:, j, cols]


class Parts:

    def __init__(self, k, src, pair, kt, gain_col=None, dst=None, slot=0, gelu=False):
        self.gelu = gelu
        self.k, self.src, self.pair, self.kt = k, src, pair, kt
        self.gain_col, self.dst, self.slot = gain_col, dst, slot
        self.b_n, self.b_r, self.b_even, self.b_odd = k.norm_out.n, k.cut_round.n, k.low_even.n, k.low_odd.n
        if dst is not None:
            k.norm_out.n += kt
        k.cut_round.n += kt
        k.low_even.n += -(-kt // 2)
        k.low_odd.n += kt // 2

    def full(self):
        return self.src if self.dst is None else self.dst

    def scalar(self, act):
        for j in range(self.kt):
            if self.dst is not None:
                act.wait_ge(self.k.norm_out.s, self.b_n + j + 1)
            if self.gelu:
                act.activation(self.pair[0][:, j, :], self.src[:, j, :], ACT.Gelu_apprx_tanh)
                act.activation(self.src[:, j, :], self.src[:, j, :], ACT.Gelu_apprx_tanh).then_inc(self.k.cut_round.s, 1)
            else:
                act.activation(self.pair[0][:, j, :], self.full()[:, j, :], ACT.Copy).then_inc(self.k.cut_round.s, 1)

    def vector(self, dve):
        k = self.k
        for j in range(self.kt + 2):
            if j < self.kt and self.dst is not None:
                dve.scalar_tensor_tensor(self.dst[:, j, :], self.src[:, j, :], k.vec[:, self.gain_col + j:self.gain_col + j + 1],
                                         k.rs[:, self.slot, :], ALU.mult, ALU.mult).then_inc(k.norm_out.s, 1)
            if j >= 2 and j % 2 == 0:
                self.low(dve, j - 2, k.low_even)

    def gpsimd(self, pool):
        for j in range(1, self.kt, 2):
            self.low(pool, j, self.k.low_odd)

    def low(self, engine, j, signal):
        engine.wait_ge(self.k.cut_round.s, self.b_r + j + 1)
        engine.tensor_tensor(self.pair[1][:, j, :], self.full()[:, j, :], self.pair[0][:, j, :].bitcast(F32), ALU.subtract)\
              .then_inc(signal.s, 1)

    def here(self, pe, j):
        if j % 2 == 0:
            pe.wait_ge(self.k.low_even.s, self.b_even + j // 2 + 1)
        else:
            pe.wait_ge(self.k.low_odd.s, self.b_odd + j // 2 + 1)


def norm(k, src, kt, gain_col, dst, width, times=1.0, pair=None, slot=0, add_to=None, side=None):
    nc = k.nc
    tag = f"{k.norm_done.n}"
    eps = k.eps if times == 1.0 else k.eps192
    with nc.sbuf_tensor("norm_sq" + tag, [P, kt, T], F32) as sq, nc.Block() as block:
        b_sq, b_sum, b_root, b_inv, b_n = k.sq_done.n, k.sum_done.n, k.root_done.n, k.norm_done.n, k.norm_out.n
        if side:
            block.sync(side)

        @block.scalar
        def _(act):
            for j in range(kt):
                act.activation(sq[:, j, :], src[:, j, :], ACT.Square).then_inc(k.sq_done.s, 1)
            act.wait_ge(k.sum_done.s, b_sum + 1)
            act.activation(k.root[:, :], k.ps[:, 0, 0:T], ACT.Sqrt, scale=times / width,
                           bias=eps[:, 0:1]).then_inc(k.root_done.s, 1)

        @block.tensor
        def _(pe):
            for j in range(kt):
                pe.wait_ge(k.sq_done.s, b_sq + j + 1)
                mm = pe.matmul(k.ps[:, 0, 0:T], k.ones[:, :], sq[:, j, :], start=(j == 0), stop=(j == kt - 1))
            mm.then_inc(k.sum_done.s, 1)

        @block.vector
        def _(dve):
            dve.wait_ge(k.root_done.s, b_root + 1)
            dve.reciprocal(k.rs[:, slot, :], k.root[:, :]).then_inc(k.norm_done.s, 1)
            if not pair:
                dve.wait_ge(k.norm_done.s, b_inv + 1)
                for j in range(kt):
                    dve.scalar_tensor_tensor(dst[:, j, :], src[:, j, :], k.vec[:, gain_col + j:gain_col + j + 1],
                                             k.rs[:, slot, :], ALU.mult, ALU.mult).then_inc(k.norm_out.s, 1)
                    if add_to is not None and j % 2:
                        dve.wait_ge(k.norm_out.s, b_n + j)
                        dve.tensor_tensor(add_to[:, j - 1, :], add_to[:, j - 1, :], dst[:, j - 1, :], ALU.add)

        if add_to is not None:
            @block.gpsimd
            def _(pool):
                for j in range(1, kt, 2):
                    pool.wait_ge(k.norm_out.s, b_n + j + 1)
                    pool.tensor_tensor(add_to[:, j, :], add_to[:, j, :], dst[:, j, :], ALU.add)
        k.sq_done.n += kt
        k.sum_done.n += 1
        k.root_done.n += 1
        k.norm_done.n += 1
        if not pair:
            k.norm_out.n += kt
    if pair:
        return Parts(k, src, pair, kt, gain_col, dst, slot)


def make_parts(k, parts):
    with k.nc.Block() as block:
        block.scalar(parts.scalar)
        block.vector(parts.vector)
        block.gpsimd(parts.gpsimd)


def linear(k, src, kt, nt, dve_out=None, act_out=None, parts=(), beside=None):
    first = k.used
    items = nt * kt // ITEM
    banks = 2 if kt > ITEM else 4
    per = ITEM * ROUND_ITEMS // kt
    rounds = nt // per if nt >= 2 * per else 0
    b_out = k.out_done.n

    def walk(engine, step):
        if rounds:
            with engine.Fori(0, rounds) as i:
                for b in range(per):
                    step(i, b)
        for n in range(rounds * per, nt):
            step(0, n)

    def computed(i, b):
        return i * ROUND_ITEMS + (first + -(-(b + 1) * kt // ITEM))

    def items_of(b):
        return range(b * kt // ITEM, (b + 1) * kt // ITEM)

    with k.nc.Block() as block:
        @block.sync
        def _(sp):
            loads(k, sp, first, items)

        @block.tensor
        def _(pe):
            if parts and rounds:
                for j in (kt - 2, kt - 1):
                    parts[-1].here(pe, j)

            def step(i, b):
                w = Weights(k, pe, first, i)
                pe.wait_ge(k.out_done.s, i * per + (b + b_out - banks + 1))
                for j in range(kt):
                    if parts and not rounds and b == 0:
                        parts[-1].here(pe, j)
                    mm = product(pe, k.ps[:, b % banks, 0:T], w.tile(b * kt + j), pair_tile(src, j),
                                 start=(j == 0), stop=(j == kt - 1))
                    if (b * kt + j) % ITEM == ITEM - 1:
                        mm.then_inc(k.item_used, 1)
                if beside:
                    beside("tensor", pe, b)
            walk(pe, step)

        @block.scalar
        def _(act):
            for p in parts:
                p.scalar(act)

            def step(i, b):
                if act_out:
                    act.wait_ge(k.item_used, computed(i, b))
                    act_out(act, i * per + b, k.ps[:, b % banks, 0:T]).then_inc(k.out_done.s, 1)
                for item in items_of(b):
                    round_item(k, act, first + item, i)
                if beside:
                    beside("scalar", act, b)
            walk(act, step)

        @block.vector
        def _(dve):
            for p in parts:
                p.vector(dve)

            def step(i, b):
                if dve_out:
                    dve.wait_ge(k.item_used, computed(i, b))
                    dve_out(dve, i * per + b, k.ps[:, b % banks, 0:T]).then_inc(k.out_done.s, 1)
                for item in items_of(b):
                    cut_item(k, dve, first + item, i)
                if beside:
                    beside("vector", dve, b)
            walk(dve, step)

        if parts or beside:
            @block.gpsimd
            def _(pool):
                for p in parts:
                    p.gpsimd(pool)
                if beside:
                    for b in range(nt):
                        beside("gpsimd", pool, b)
    k.used += items
    k.out_done.n += nt


def swiglu(k, src, out, parts):
    first = k.used
    items = 3 * FT
    per = ROUND_ITEMS // 3
    rounds = (FT - 2) // per
    b_silu, b_hid, b_prod = k.silu_done.n, k.hidden_done.n, k.mul_done.n

    def walk(engine, step):
        with engine.Fori(0, rounds) as i:
            for b in range(per):
                step(i, b)
        for j in range(rounds * per, FT):
            step(0, j)

    with k.nc.sbuf_tensor(f"silu{first}", [P, 2, T], F32) as silu, k.nc.sbuf_tensor(f"hidden{first}", [P, 2, T], F32) as hidden, \
            k.nc.sbuf_tensor(f"hidden_h{first}", [P, 2, T], F32R) as hid_h, \
            k.nc.sbuf_tensor(f"hidden_l{first}", [P, 2, T], F32R) as hid_l, \
            k.nc.Block() as block:
        @block.sync
        def _(sp):
            loads(k, sp, first, items)

        @block.tensor
        def _(pe):
            def gate_up(i, b):
                w = Weights(k, pe, first, i)
                at = 0 if (isinstance(i, int) and b == 0) else 2 + 3 * (b - 1)
                for half in range(2):
                    for j in range(KT):
                        if isinstance(i, int) and b == 0 and half == 0:
                            parts.here(pe, j)
                        mm = product(pe, k.ps[:, 4 + b % 2, half * T:(half + 1) * T], w.tile((at + half) * ITEM + j),
                                     pair_tile(src, j), start=(j == 0), stop=(j == KT - 1))
                    mm.then_inc(k.item_used, 1)

            def down(i, b):
                w = Weights(k, pe, first, i)
                at = 4 + 3 * b if not (isinstance(i, int) and b == FT - 1) else items - 1
                pe.wait_ge(k.hidden_done.s, i * per + (b + b_hid + 1))
                for n in range(KT):
                    mm = product(pe, k.ps[:, n // 2, n % 2 * T:(n % 2 + 1) * T], w.tile(at * ITEM + n),
                                 pair_tile((hid_h, hid_l), b % 2), start=False, stop=False, skip_group_check=True)
                mm.then_inc(k.item_used, 1)

            for n in range(KT // 2):
                pe.matmul(k.ps[:, n, :], k.zeros[:, 0:P], k.zeros[:, :], start=True, stop=False, skip_group_check=True)
            gate_up(0, 0)

            def step(i, b):
                if not (isinstance(i, int) and b == FT - 1):
                    gate_up(i, b + 1)
                down(i, b)
            walk(pe, step)

        def beside(engine, part, i, b):
            for item in range(3 * b, 3 * b + 3):
                part(k, engine, first + item, i)

        block.gpsimd(parts.gpsimd)

        @block.scalar
        def _(act):
            parts.scalar(act)

            def step(i, b):
                act.wait_ge(k.item_used, i * ROUND_ITEMS + (first + 3 * b + (2 if b == 0 else 1)))
                act.wait_ge(k.hidden_done.s, i * per + (b + b_hid - 1))
                act.activation(silu[:, b % 2, :], k.ps[:, 4 + b % 2, 0:T], ACT.Silu).then_inc(k.silu_done.s, 1)
                beside(act, round_item, i, b)
            walk(act, step)

        @block.vector
        def _(dve):
            parts.vector(dve)

            def step(i, b):
                dve.wait_ge(k.silu_done.s, i * per + (b + b_silu + 1))
                dve.wait_ge(k.item_used, i * ROUND_ITEMS + (first + 3 * b - 1))
                dve.tensor_tensor(hid_h[:, b % 2, :], silu[:, b % 2, :], k.ps[:, 4 + b % 2, T:2 * T], ALU.mult)
                dve.tensor_tensor(hidden[:, b % 2, :], silu[:, b % 2, :], k.ps[:, 4 + b % 2, T:2 * T], ALU.mult)\
                   .then_inc(k.mul_done.s, 1)
                dve.wait_ge(k.mul_done.s, i * per + (b + b_prod + 1))
                dve.tensor_tensor(hid_l[:, b % 2, :], hidden[:, b % 2, :], hid_h[:, b % 2, :].bitcast(F32), ALU.subtract)\
                   .then_inc(k.hidden_done.s, 1)
                beside(dve, cut_item, i, b)
            walk(dve, step)
            dve.wait_ge(k.item_used, first + items)
            for n in range(KT):
                out(dve, n, k.ps[:, n // 2, n % 2 * T:(n % 2 + 1) * T])
    k.used += items
    k.silu_done.n += FT
    k.mul_done.n += FT
    k.hidden_done.n += FT



def prime(k, block):
    @block.sync
    def _(sp):
        loads(k, sp, START - CUT, CUT)

    @block.gpsimd
    def _(pool):
        for s in range(CUT):
            cut_item(k, pool, START - CUT + s)


def fourier(k, first=False):
    nc = k.nc
    with nc.sbuf_tensor(f"dft_hf{k.used}", [P, 2, 2, 2 * P], F32) as hf, \
            nc.sbuf_tensor(f"dft_h{k.used}", [P, KT, T], F32R) as f_h, nc.sbuf_tensor(f"dft_l{k.used}", [P, KT, T], F32R) as f_l:
        dft = const(k, "dft_feature")
        cs = const(k, "dft_cos").rearrange("p (a n) -> p a n", a=2)
        ns = const(k, "dft_nsin").rearrange("p (a n) -> p a n", a=2)
        b_f, b_c, b_s, b_o, b_l = k.dft1_done.n, k.dft1_out.n, k.dft2_done.n, k.dft2_out.n, k.dft2_low.n
        with nc.Block() as block:
            if first:
                prime(k, block)

            @block.tensor
            def _(pe):
                def over_features(g):
                    if g >= 2:
                        pe.wait_ge(k.dft1_out.s, b_c + g - 1)
                    for a in range(2):
                        mm = pe.matmul(k.ps[:, g % 2, a * T:(a + 1) * T], k.h[:, g, a * P:(a + 1) * P], dft,
                                       start=True, stop=True)
                    mm.then_inc(k.dft1_done.s, 1)

                over_features(0)
                for g in range(KT):
                    if g + 1 < KT:
                        over_features(g + 1)
                    pe.wait_ge(k.dft1_out.s, b_c + g + 1)
                    if g >= 2:
                        pe.wait_ge(k.dft2_low.s, b_l + g - 1)
                    for a in range(2):
                        pe.matmul(k.ps[:, 2 + g % 2, 0:T], hf[:, g % 2, a, 0:P], cs[:, a, :], start=(a == 0), stop=False)
                        mm = pe.matmul(k.ps[:, 2 + g % 2, 0:T], hf[:, g % 2, a, P:2 * P], ns[:, a, :], start=False,
                                       stop=(a == 1))
                    mm.then_inc(k.dft2_done.s, 1)

            def low(dve, g):
                dve.wait_ge(k.dft2_out.s, b_o + g + 1)
                dve.tensor_tensor(f_l[:, g, :], k.ps[:, 2 + g % 2, 0:T], f_h[:, g, :].bitcast(F32), ALU.subtract)\
                   .then_inc(k.dft2_low.s, 1)

            @block.vector
            def _(dve):
                for g in range(KT):
                    dve.wait_ge(k.dft1_done.s, b_f + g + 1)
                    if g >= 2:
                        dve.wait_ge(k.dft2_done.s, b_s + g - 1)
                    dve.tensor_copy(hf[:, g % 2, :, :], k.ps[:, g % 2, :].rearrange("p (a n) -> p a n", a=2))\
                       .then_inc(k.dft1_out.s, 1)
                    if g:
                        low(dve, g - 1)
                low(dve, KT - 1)

            @block.scalar
            def _(act):
                for g in range(KT):
                    act.wait_ge(k.dft2_done.s, b_s + g + 1)
                    act.activation(f_h[:, g, :], k.ps[:, 2 + g % 2, 0:T], ACT.Copy).then_inc(k.dft2_out.s, 1)
                    if first and g < CUT:
                        round_item(k, act, START - CUT + g)
        for s in (k.dft1_done, k.dft1_out, k.dft2_done, k.dft2_out, k.dft2_low):
            s.n += KT
        linear(k, (f_h, f_l), KT, KT, dve_out=residual(k))


SG, SP_, SN = 64, 16, 64
ST = 2 * SG // 2


DRIVE_BANKS = 0, 1, 4


def s5(k):
    nc = k.nc
    with ExitStack() as ctx:
        def sb(name, shape, dt=F32):
            return ctx.enter_context(nc.sbuf_tensor(name, shape, dt))
        lam = sb("lam", [P, 3, ST])
        w = sb("s5_w", [P, 12, ST])
        dt_, r, y, th, sn, cs_, ar, ai, m2, cr, ci, t0 = (w[:, j, :] for j in range(12))
        bT = sb("s5_bT", [P, 2, 2, KT, 2, SN])
        cT = sb("s5_cT", [P, 3, ST, 2, SP_])
        yd = sb("s5_yd", [P, KT, T])
        even_odd = const(k, "b_half")
        c_half = const(k, "c_half")
        V = k.s5v
        A = k.s5a
        with nc.sbuf_tensor("s5_b_raw", [P, 2, 2, KT, SN], F32) as b_raw, \
                nc.sbuf_tensor("s5_c_raw", [P, 2, ST, SP_], F32) as c_raw:
            def side(sp):
                sp.dma_start(lam[:, :, :], k.ins["s5_lam"]).then_inc(k.side_here.s, 16)
                sp.dma_start(b_raw[:, :, :, :, :].rearrange("p a b c d -> p (a b c d)"), k.ins["s5_b"]).then_inc(k.side_here.s, 16)
                sp.dma_start(c_raw[:, :, :, :].rearrange("p a b c -> p (a b c)"), k.ins["s5_c"]).then_inc(k.side_here.s, 16)

            norm(k, k.x, KT, VEC_AT["norm_mix_g"] + KT, k.h, D, side=side)
            with nc.sbuf_tensor("s5_c_w", [P, 4, ST, SP_], F32) as c_w, nc.Block() as block:
                b0, v0, a0 = k.side_here.n, V.n, A.n

                @block.gpsimd
                def _(pool):
                    pool.wait_ge(k.side_here.s, b0 + 48)
                    for half in range(2):
                        for a in range(2):
                            pool.tensor_scalar(bT[:, a, :, :, half, :].rearrange("p a b n -> p (a b) n"),
                                               b_raw[:, a, :, :, :].rearrange("p a b n -> p (a b) n"),
                                               even_odd[:, half:half + 1], None, ALU.mult)

                @block.scalar
                def _(act):
                    act.wait_ge(k.side_here.s, b0 + 48)
                    act.activation(dt_, lam[:, 2, :], ACT.Exp).then_inc(A.s, 1)
                    act.wait_ge(V.s, v0 + 1)
                    act.activation(r, ar, ACT.Exp).then_inc(A.s, 1)
                    act.wait_ge(V.s, v0 + 4)
                    act.activation(sn, y, ACT.Sin, scale=TWO_PI).then_inc(A.s, 1)
                    act.activation(t0, y, ACT.Abs).then_inc(A.s, 1)
                    act.wait_ge(A.s, a0 + 4)
                    act.activation(cs_, t0, ACT.Sin, scale=-TWO_PI, bias=k.half_pi[:, 0:1]).then_inc(A.s, 1)

                @block.vector
                def _(dve):
                    n = [v0]

                    def tick(ins):
                        n[0] += 1
                        ins.then_inc(V.s, 1)
                        dve.wait_ge(V.s, n[0])
                    dve.wait_ge(A.s, a0 + 1)
                    tick(dve.tensor_tensor(ar, lam[:, 0, :], dt_, ALU.mult))
                    tick(dve.scalar_tensor_tensor(th, lam[:, 1, :], 1.0 / (2 * math.pi), dt_, ALU.mult, ALU.mult))
                    tick(dve.tensor_scalar(m2, th, ROUND, -ROUND, ALU.add, ALU.add))
                    tick(dve.tensor_tensor(y, th, m2, ALU.subtract))
                    dve.wait_ge(A.s, a0 + 5)
                    tick(dve.tensor_tensor(ar, r, cs_, ALU.mult))
                    tick(dve.tensor_scalar(ar, ar, -1.0, None, ALU.add))
                    tick(dve.tensor_tensor(ai, r, sn, ALU.mult))
                    tick(dve.tensor_tensor(m2, lam[:, 0, :], lam[:, 0, :], ALU.mult))
                    tick(dve.tensor_tensor(t0, lam[:, 1, :], lam[:, 1, :], ALU.mult))
                    tick(dve.tensor_tensor(m2, m2, t0, ALU.add))
                    tick(dve.reciprocal(m2, m2))
                    tick(dve.tensor_tensor(cr, ar, lam[:, 0, :], ALU.mult))
                    tick(dve.tensor_tensor(t0, ai, lam[:, 1, :], ALU.mult))
                    tick(dve.tensor_tensor(cr, cr, t0, ALU.add))
                    tick(dve.tensor_tensor(cr, cr, m2, ALU.mult))
                    tick(dve.tensor_tensor(ci, ai, lam[:, 0, :], ALU.mult))
                    tick(dve.tensor_tensor(t0, ar, lam[:, 1, :], ALU.mult))
                    tick(dve.tensor_tensor(ci, ci, t0, ALU.subtract))
                    tick(dve.tensor_tensor(ci, ci, m2, ALU.mult))
                    crb = spread(cr.rearrange("p (c o) -> p c o", o=1), 2, SP_)
                    cib = spread(ci.rearrange("p (c o) -> p c o", o=1), 2, SP_)
                    tick(dve.tensor_tensor(c_w[:, 0, :, :], c_raw[:, 0, :, :], crb, ALU.mult))
                    tick(dve.tensor_tensor(c_w[:, 1, :, :], c_raw[:, 1, :, :], cib, ALU.mult))
                    tick(dve.tensor_tensor(c_w[:, 0, :, :], c_w[:, 0, :, :], c_w[:, 1, :, :], ALU.subtract))
                    tick(dve.tensor_tensor(c_w[:, 2, :, :], c_raw[:, 0, :, :], cib, ALU.mult))
                    tick(dve.tensor_tensor(c_w[:, 3, :, :], c_raw[:, 1, :, :], crb, ALU.mult))
                    tick(dve.tensor_tensor(c_w[:, 2, :, :], c_w[:, 2, :, :], c_w[:, 3, :, :], ALU.add))
                    for half in range(2):
                        for j, (src, sign) in enumerate(((0, 1.0), (0, -1.0), (2, -1.0))):
                            tick(dve.tensor_scalar(cT[:, j, :, half, :], c_w[:, src, :, :], c_half[:, half:half + 1], sign,
                                                   ALU.mult, ALU.mult))
                    tick(dve.tensor_scalar(y[:, ST // 2:ST], y[:, ST // 2:ST], -1.0, None, ALU.mult))
                    k.s5_ticks = n[0] - v0
                k.side_here.n += 48
                V.n += k.s5_ticks
                A.n += 5

        with nc.sbuf_tensor([P, 2, 2, T], F32) as ph, nc.sbuf_tensor([P, 2, 3, T], F32) as ang, \
                nc.sbuf_tensor([P, 3, 2, T], F32) as tab, nc.sbuf_tensor([P, 2, 2, T], F32) as mod, \
                nc.sbuf_tensor([P, 2, 2, T], F32) as bm, nc.sbuf_tensor([P, 2, 2, T], F32) as g, \
                nc.sbuf_tensor([P, 2, 2, 2, T], F32) as prod, nc.Block() as block:
            order = [(kt, j, d) for kt in range(KT) for j in range(4) for d in range(2)]
            s_bu, s_y, s_ang, s_phase, s_tab = k.s5_bu, k.s5_y, k.s5_ang, k.s5_phase, k.s5_tab
            s_abs, s_bm = k.s5_abs, k.s5_bm
            s_free, s_scan, s_prod, s_out = k.s5_free, k.s5_scan, k.s5_prod, k.s5_out
            tvec = const(k, "time")
            v1 = V.n

            def cidx(kt, j, d):
                return d * (ST // 2) + kt * 4 + j

            @block.tensor
            def _(pe):
                def drive(q):
                    kt, j, d = order[q]
                    if q >= 3:
                        pe.wait_ge(s_free.s, q - 2)
                    for a in range(2):
                        mm = pe.matmul(k.ps[:, DRIVE_BANKS[q % 3], a * T:(a + 1) * T],
                                       bT[32 * j:32 * j + 32, a, d, kt, :, :].rearrange("p a b -> p (a b)"),
                                       k.h[32 * j:32 * j + 32, kt, :], start=True, stop=True, tile_position=(32 * j, 0))
                    mm.then_inc(s_bu.s, 1)
                drive(0)
                drive(1)
                for q, (kt, j, d) in enumerate(order):
                    if q + 2 < ST:
                        drive(q + 2)
                    if j == 0 and d == 0 and kt >= 2:
                        pe.wait_ge(s_out.s, kt - 1)
                    pe.wait_ge(s_prod.s, q + 1)
                    c = cidx(kt, j, d)
                    for m, (a, b, which) in enumerate(((0, 0, 0), (1, 1, 1), (0, 1, 2), (1, 0, 2))):
                        mm = pe.matmul(k.ps[32 * j:32 * j + 32, 2 + kt % 2, 0:T],
                                       cT[:, which, c, :, :].rearrange("p a b -> p (a b)"), prod[:, q % 2, a, b, :],
                                       start=(d == 0 and m == 0), stop=(d == 1 and m == 3), tile_position=(0, 32 * j))
                    mm.then_inc(s_y.s, 1)

            @block.scalar
            def _(act):
                def phase(q):
                    c = cidx(*order[q])
                    if q >= 2:
                        act.wait_ge(s_ang.s, q - 1)
                    act.activation(ph[:, q % 2, 0, :], tvec, ACT.Identity, scale=y[:, c:c + 1], bias=k.round_c[:, 0:1])
                    act.activation(ph[:, q % 2, 1, :], tvec, ACT.Copy, scale=y[:, c:c + 1]).then_inc(s_phase.s, 1)
                act.wait_ge(V.s, v1)
                phase(0)
                for q in range(ST):
                    if q + 1 < ST:
                        phase(q + 1)
                    act.wait_ge(s_ang.s, q + 1)
                    if q >= 3:
                        act.wait_ge(s_prod.s, q - 2)
                    act.activation(tab[:, q % 3, 1, :], ang[:, q % 2, 0, :], ACT.Sin, scale=-TWO_PI)
                    act.activation(ang[:, q % 2, 1, :], ang[:, q % 2, 0, :], ACT.Abs).then_inc(s_abs.s, 1)
                    act.wait_ge(s_abs.s, q + 1)
                    act.activation(tab[:, q % 3, 0, :], ang[:, q % 2, 1, :], ACT.Sin, scale=-TWO_PI,
                                   bias=k.half_pi[:, 0:1]).then_inc(s_tab.s, 1)

            def y_out(dve, kt):
                dve.wait_ge(s_y.s, 8 * (kt + 1))
                dve.scalar_tensor_tensor(yd[:, kt, :], k.h[:, kt, :], k.vec[:, VEC_AT["s5_d"] + kt:VEC_AT["s5_d"] + kt + 1],
                                         k.ps[:, 2 + kt % 2, 0:T], ALU.mult, ALU.add).then_inc(s_out.s, 1)

            @block.vector
            def _(dve):
                def angle(q):
                    dve.wait_ge(s_phase.s, q + 1)
                    if q >= 2:
                        dve.wait_ge(s_tab.s, q - 1)
                    dve.scalar_tensor_tensor(ang[:, q % 2, 0, :], ph[:, q % 2, 0, :], -ROUND, ph[:, q % 2, 1, :],
                                             ALU.add, ALU.subtract).then_inc(s_ang.s, 1)
                angle(0)
                for q, (kt, j, d) in enumerate(order):
                    c = cidx(kt, j, d)
                    if q + 1 < ST:
                        angle(q + 1)
                    s = q % 2
                    cosb = spread(tab[:, q % 3, 0:1, :], 1, 2)
                    sinb = spread(tab[:, q % 3, 1:2, :], 1, 2)
                    bu = k.ps[:, DRIVE_BANKS[q % 3], :].rearrange("p (a n) -> p a n", a=2)
                    dve.wait_ge(s_bu.s, q + 1)
                    dve.wait_ge(s_tab.s, q + 1)
                    dve.tensor_tensor(mod[:, 0, :, :], bu, cosb, ALU.mult)
                    dve.tensor_tensor(mod[:, 1, :, :], bu, sinb, ALU.mult).then_inc(s_free.s, 1)
                    dve.wait_ge(s_free.s, q + 1)
                    dve.tensor_tensor(bm[:, s, 0, :], mod[:, 0, 0, :], mod[:, 1, 1, :], ALU.add)
                    dve.tensor_tensor(bm[:, s, 1, :], mod[:, 0, 1, :], mod[:, 1, 0, :], ALU.subtract).then_inc(s_bm.s, 1)
                    dve.wait_ge(s_bm.s, q + 1)
                    if q >= 2:
                        dve.wait_ge(s_prod.s, q - 1)
                    rb = spread(r[:, c:c + 1], 1, T)
                    for a in range(2):
                        if d == 0:
                            mm = dve.tensor_tensor_scan(g[:, s, a, :], rb, bm[:, s, a, :], 0.0, ALU.mult, ALU.add)
                        else:
                            mm = dve.tensor_tensor_scan(g[:, s, a, ::-1], rb, bm[:, s, a, ::-1], 0.0, ALU.mult, ALU.add)
                    mm.then_inc(s_scan.s, 1)
                    if j == 3 and d == 1:
                        if kt > 0:
                            y_out(dve, kt - 1)
                y_out(dve, KT - 1)

            @block.gpsimd
            def _(pool):
                for q, (kt, j, d) in enumerate(order):
                    s = q % 2
                    pool.wait_ge(s_scan.s, q + 1)
                    if q >= 2:
                        pool.wait_ge(s_y.s, q - 1)
                    for a in range(2):
                        mm = pool.tensor_tensor(prod[:, s, a, :, :], spread(g[:, s, a:a + 1, :], 1, 2), tab[:, q % 3, :, :], ALU.mult)
                    mm.then_inc(s_prod.s, 1)

        parts = Parts(k, yd, k.hp, KT, gelu=True)

        with nc.sbuf_tensor([P, 2, T], F32) as sg, nc.sbuf_tensor([P, 2, T], F32) as pr:
            glu(k, k.hp, sg, pr, parts)


def spread(ap, axis, n):
    shape = list(ap.shape)
    shape[axis] = n
    return ap.broadcast_to(shape)


def glu(k, src, sg, pr, parts):
    first = k.used
    b_sig, b_out, b_mul = k.act_done.n, k.out_done.n, k.mul_done.n
    with k.nc.Block() as block:
        @block.sync
        def _(sp):
            loads(k, sp, first, 2 * KT)

        @block.tensor
        def _(pe):
            w = Weights(k, pe, first)
            for n in range(KT):
                if n >= 2:
                    pe.wait_ge(k.mul_done.s, b_mul + n - 1)
                for half in range(2):
                    for j in range(KT):
                        if n == 0 and half == 0:
                            parts.here(pe, j)
                        mm = product(pe, k.ps[:, n % 2, half * T:(half + 1) * T], w.tile((2 * n + half) * ITEM + j),
                                     pair_tile(src, j), start=(j == 0), stop=(j == KT - 1))
                    mm.then_inc(k.item_used, 1)

        block.gpsimd(parts.gpsimd)

        @block.scalar
        def _(act):
            parts.scalar(act)
            for n in range(KT):
                act.wait_ge(k.item_used, first + 2 * n + 2)
                if n >= 2:
                    act.wait_ge(k.mul_done.s, b_mul + n - 1)
                act.activation(sg[:, n % 2, :], k.ps[:, n % 2, 0:T], ACT.Sigmoid).then_inc(k.act_done.s, 1)
                for half in range(2):
                    round_item(k, act, first + 2 * n + half)

        @block.vector
        def _(dve):
            parts.vector(dve)
            for n in range(KT):
                dve.wait_ge(k.act_done.s, b_sig + n + 1)
                dve.tensor_tensor(pr[:, n % 2, :], sg[:, n % 2, :], k.ps[:, n % 2, T:2 * T], ALU.mult)\
                   .then_inc(k.mul_done.s, 1)
                dve.wait_ge(k.mul_done.s, b_mul + n + 1)
                dve.tensor_tensor(k.x[:, n, :], k.x[:, n, :], pr[:, n % 2, :], ALU.add)
                for half in range(2):
                    cut_item(k, dve, first + 2 * n + half)
    k.used += 2 * KT
    k.act_done.n += KT
    k.mul_done.n += KT



AH = 16
GROUPS = 3
SCORE_BANKS = 0, 1, 6
NEG = -1e30


def token_major(k, jobs, kt=KT):
    first = k.used
    b_out = k.out_done.n
    with k.nc.Block() as block:
        @block.sync
        def _(sp):
            loads(k, sp, first, kt * len(jobs))

        @block.tensor
        def _(pe):
            w = Weights(k, pe, first)
            for n, (src, _) in enumerate(jobs):
                if n >= 2:
                    pe.wait_ge(k.out_done.s, b_out + n - 1)
                    pe.wait_ge(k.token_out.s, k.token_out.n + n - 1)
                for j in range(kt):
                    wh, wl = w.tile((n * kt + j) * ITEM, ITEM * P)
                    for a in range(2):
                        for c in range(2):
                            half = slice(c * 512, (c + 1) * 512)
                            mm = product(pe, k.ps[:, n % 2 * 4 + 2 * a + c, :], pair_tile(src, j, slice(a * P, (a + 1) * P)),
                                         (wh[:, half], wl[:, half]), start=(j == 0), stop=(j == kt - 1))
                    mm.then_inc(k.item_used, 1)

        @block.scalar
        def _(act):
            for n, (_, out3) in enumerate(jobs):
                for j in range(kt):
                    round_item(k, act, first + n * kt + j)
                act.wait_ge(k.item_used, first + (n + 1) * kt)
                act.activation(out3[:, 0, 0:512], k.ps[:, n % 2 * 4, :], ACT.Copy)
                act.activation(out3[:, 0, 512:1024], k.ps[:, n % 2 * 4 + 1, :], ACT.Copy).then_inc(k.token_out.s, 1)

        @block.vector
        def _(dve):
            for n, (_, out3) in enumerate(jobs):
                for j in range(kt):
                    cut_item(k, dve, first + n * kt + j)
                dve.wait_ge(k.item_used, first + (n + 1) * kt)
                dve.tensor_copy(out3[:, 1, 0:512], k.ps[:, n % 2 * 4 + 2, :])
                dve.tensor_copy(out3[:, 1, 512:1024], k.ps[:, n % 2 * 4 + 3, :]).then_inc(k.out_done.s, 1)
    k.used += kt * len(jobs)
    k.out_done.n += len(jobs)
    k.token_out.n += len(jobs)


def attention_bias(k, tab0, tab12):
    nc = k.nc
    with nc.sbuf_tensor("ab_onehot", [32, 3, 512], F32) as onehot, nc.sbuf_tensor("ab_mask", [AH, 3, 512], F32) as mask, \
            nc.sbuf_tensor("ab_rel", [32, GROUPS * AH], F32) as rel, \
            nc.sbuf_tensor("ab_tab", [AH, 3, 512], F32) as tab, nc.Block() as block:
        b_in, b_p, b_t, b_w = k.side_here.n, k.bias_ps.n, k.bias_tab.n, k.bias_written.n

        @block.sync
        def _(sp):
            sp.dma_start(onehot[:, :, :], k.ins["bias_onehot"]).then_inc(k.side_here.s, 16)
            sp.dma_start(mask[:, :, :], k.ins["bias_mask"]).then_inc(k.side_here.s, 16)
            sp.dma_start(rel[:, :], k.ins["rel_bias"]).then_inc(k.side_here.s, 16)
            sp.wait_ge(k.bias_tab.s, b_t + 1)
            sp.dma_start(tab0, tab[:, 0, :]).then_inc(k.bias_written.s, 16)
            sp.dma_start(tab12, tab[:, 1:3, 0:P]).then_inc(k.bias_written.s, 16)
            sp.wait_ge(k.bias_written.s, b_w + 32)

        @block.tensor
        def _(pe):
            pe.wait_ge(k.side_here.s, b_in + 48)
            for g in range(GROUPS):
                mm = pe.matmul(k.ps[0:AH, g, :], rel[:, g * AH:(g + 1) * AH], onehot[:, g, :], start=True, stop=True)
            mm.then_inc(k.bias_ps.s, 1)

        @block.vector
        def _(dve):
            dve.wait_ge(k.bias_ps.s, b_p + 1)
            dve.tensor_tensor(tab[:, :, :], k.ps[0:AH, 0:3, :], mask[:, :, :], ALU.add).then_inc(k.bias_tab.s, 1)
        k.side_here.n += 48
        k.bias_ps.n += 1
        k.bias_tab.n += 1
        k.bias_written.n += 32


def attention(k):
    nc = k.nc
    with ExitStack() as ctx:
        def sb(name, shape, dt=F32):
            return ctx.enter_context(nc.sbuf_tensor(name, shape, dt))
        tab0 = nc.dram_tensor("bias_group0", (AH, 512), F32, kind="Internal").ap()
        tab12 = nc.dram_tensor("bias_groups12", (AH, 2, P), F32, kind="Internal").ap()
        attention_bias(k, tab0, tab12)
        qT = sb("at_q", [P, 24, T])
        kT = sb("at_k", [P, 24, T])
        v = sb("at_v", [P, GROUPS, 2, D])
        with nc.sbuf_tensor("at_ph", [P, KT, T], F32R) as ph, nc.sbuf_tensor("at_pl", [P, KT, T], F32R) as pl:
            sort_tokens(k, (ph, pl), falling=True)
            project_heads(k, [(ph, pl)] * GROUPS, VEC_AT["attn_q_gain"], qT, scaled=True)
            sort_tokens(k, (ph, pl), falling=False)
            srcs = [k.hp, (ph, pl), (ph, pl)]
            project_heads(k, srcs, VEC_AT["attn_k_gain"], kT, scaled=False)
            token_major(k, [(srcs[g], v[:, g, :, :]) for g in range(GROUPS)])
        oT = k.h
        attend(k, tab0, tab12, qT, kT, v, oT)
        advance([k.at_sc, k.at_max, k.at_neg, k.at_exp, k.at_rd, k.at_diag, k.at_tr, k.at_cp, k.at_pv], 2 * AH)
        advance([k.at_o], AH // 2)
        linear(k, k.hp, KT, KT, dve_out=residual(k), parts=(Parts(k, oT, k.hp, KT),))


def sort_tokens(k, dst, falling):
    with k.nc.Block() as block:
        def part(a, j):
            by_class = k.hp[a][:, j, :].rearrange("p (m c) -> p c m", c=4).bitcast(F32)
            return dst[a][:, j, :].rearrange("p (c m) -> p c m", c=4), by_class[:, :, ::-1] if falling else by_class

        @block.vector
        def _(dve):
            for j in range(KT):
                dve.tensor_copy(*part(0, j))

        @block.scalar
        def _(act):
            for j in range(KT):
                out, src = part(1, j)
                act.activation(out, src, ACT.Copy)


def advance(signals, n):
    for s in signals:
        s.n += n


def project_heads(k, srcs, gain_col, dst, scaled):
    nc = k.nc
    first = k.used
    N = KT * GROUPS
    b_sq, b_ss, b_rt, b_inv, b_out = k.sq_done.n, k.sum_done.n, k.root_done.n, k.norm_done.n, k.out_done.n
    with nc.sbuf_tensor(f"ph_sq{first}", [P, 2, T], F32) as sq, nc.sbuf_tensor(f"ph_rt{first}", [P, 2, T], F32) as rt, \
            nc.sbuf_tensor(f"ph_inv{first}", [P, 2, T], F32) as inv, nc.Block() as block:
        @block.sync
        def _(sp):
            loads(k, sp, first, N)

        @block.tensor
        def _(pe):
            w = Weights(k, pe, first)

            def project(n):
                if n >= 4:
                    pe.wait_ge(k.out_done.s, b_out + n - 3)
                for j in range(KT):
                    mm = product(pe, k.ps[:, n % 4, 0:T], w.tile(n * ITEM + j), pair_tile(srcs[n // KT], j), start=(j == 0), stop=(j == KT - 1))
                mm.then_inc(k.item_used, 1)
            project(0)
            for n in range(N):
                if n + 1 < N:
                    project(n + 1)
                pe.wait_ge(k.sq_done.s, b_sq + n + 1)
                if n >= 2:
                    pe.wait_ge(k.root_done.s, b_rt + n - 1)
                pe.matmul(k.ps[:, 4 + n % 2, 0:T], const(k, "two_heads"), sq[:, n % 2, :], start=True, stop=True)\
                  .then_inc(k.sum_done.s, 1)

        @block.scalar
        def _(act):
            for n in range(N):
                act.wait_ge(k.item_used, first + n + 1)
                if n >= 2:
                    act.wait_ge(k.sum_done.s, b_ss + n - 1)
                act.activation(sq[:, n % 2, :], k.ps[:, n % 4, 0:T], ACT.Square).then_inc(k.sq_done.s, 1)
                act.wait_ge(k.sum_done.s, b_ss + n + 1)
                if n >= 2:
                    act.wait_ge(k.norm_done.s, b_inv + n - 1)
                act.activation(rt[:, n % 2, :], k.ps[:, 4 + n % 2, 0:T], ACT.Sqrt, scale=1.0 if scaled else 1.0 / 64,
                               bias=k.eps64[:, 0:1] if scaled else k.eps[:, 0:1]).then_inc(k.root_done.s, 1)
                round_item(k, act, first + n)

        @block.gpsimd
        def _(pool):
            for n in range(N):
                cut_item(k, pool, first + n)

        @block.vector
        def _(dve):
            for n in range(N):
                dve.wait_ge(k.root_done.s, b_rt + n + 1)
                dve.reciprocal(inv[:, n % 2, :], rt[:, n % 2, :]).then_inc(k.norm_done.s, 1)
                dve.wait_ge(k.norm_done.s, b_inv + n + 1)
                dve.scalar_tensor_tensor(dst[:, n, :], k.ps[:, n % 4, 0:T], k.vec[:, gain_col + n // KT:gain_col + n // KT + 1],
                                         inv[:, n % 2, :], ALU.mult, ALU.mult).then_inc(k.out_done.s, 1)
    k.used += N
    for s in (k.sq_done, k.sum_done, k.root_done, k.norm_done, k.out_done):
        s.n += N


def attend(k, tab0, tab12, qT, kT, v, oT):
    nc = k.nc
    HG = 2
    with ExitStack() as ctx:
        def sb(name, shape, dt=F32):
            return ctx.enter_context(nc.sbuf_tensor(name, shape, dt))
        bias0 = sb("at_bias0", [P, 2, HG, 2, T])
        bias12 = sb("at_bias12", [P, 2, HG, 2, P])
        sc = sb("at_scores", [P, 2, 512])
        pr = sb("at_probs", [P, 2, 512])
        pt = sb("at_probs_t", [P, 2, 512])
        st = sb("at_stats", [P, 2, 4])
        dg = sb("at_diag", [P, 2, P])
        steps = [(h, a) for h in range(AH) for a in range(2)]
        N = len(steps)
        ident = const(k, "ident")
        s_bias, s_fill = k.at_bias, k.at_fill
        s_sc, s_max, s_neg, s_exp, s_rd, s_diag, s_tr, s_cp, s_pv, s_o = (
            k.at_sc, k.at_max, k.at_neg, k.at_exp, k.at_rd, k.at_diag, k.at_tr, k.at_cp, k.at_pv, k.at_o)
        block = ctx.enter_context(nc.Block())

        @block.sync
        def _(sp):
            sp.wait_ge(s_fill.s, 1)
            for hg in range(AH // HG):
                if hg >= 2:
                    sp.wait_ge(s_max.s, 2 * HG * (hg - 1))
                for c in range(2):
                    rows = slice(64 * c, 64 * c + 64)
                    for hh in range(HG):
                        h = hg * HG + hh
                        for a in range(2):
                            src = bass.AP(tab0.tensor, h * 512 + 3 - (2 * a + c), [[4, 64], [1, T]])
                            sp.dma_start(bias0[rows, hg % 2, hh, a, :], src).then_inc(s_bias[hg % 2].s, 16)
                    src = bass.AP(tab12.tensor, hg * HG * 2 * P, [[1, 64], [P, 2 * HG], [1, 64]])
                    sp.dma_start(bias12[rows, hg % 2, :, :, 64 * c:64 * c + 64].rearrange("p h g n -> p (h g) n"), src)\
                      .then_inc(s_bias[hg % 2].s, 16)

        @block.gpsimd
        def _(pool):
            pool.memset(bias12[:, :, :, :, :], NEG).then_inc(s_fill.s, 1)

        @block.tensor
        def _(pe):
            def scores(q):
                h, a = steps[q]
                p0, n = 64 * (h % 2), h // 2
                if q >= 3:
                    pe.wait_ge(s_max.s, q - 2)
                for g in range(GROUPS):
                    keys = slice(0, T) if g == 0 else slice(a * P, (a + 1) * P)
                    col = 0 if g == 0 else T + (g - 1) * P
                    mm = pe.matmul(k.ps[:, SCORE_BANKS[q % 3], col:col + (T if g == 0 else P)], qT[p0:p0 + 64, 8 * g + n, a * P:(a + 1) * P],
                                   kT[p0:p0 + 64, 8 * g + n, keys], start=True, stop=True, tile_position=(p0, 0))
                mm.then_inc(s_sc.s, 1)

            def transposed(q):
                pe.wait_ge(s_diag.s, q + 1)
                if q >= 2:
                    pe.wait_ge(s_cp.s, q - 1)
                for j in range(4):
                    mm = pe.matmul(k.ps[:, 2 + q % 2, j * P:(j + 1) * P], pr[:, q % 2, j * P:(j + 1) * P], dg[:, q % 2, :],
                                   start=True, stop=True)
                mm.then_inc(s_tr.s, 1)

            def values(q):
                h, a = steps[q]
                p0, n = 64 * (h % 2), h // 2
                pe.wait_ge(s_cp.s, q + 1)
                if q % 4 == 0 and n >= 2:
                    pe.wait_ge(s_o.s, n - 1)
                vs = [v[:, 0, 0, :], v[:, 0, 1, :], v[:, 1, a, :], v[:, 2, a, :]]
                for j in range(4):
                    mm = pe.matmul(k.ps[p0:p0 + 64, 4 + n % 2, a * P:(a + 1) * P], vs[j][:, h * 64:(h + 1) * 64],
                                   pt[:, q % 2, j * P:(j + 1) * P], start=(j == 0), stop=(j == 3), tile_position=(0, p0))
                mm.then_inc(s_pv.s, 1)
            scores(0)
            scores(1)
            scores(2)
            for q in range(N):
                transposed(q)
                if q + 3 < N:
                    scores(q + 3)
                if q > 0:
                    values(q - 1)
            values(N - 1)

        def head_pair_out(dve, n):
            dve.wait_ge(s_pv.s, 4 * (n + 1))
            dst = oT[:, n, :].rearrange("p (m c) -> p c m", c=4)
            dve.tensor_copy(dst[:, :, ::-1], k.ps[:, 4 + n % 2, 0:T].rearrange("p (c m) -> p c m", c=4))\
               .then_inc(s_o.s, 1)

        @block.vector
        def _(dve):
            def masked(q):
                h, a = steps[q]
                hg, hh = h // HG, h % HG
                dve.wait_ge(s_sc.s, q + 1)
                if a == 0 and hh == 0:
                    dve.wait_ge(s_bias[hg % 2].s, 16 * (4 * HG // 2 * 2 + 2) * (hg // 2 + 1))
                if q >= 2:
                    dve.wait_ge(s_exp.s, q - 1)
                b12 = bias12[:, hg % 2, hh, :, :].rearrange("p g n -> p (g n)")
                dve.tensor_tensor(sc[:, q % 2, 0:T], k.ps[:, SCORE_BANKS[q % 3], 0:T], bias0[:, hg % 2, hh, a, :], ALU.add)
                dve.tensor_tensor(sc[:, q % 2, T:512], k.ps[:, SCORE_BANKS[q % 3], T:512], b12, ALU.add).then_inc(s_max.s, 1)
                dve.wait_ge(s_max.s, q + 1)
                dve.tensor_reduce(st[:, q % 2, 1:2], sc[:, q % 2, :], op=ALU.max, axis=AX.X, negate=True).then_inc(s_neg.s, 1)
            masked(0)
            for q in range(N):
                if q + 1 < N:
                    masked(q + 1)
                dve.wait_ge(s_exp.s, q + 1)
                dve.reciprocal(st[:, q % 2, 3:4], st[:, q % 2, 2:3]).then_inc(s_rd.s, 1)
                dve.wait_ge(s_rd.s, q + 1)
                if q >= 2:
                    dve.wait_ge(s_tr.s, q - 1)
                dve.tensor_scalar(dg[:, q % 2, :], ident, st[:, q % 2, 3:4], None, ALU.mult).then_inc(s_diag.s, 1)
                h, a = steps[q]
                if h % 2 == 0 and a == 0 and h > 0:
                    head_pair_out(dve, h // 2 - 1)
            head_pair_out(dve, AH // 2 - 1)

        @block.scalar
        def _(act):
            def copied(q):
                act.wait_ge(s_tr.s, q + 1)
                if q >= 2:
                    act.wait_ge(s_pv.s, q - 1)
                act.activation(pt[:, q % 2, :], k.ps[:, 2 + q % 2, :], ACT.Copy).then_inc(s_cp.s, 1)
            for q in range(N):
                act.wait_ge(s_neg.s, q + 1)
                if q >= 2:
                    act.wait_ge(s_tr.s, q - 1)
                    act.wait_ge(s_rd.s, q - 1)
                act.activation(pr[:, q % 2, :], sc[:, q % 2, :], ACT.Exp, bias=st[:, q % 2, 1:2],
                               accum_out=st[:, q % 2, 2:3]).then_inc(s_exp.s, 1)
                if q > 0:
                    copied(q - 1)
            copied(N - 1)



def post_norm(k, m, gain_col):
    norm(k, m, KT, gain_col, k.h, D, add_to=k.x)


def store_to(dst):
    def out(dve, n, ps):
        return dve.tensor_copy(tile_of(dst, n), ps)
    return out


def ffn_second(k, layer):
    parts = norm(k, k.x, KT, VEC_AT["norm_ffn_pre_2"] + KT * layer, k.h, D, pair=k.hp)
    with k.nc.sbuf_tensor(f"ffn_m{layer}", [P, KT, T], F32) as m:
        swiglu(k, k.hp, store_to(m), parts)
        post_norm(k, m, VEC_AT["norm_ffn_post_2"] + KT * layer)


QL, KVL = 4, 2
MH = 8
MLA_SCALE = 192.0


def hybrid(k):
    nc = k.nc
    with ExitStack() as ctx:
        def sb(name, shape, dt=F32):
            return ctx.enter_context(nc.sbuf_tensor(name, shape, dt))
        parts = norm(k, k.x, KT, VEC_AT["norm_mix_pre_2"], k.h, D, pair=k.hp)
        y = sb("hy_y", [P, 2 * KT, T])
        cq = sb("hy_cq", [P, QL, T])
        ckv = sb("hy_ckv", [P, KVL, T])
        kpe = sb("hy_kpe", [P, T])
        with nc.sbuf_tensor("rg_x", [P, KT, T + 3], F32) as xr, nc.sbuf_tensor("rg_gate", [P, KT, T], F32) as gate:
            with nc.Block() as block:
                @block.gpsimd
                def _(pool):
                    pool.memset(xr[:, :, 0:3], 0.0)

            def project_out(act, n, ps):
                if n < KT:
                    return act.activation(xr[:, n, 3:3 + T], ps, ACT.Copy)
                if n < 2 * KT:
                    return act.activation(gate[:, n - KT, :], ps, ACT.Gelu_apprx_tanh)
                if n < 2 * KT + QL:
                    return act.activation(cq[:, n - 2 * KT, :], ps, ACT.Copy)
                if n < 2 * KT + QL + KVL:
                    return act.activation(ckv[:, n - 2 * KT - QL, :], ps, ACT.Copy)
                return act.activation(kpe[:, :], ps, ACT.Copy)
            with nc.sbuf_tensor("rg_xc", [P, KT, T], F32) as xc, nc.sbuf_tensor("rg_xch", [P, KT, T], F32R) as xch, \
                    nc.sbuf_tensor("rg_xcl", [P, KT, T], F32R) as xcl:
                linear(k, k.hp, KT, 2 * KT + QL + KVL + 1, act_out=project_out, parts=(parts,),
                       beside=RgConv(k, xr, xc, xch, xcl).beside)
                rg_lru(k, xr, xc, xch, xcl, gate, y)
        mla(k, cq, ckv, kpe, y)
        with nc.sbuf_tensor("hy_m", [P, KT, T], F32) as m, nc.sbuf_tensor("hy_yh", [P, 2 * KT, T], F32R) as yh, \
                nc.sbuf_tensor("hy_yl", [P, 2 * KT, T], F32R) as yl:
            linear(k, (yh, yl), 2 * KT, KT, dve_out=store_to(m), parts=(Parts(k, y, (yh, yl), 2 * KT),))
            post_norm(k, m, VEC_AT["norm_mix_post_2"])


class RgConv:

    def __init__(self, k, xr, xc, xch, xcl):
        self.k, self.xr, self.xc, self.xch, self.xcl = k, xr, xc, xch, xcl
        self.b_out, self.b_v = k.out_done.n, k.s5v.n
        advance((k.s5v,), 3 * KT)

    def beside(self, name, engine, b):
        if b < KT or b % 2:
            return
        k, n = self.k, (b - KT) // 2
        if name == "vector":
            engine.wait_ge(k.out_done.s, self.b_out + n + 1)
            bc = VEC_AT["rg_conv_b_2"] + n
            for j in range(4):
                wc = VEC_AT["rg_conv_w_2"] + KT * j + n
                w = k.vec[:, wc:wc + 1]
                if j == 0:
                    ins = engine.tensor_scalar(self.xc[:, n, :], self.xr[:, n, 0:T], w, k.vec[:, bc:bc + 1], ALU.mult, ALU.add)
                else:
                    engine.wait_ge(k.s5v.s, self.b_v + 3 * n + j)
                    ins = engine.scalar_tensor_tensor(self.xc[:, n, :], self.xr[:, n, j:j + T], w, self.xc[:, n, :], ALU.mult, ALU.add)
                ins.then_inc(k.s5v.s if j < 3 else k.rg_xc.s, 1)
        elif name == "scalar":
            engine.wait_ge(k.rg_xc.s, n + 1)
            engine.activation(self.xch[:, n, :], self.xc[:, n, :], ACT.Copy).then_inc(k.rg_high.s, 1)
        elif name == "gpsimd":
            engine.wait_ge(k.rg_high.s, n + 1)
            engine.tensor_tensor(self.xcl[:, n, :], self.xc[:, n, :], self.xch[:, n, :].bitcast(F32), ALU.subtract)


def rg_lru(k, xr, xc, xch, xcl, gate, y):
    nc = k.nc
    first = k.used
    V, A = k.s5v, k.s5a
    lam = VEC_AT["rg_lambda_2"]
    with ExitStack() as ctx:
        def sb(name, shape, dt=F32):
            return ctx.enter_context(nc.sbuf_tensor(name, shape, dt))
        col = sb("rg_col", [P, 6, KT])
        rc = sb("rg_rc", [P, 2, 2, T])
        b0 = sb("rg_b0", [P, KT, T])
        b1 = sb("rg_b1", [P, 2, T])
        hs = sb("rg_h", [P, 2, T])
        v0, a0 = V.n, A.n
        s_gate, s_sig, s_at, s_q, s_root, s_fin = (k.rg_gate.s, k.rg_sig.s, k.rg_at.s, k.rg_q.s, k.rg_root.s, k.rg_fin.s)
        s_tanh, s_quot, s_b0, s_h = k.rg_tanh.s, k.rg_quotient.s, k.rg_input.s, k.rg_scanned.s
        block = ctx.enter_context(nc.Block())
        lcol = k.vec[:, lam:lam + KT]

        @block.sync
        def _(sp):
            loads(k, sp, first, 2)

        @block.tensor
        def _(pe):
            w = Weights(k, pe, first)
            for n in range(KT):
                if n >= 4:
                    pe.wait_ge(s_sig, n - 3)
                for half in range(2):
                    mm = product(pe, k.ps[:, n % 4, half * T:(half + 1) * T], w.tile(2 * n + half), (xch[:, n, :], xcl[:, n, :]),
                                 start=True, stop=True)
                if n % 4 == 3:
                    mm.then_inc(k.item_used, 1)
                else:
                    mm.then_inc(s_gate, 1)

        def gates_ready(n):
            return (k.item_used, first + n // 4 + 1) if n % 4 == 3 else (s_gate, 3 * (n // 4) + n % 4 + 1)

        @block.scalar
        def _(act):
            act.activation(col[:, 0, :], lcol, ACT.Abs).then_inc(A.s, 1)
            act.wait_ge(A.s, a0 + 1)
            act.activation(col[:, 1, :], col[:, 0, :], ACT.Exp, scale=-1.0).then_inc(A.s, 1)
            act.wait_ge(A.s, a0 + 2)
            act.activation(col[:, 2, :], col[:, 1, :], ACT.Ln, bias=k.one_c[:, 0:1]).then_inc(A.s, 1)
            act.wait_ge(V.s, v0 + 3)
            for n in range(KT):
                act.wait_ge(*gates_ready(n))
                ba, bx = VEC_AT["rg_gate_a_b_2"] + n, VEC_AT["rg_gate_x_b_2"] + n
                act.activation(xr[:, n, 0:T], k.ps[:, n % 4, 0:T], ACT.Sigmoid, bias=k.vec[:, ba:ba + 1])
                act.activation(y[:, KT + n, :], k.ps[:, n % 4, T:2 * T], ACT.Sigmoid, bias=k.vec[:, bx:bx + 1]).then_inc(s_sig, 1)
                act.wait_ge(s_sig, n + 1)
                act.activation(y[:, n, :], xr[:, n, 0:T], ACT.Tanh, scale=col[:, 5, n:n + 1]).then_inc(s_tanh, 1)
            for item in range(2):
                round_item(k, act, first + item)
            for n in range(KT):
                act.activation(xr[:, n, 0:T], xr[:, n, 0:T], ACT.Exp, scale=col[:, 4, n:n + 1]).then_inc(s_at, 1)
            for n in range(KT):
                act.wait_ge(s_q, n + 1)
                act.activation(y[:, n, :], y[:, n, :], ACT.Sqrt, scale=2.0).then_inc(s_root, 1)

        @block.gpsimd
        def _(pool):
            for n in range(KT):
                pool.wait_ge(s_sig, n + 1)
                pool.tensor_tensor(b0[:, n, :], y[:, KT + n, :], xc[:, n, :], ALU.mult).then_inc(s_b0, 1)
                pool.wait_ge(s_quot, n + 1)
                pool.tensor_tensor(y[:, n, :], y[:, n, :], rc[:, n % 2, 1, :], ALU.mult).then_inc(s_q, 1)
            for item in range(2):
                cut_item(k, pool, first + item)
            for n in range(KT):
                pool.wait_ge(s_h, n + 1)
                pool.tensor_tensor(y[:, n, :], hs[:, n % 2, :], gate[:, n, :], ALU.mult).then_inc(s_fin, 1)

        @block.vector
        def _(dve):
            dve.wait_ge(A.s, a0 + 3)
            dve.tensor_scalar(col[:, 3, :], lcol, -1.0, 0.0, ALU.mult, ALU.max).then_inc(V.s, 1)
            dve.wait_ge(V.s, v0 + 1)
            dve.tensor_tensor(col[:, 3, :], col[:, 3, :], col[:, 2, :], ALU.add).then_inc(V.s, 1)
            dve.wait_ge(V.s, v0 + 2)
            dve.tensor_scalar(col[:, 5, :], col[:, 3, :], 8.0, None, ALU.mult)
            dve.tensor_scalar(col[:, 4, :], col[:, 3, :], -8.0, None, ALU.mult).then_inc(V.s, 1)
            for n in range(KT):
                dve.wait_ge(s_tanh, n + 1)
                dve.tensor_scalar(rc[:, n % 2, 0, :], y[:, n, :], 1.0, None, ALU.add).then_inc(V.s, 1)
                dve.wait_ge(V.s, v0 + 3 + n + 1)
                if n >= 2:
                    dve.wait_ge(s_q, n - 1)
                dve.reciprocal(rc[:, n % 2, 1, :], rc[:, n % 2, 0, :]).then_inc(s_quot, 1)
            for n in range(KT):
                dve.wait_ge(s_root, n + 1)
                dve.wait_ge(s_b0, n + 1)
                dve.tensor_tensor(b1[:, n % 2, :], b0[:, n, :], y[:, n, :], ALU.mult).then_inc(V.s, 1)
                dve.wait_ge(V.s, v0 + 3 + KT + n + 1)
                if n == 0:
                    dve.wait_ge(s_at, KT)
                if n >= 2:
                    dve.wait_ge(s_fin, n - 1)
                dve.tensor_tensor_scan(hs[:, n % 2, :], xr[:, n, 0:T], b1[:, n % 2, :], 0.0, ALU.mult, ALU.add).then_inc(s_h, 1)
    V.n += 3 + 2 * KT
    A.n += 3
    k.used += 2


def mla(k, cq, ckv, kpe, y):
    nc = k.nc
    with ExitStack() as ctx:
        def sb(name, shape, dt=F32):
            return ctx.enter_context(nc.sbuf_tensor(name, shape, dt))
        q = sb("mla_q", [P, MH + MH // 2, T])
        kn = sb("mla_k", [P, MH, T])
        v = sb("mla_v", [P, 2, D])
        kr = sb("mla_kr", [P, T])
        cs = sb("mla_cs", [P, 2, T])
        cn = sb("mla_cn", [P, QL, T])
        kvn = sb("mla_kvn", [P, KVL, T])
        cnp = sb("mla_cnh", [P, QL, T], F32R), sb("mla_cnl", [P, QL, T], F32R)
        kvp = sb("mla_kvh", [P, KVL, T], F32R), sb("mla_kvl", [P, KVL, T], F32R)
        q_parts = norm(k, cq, QL, VEC_AT["mla_q_norm_2"], cn, QL * P, times=MLA_SCALE, pair=cnp)
        kv_parts = norm(k, ckv, KVL, VEC_AT["mla_kv_norm_2"], kvn, KVL * P, pair=kvp, slot=1)
        linear(k, cnp, QL, MH + MH // 2, dve_out=store_to(q), parts=(q_parts,))
        linear(k, kvp, KVL, MH, dve_out=store_to(kn), parts=(kv_parts,))
        token_major(k, [(kvp, v)], KVL)
        rope(k, q, kpe, kr, cs)
        mla_attend(k, q, kn, kr, v, y)


def rope(k, q, kpe, kr, cs):
    nc = k.nc
    C1 = 6.28125
    C2 = 2 * math.pi - C1
    V, A = k.s5v, k.s5a
    with ExitStack() as ctx:
        def sb(name, shape, dt=F32):
            return ctx.enter_context(nc.sbuf_tensor(name, shape, dt))
        posi = sb("rope_pos", [P, T], I32)
        w = sb("rope_w", [P, 5, T])
        pr = sb("rope_pr", [P, 2, 2, T])
        v0, a0, i0 = V.n, A.n, k.side_here.n
        block = ctx.enter_context(nc.Block())
        tiles_ = [(q[:, MH + j, :], q[:, MH + j, :]) for j in range(MH // 2)] + [(kpe[:, :], kr[:, :])]

        @block.sync
        def _(sp):
            sp.dma_start(posi[:, :], k.ins["positions"].broadcast_to([P, T])).then_inc(k.side_here.s, 16)

        @block.tensor
        def _(pe):
            for j, (x, _) in enumerate(tiles_):
                if j >= 2:
                    pe.wait_ge(k.rope_out.s, j - 1)
                pe.matmul(k.ps[:, j % 2, 0:T], const(k, "rope_swap"), x, start=True, stop=True).then_inc(k.rope_sw.s, 1)

        @block.scalar
        def _(act):
            act.wait_ge(V.s, v0 + 7)
            act.activation(w[:, 3, :], w[:, 2, :], ACT.Abs).then_inc(A.s, 1)
            act.activation(cs[:, 1, :], w[:, 2, :], ACT.Sin).then_inc(A.s, 1)
            act.wait_ge(A.s, a0 + 1)
            act.activation(cs[:, 0, :], w[:, 3, :], ACT.Sin, scale=-1.0, bias=k.half_pi[:, 0:1]).then_inc(A.s, 1)

        @block.vector
        def _(dve):
            cnt = [v0]

            def tick(ins):
                cnt[0] += 1
                ins.then_inc(V.s, 1)
                dve.wait_ge(V.s, cnt[0])
            dve.wait_ge(k.side_here.s, i0 + 16)
            tick(dve.tensor_copy(w[:, 0, :], posi[:, :]))
            tick(dve.tensor_scalar(w[:, 1, :], w[:, 0, :], const(k, "inv_freq"), None, ALU.mult))
            tick(dve.tensor_scalar(w[:, 2, :], w[:, 1, :], 1.0 / (2 * math.pi), ROUND, ALU.mult, ALU.add))
            tick(dve.tensor_scalar(w[:, 4, :], w[:, 2, :], -ROUND, None, ALU.add))
            tick(dve.scalar_tensor_tensor(w[:, 0, :], w[:, 4, :], -C1, w[:, 1, :], ALU.mult, ALU.add))
            tick(dve.scalar_tensor_tensor(w[:, 1, :], w[:, 4, :], -C2, w[:, 0, :], ALU.mult, ALU.add))
            tick(dve.tensor_scalar(w[:, 2, :], w[:, 1, :], 3.1415925, -3.1415925, ALU.min, ALU.max))
            dve.wait_ge(A.s, a0 + 3)
            for j, (x, out) in enumerate(tiles_):
                dve.wait_ge(k.rope_sw.s, j + 1)
                dve.tensor_tensor(pr[:, j % 2, 0, :], x, cs[:, 0, :], ALU.mult)
                dve.tensor_tensor(pr[:, j % 2, 1, :], k.ps[:, j % 2, 0:T], cs[:, 1, :], ALU.mult).then_inc(k.rope_out.s, 1)
                dve.wait_ge(k.rope_out.s, j + 1)
                dve.tensor_tensor(out, pr[:, j % 2, 0, :], pr[:, j % 2, 1, :], ALU.add)
            V.n = cnt[0]
        A.n += 3
        k.side_here.n += 16


def mla_attend(k, q, kn, kr, v, y):
    nc = k.nc
    with ExitStack() as ctx:
        def sb(name, shape, dt=F32):
            return ctx.enter_context(nc.sbuf_tensor(name, shape, dt))
        sc = sb("ma_scores", [P, 2, T])
        pr = sb("ma_probs", [P, 2, T])
        pt = sb("ma_probs_t", [P, 2, T])
        st = sb("ma_stats", [P, 2, 4])
        dg = sb("ma_diag", [P, 2, P])
        steps = [(h, a) for h in range(MH) for a in range(2)]
        N = len(steps)
        at = {"sc": k.at_sc, "max": k.at_max, "neg": k.at_neg, "exp": k.at_exp, "rd": k.at_rd, "diag": k.at_diag,
              "tr": k.at_tr, "cp": k.at_cp, "pv": k.at_pv, "o": k.at_o}
        s_ = {name: one.s for name, one in at.items()}
        b_ = {name: one.n for name, one in at.items()}
        block = ctx.enter_context(nc.Block())

        @block.tensor
        def _(pe):
            def scores(i):
                h, a = steps[i]
                p0, n = 64 * (h % 2), (a + 1) * P
                if i >= 3:
                    pe.wait_ge(s_["max"], b_["max"] + i - 2)
                pe.matmul(k.ps[:, SCORE_BANKS[i % 3], 0:n], q[:, h, a * P:(a + 1) * P], kn[:, h, 0:n], start=True, stop=False)
                pe.matmul(k.ps[:, SCORE_BANKS[i % 3], 0:n], q[p0:p0 + 64, MH + h // 2, a * P:(a + 1) * P], kr[p0:p0 + 64, 0:n],
                          start=False, stop=True, tile_position=(p0, 0)).then_inc(s_["sc"], 1)

            def transposed(i):
                h, a = steps[i]
                pe.wait_ge(s_["diag"], b_["diag"] + i + 1)
                if i >= 2:
                    pe.wait_ge(s_["cp"], b_["cp"] + i - 1)
                for j in range(a + 1):
                    mm = pe.matmul(k.ps[:, 2 + i % 2, j * P:(j + 1) * P], pr[:, i % 2, j * P:(j + 1) * P], dg[:, i % 2, :],
                                   start=True, stop=True)
                mm.then_inc(s_["tr"], 1)

            def values(i):
                h, a = steps[i]
                pe.wait_ge(s_["cp"], b_["cp"] + i + 1)
                if a == 0 and h >= 2:
                    pe.wait_ge(s_["o"], b_["o"] + h - 1)
                for j in range(a + 1):
                    mm = pe.matmul(k.ps[:, 4 + h % 2, a * P:(a + 1) * P], v[:, j, h * P:(h + 1) * P],
                                   pt[:, i % 2, j * P:(j + 1) * P], start=(j == 0), stop=(j == a))
                mm.then_inc(s_["pv"], 1)
            scores(0)
            scores(1)
            scores(2)
            for i in range(N):
                transposed(i)
                if i + 3 < N:
                    scores(i + 3)
                if i > 0:
                    values(i - 1)
            values(N - 1)

        @block.vector
        def _(dve):
            mask = const(k, "causal")

            def masked(i):
                h, a = steps[i]
                n = (a + 1) * P
                dve.wait_ge(s_["sc"], b_["sc"] + i + 1)
                if i >= 2:
                    dve.wait_ge(s_["exp"], b_["exp"] + i - 1)
                dve.tensor_tensor(sc[:, i % 2, 0:n], k.ps[:, SCORE_BANKS[i % 3], 0:n], mask[:, T - n:T], ALU.add).then_inc(s_["max"], 1)
                dve.wait_ge(s_["max"], b_["max"] + i + 1)
                dve.tensor_reduce(st[:, i % 2, 1:2], sc[:, i % 2, 0:n], op=ALU.max, axis=AX.X, negate=True).then_inc(s_["neg"], 1)

            def head_out(h):
                dve.wait_ge(s_["pv"], b_["pv"] + 2 * (h + 1))
                dve.tensor_copy(y[:, KT + h, :], k.ps[:, 4 + h % 2, 0:T]).then_inc(s_["o"], 1)
            masked(0)
            for i in range(N):
                if i + 1 < N:
                    masked(i + 1)
                dve.wait_ge(s_["exp"], b_["exp"] + i + 1)
                dve.reciprocal(st[:, i % 2, 3:4], st[:, i % 2, 2:3]).then_inc(s_["rd"], 1)
                dve.wait_ge(s_["rd"], b_["rd"] + i + 1)
                if i >= 2:
                    dve.wait_ge(s_["tr"], b_["tr"] + i - 1)
                dve.tensor_scalar(dg[:, i % 2, :], const(k, "ident"), st[:, i % 2, 3:4], None, ALU.mult).then_inc(s_["diag"], 1)
                h, a = steps[i]
                if a == 0 and h > 0:
                    head_out(h - 1)
            head_out(MH - 1)

        @block.scalar
        def _(act):
            def copied(i):
                n = (steps[i][1] + 1) * P
                act.wait_ge(s_["tr"], b_["tr"] + i + 1)
                if i >= 2:
                    act.wait_ge(s_["pv"], b_["pv"] + i - 1)
                act.activation(pt[:, i % 2, 0:n], k.ps[:, 2 + i % 2, 0:n], ACT.Copy).then_inc(s_["cp"], 1)
            for i in range(N):
                n = (steps[i][1] + 1) * P
                act.wait_ge(s_["neg"], b_["neg"] + i + 1)
                if i >= 2:
                    act.wait_ge(s_["tr"], b_["tr"] + i - 1)
                    act.wait_ge(s_["rd"], b_["rd"] + i - 1)
                act.activation(pr[:, i % 2, 0:n], sc[:, i % 2, 0:n], ACT.Exp, bias=st[:, i % 2, 1:2],
                               accum_out=st[:, i % 2, 2:3]).then_inc(s_["exp"], 1)
                if i > 0:
                    copied(i - 1)
            copied(N - 1)



GH = 16
GC = 64
LEVELS = 6


def gdn(k):
    nc = k.nc
    with ExitStack() as ctx:
        def sb(name, shape, dt=F32):
            return ctx.enter_context(nc.sbuf_tensor(name, shape, dt))
        z = sb("gdn_z", [P, GH, T])
        wba = z[:, 0, :].rearrange("p (k n) -> p k n", k=KT)
        par = z[:, 1, 0:2 * GH].rearrange("p (a n) -> p a n", a=2)

        def side(sp):
            sp.dma_start(z[:, 0, :], k.ins["gdn_ba"]).then_inc(k.side_here.s, 16)
            sp.dma_start(par[:, 0, :], k.ins["gdn_a_log"].broadcast_to([P, GH])).then_inc(k.side_here.s, 16)
            sp.dma_start(par[:, 1, :], k.ins["gdn_dt_bias"].broadcast_to([P, GH])).then_inc(k.side_here.s, 16)
        parts = norm(k, k.x, KT, VEC_AT["norm_mix_pre_2"] + KT, k.h, D, pair=k.hp, side=side)
        col = sb("gdn_col", [P, 2, 6, GH])
        qk = sb("gdn_qk", [P, GH, T])
        v = sb("gdn_v", [P, GH, T])
        conv_silu(k, qk, v, parts)
        gdn_gates(k, col, wba, par)

        def silu_out(act, n, ps):
            return act.activation(tile_of(z, n), ps, ACT.Silu)
        with nc.sbuf_tensor("l2_sq", [P, 2, 2 * T], F32) as sq, nc.sbuf_tensor("l2_rt", [P, 2, 2 * T], F32) as rt, \
                nc.sbuf_tensor("l2_inv", [P, 2, 2 * T], F32) as inv:
            linear(k, k.hp, KT, GH, act_out=silu_out, beside=L2Norms(k, qk, sq, rt, inv).beside)
        delta_rule(k, col, qk, v)
        head_norms(k, v, z)
        with nc.sbuf_tensor("gdn_m", [P, KT, T], F32) as m, nc.sbuf_tensor("gdn_vh", [P, 2 * KT, T], F32R) as vh, \
                nc.sbuf_tensor("gdn_vl", [P, 2 * KT, T], F32R) as vl:
            linear(k, (vh, vl), 2 * KT, KT, dve_out=store_to(m), parts=(Parts(k, v, (vh, vl), 2 * KT),))
            post_norm(k, m, VEC_AT["norm_mix_post_2"] + KT)


def gdn_gates(k, col, wba, par):
    nc = k.nc
    V, A = k.s5v, k.s5a
    with ExitStack() as ctx:
        def sb(name, shape, dt=F32):
            return ctx.enter_context(nc.sbuf_tensor(name, shape, dt))
        zz = sb("gg_z", [P, 2, 2, GH])
        e = sb("gg_e", [P, 4, 2, 2, GH])
        ea = sb("gg_ea", [P, GH])
        t0 = sb("gg_t", [P, 2, 2, GH])
        v0, a0, i0 = V.n, A.n, k.side_here.n
        block = ctx.enter_context(nc.Block())

        @block.tensor
        def _(pe):
            pe.wait_ge(k.side_here.s, i0 + 48)
            for a in range(2):
                for j in range(KT):
                    mm = pe.matmul(k.ps[:, a, 0:2 * GH], k.h[:, j, a * P:(a + 1) * P], wba[:, j, :], start=(j == 0), stop=(j == KT - 1))
            mm.then_inc(k.gg_ba.s, 1)
            pe.wait_ge(k.gg_g.s, 1)
            for a in range(2):
                pe.matmul(k.ps[:, 2 + a, 0:GH], const(k, "cumulate")[:, 0:P], col[:, a, 4, :], start=True, stop=True)
                mm = pe.matmul(k.ps[:, 4 + a, 0:GH], const(k, "chunk_sum"), col[:, a, 4, :], start=True, stop=True)
            mm.then_inc(k.gg_gc.s, 1)

        @block.scalar
        def _(act):
            act.wait_ge(k.side_here.s, i0 + 48)
            act.activation(ea[:, :], par[:, 0, :], ACT.Exp).then_inc(A.s, 1)
            act.wait_ge(V.s, v0 + 4)
            act.activation(e[:, 0, :, :, :], zz[:, :, :, :], ACT.Abs).then_inc(A.s, 1)
            act.wait_ge(A.s, a0 + 2)
            act.activation(e[:, 1, :, :, :], e[:, 0, :, :, :], ACT.Exp, scale=-1.0).then_inc(A.s, 1)
            act.wait_ge(A.s, a0 + 3)
            act.activation(e[:, 2, :, :, :], e[:, 1, :, :, :], ACT.Ln, bias=k.one_c[:, 0:1]).then_inc(A.s, 1)
            act.wait_ge(V.s, v0 + 9)
            act.activation(col[:, :, 0, :], col[:, :, 5, :], ACT.Exp).then_inc(A.s, 1)
            act.wait_ge(V.s, v0 + 12)
            act.activation(col[:, :, 2, :], t0[:, :, 0, :], ACT.Exp)
            act.activation(col[:, :, 3, :], t0[:, :, 1, :], ACT.Exp)

        @block.vector
        def _(dve):
            cnt = [v0]

            def tick(ins):
                cnt[0] += 1
                ins.then_inc(V.s, 1)
                dve.wait_ge(V.s, cnt[0])
            dve.wait_ge(k.gg_ba.s, 1)
            for a in range(2):
                tick(dve.tensor_scalar(zz[:, a, 0, :], k.ps[:, a, 0:GH], -1.0, None, ALU.mult))
                tick(dve.tensor_tensor(zz[:, a, 1, :], k.ps[:, a, GH:2 * GH], par[:, 1, :], ALU.add))
            tick(dve.tensor_scalar(e[:, 3, :, :, :], zz[:, :, :, :], 0.0, None, ALU.max))
            dve.wait_ge(A.s, a0 + 4)
            tick(dve.tensor_tensor(e[:, 0, :, :, :], e[:, 3, :, :, :], e[:, 2, :, :, :], ALU.add))
            for a in range(2):
                dve.scalar_tensor_tensor(col[:, a, 4, :], e[:, 0, a, 1, :], -1.0, ea[:, :], ALU.mult, ALU.mult)\
                   .then_inc(V.s, 1)
                cnt[0] += 1
            tick(dve.tensor_scalar(col[:, :, 5, :], e[:, 0, :, 0, :], -1.0, None, ALU.mult))
            dve.sem_inc(k.gg_g.s, 1)
            dve.wait_ge(k.gg_gc.s, 1)
            tick(dve.tensor_scalar(col[:, :, 1, :], k.ps[:, 2:4, 0:GH], -1.0, None, ALU.mult))
            tick(dve.tensor_tensor(t0[:, :, 0, :], col[:, :, 5, :], col[:, :, 1, :], ALU.subtract))
            tick(dve.tensor_tensor(t0[:, :, 1, :], k.ps[:, 4:6, 0:GH], col[:, :, 1, :], ALU.add))
            V.n = cnt[0]
        A.n += 5
        k.side_here.n += 48


def conv_silu(k, qk, v, parts):
    first = k.used
    nt = 2 * GH
    V = k.s5v
    with k.nc.sbuf_tensor("conv_acc", [P, 2, T], F32) as acc, k.nc.Block() as block:
        v0 = V.n

        @block.sync
        def _(sp):
            loads(k, sp, first, nt)

        @block.tensor
        def _(pe):
            w = Weights(k, pe, first)
            for n in range(nt):
                if n >= 4:
                    pe.wait_ge(V.s, v0 + 4 * (n - 3))
                for j in range(KT):
                    if n == 0:
                        parts.here(pe, j)
                    mm = product(pe, k.ps[:, n % 4, 0:T], w.tile(n * ITEM + j), pair_tile(k.hp, j), start=(j == 0), stop=(j == KT - 1))
                mm.then_inc(k.item_used, 1)

        @block.vector
        def _(dve):
            parts.vector(dve)
            for n in range(nt):
                dve.wait_ge(k.item_used, first + n + 1)
                if n >= 2:
                    dve.wait_ge(k.cv_silu.s, n - 1)
                for s in range(4):
                    c = VEC_AT["gdn_conv_w_2"] + nt * (3 - s) + n
                    wc = k.vec[:, c:c + 1]
                    if s == 0:
                        ins = dve.tensor_scalar(acc[:, n % 2, :], k.ps[:, n % 4, 0:T], wc, None, ALU.mult)
                    else:
                        ins = dve.scalar_tensor_tensor(acc[:, n % 2, s:T], k.ps[:, n % 4, 0:T - s], wc, acc[:, n % 2, s:T],
                                                       ALU.mult, ALU.add)
                    ins.then_inc(V.s, 1)
                    if s < 3:
                        dve.wait_ge(V.s, v0 + 4 * n + s + 1)

        @block.scalar
        def _(act):
            parts.scalar(act)
            for n in range(nt):
                act.wait_ge(V.s, v0 + 4 * (n + 1))
                dst = qk[:, n, :] if n < GH else v[:, n - GH, :]
                act.activation(dst, acc[:, n % 2, :], ACT.Silu).then_inc(k.cv_silu.s, 1)
                round_item(k, act, first + n)

        @block.gpsimd
        def _(pool):
            parts.gpsimd(pool)
            for n in range(nt):
                cut_item(k, pool, first + n)
    V.n += 4 * nt
    k.used += nt


class L2Norms:

    def __init__(self, k, qk, sq, rt, inv):
        self.k, self.qk, self.sq, self.rt, self.inv = k, qk, sq, rt, inv
        self.base = k.sq_done.n, k.sum_done.n, k.root_done.n, k.norm_done.n, k.mul_done.n
        advance((k.sq_done, k.sum_done, k.root_done, k.norm_done, k.mul_done), KT)

    def tiles(self, n):
        return self.qk[:, 2 * n:2 * n + 2, :].rearrange("p a n -> p (a n)")

    def beside(self, name, engine, b):
        n = b // 2
        if name == "tensor" and b % 2:
            self.tensor(engine, n)
        elif name == "scalar":
            (self.root if b % 2 else self.square)(engine, n)
        elif name == "vector" and b % 2:
            self.vector(engine, n)
        elif name == "gpsimd" and b % 2:
            self.gpsimd(engine, n)

    def tensor(self, pe, n):
        k, (b_sq, b_ss, b_rt, b_inv, b_m) = self.k, self.base
        pe.wait_ge(k.sq_done.s, b_sq + n + 1)
        if n >= 2:
            pe.wait_ge(k.root_done.s, b_rt + n - 1)
        pe.matmul(k.ps[:, 4 + n % 2, :], k.ones[:, :], self.sq[:, n % 2, :], start=True, stop=True).then_inc(k.sum_done.s, 1)

    def square(self, act, n):
        k, (b_sq, b_ss, b_rt, b_inv, b_m) = self.k, self.base
        if n >= 2:
            act.wait_ge(k.sum_done.s, b_ss + n - 1)
        act.activation(self.sq[:, n % 2, :], self.tiles(n), ACT.Square).then_inc(k.sq_done.s, 1)

    def root(self, act, n):
        k, (b_sq, b_ss, b_rt, b_inv, b_m) = self.k, self.base
        act.wait_ge(k.sum_done.s, b_ss + n + 1)
        if n >= 2:
            act.wait_ge(k.norm_done.s, b_inv + n - 1)
        query = n < KT // 2
        act.activation(self.rt[:, n % 2, :], k.ps[:, 4 + n % 2, :], ACT.Sqrt, scale=float(P) if query else 1.0,
                       bias=(k.eps128 if query else k.eps)[:, 0:1]).then_inc(k.root_done.s, 1)

    def vector(self, dve, n):
        k, (b_sq, b_ss, b_rt, b_inv, b_m) = self.k, self.base
        dve.wait_ge(k.root_done.s, b_rt + n + 1)
        if n >= 2:
            dve.wait_ge(k.mul_done.s, b_m + n - 1)
        dve.reciprocal(self.inv[:, n % 2, :], self.rt[:, n % 2, :]).then_inc(k.norm_done.s, 1)

    def gpsimd(self, pool, n):
        k, (b_sq, b_ss, b_rt, b_inv, b_m) = self.k, self.base
        pool.wait_ge(k.norm_done.s, b_inv + n + 1)
        pool.tensor_tensor(self.tiles(n), self.tiles(n), self.inv[:, n % 2, :], ALU.mult).then_inc(k.mul_done.s, 1)


def head_norms(k, o, z):
    with k.nc.sbuf_tensor("hn_sq", [P, 2, 2 * T], F32) as sq, k.nc.sbuf_tensor("hn_rt", [P, 2, 2 * GH], F32) as rt, \
            k.nc.sbuf_tensor("hn_inv", [P, 4, 2 * T], F32) as inv, k.nc.Block() as block:
        b_sq, b_ss, b_rt, b_inv = k.sq_done.n, k.sum_done.n, k.root_done.n, k.norm_done.n
        gain = k.vec[:, VEC_AT["gdn_norm_2"]:VEC_AT["gdn_norm_2"] + 1]
        ident = const(k, "ident")

        def pair(t3, n):
            return t3[:, 2 * n:2 * n + 2, :].rearrange("p a n -> p (a n)")

        @block.tensor
        def _(pe):
            for n in range(KT):
                pe.wait_ge(k.sq_done.s, b_sq + n + 1)
                for c in range(4):
                    mm = pe.matmul(k.ps[:, 7, 4 * n + c:4 * n + c + 1], sq[:, n % 2, c * P:(c + 1) * P], k.ones[:, 0:1],
                                   start=True, stop=True)
                mm.then_inc(k.sum_done.s, 1)
            pe.wait_ge(k.hn_inv.s, 1)
            for n in range(KT):
                if n >= 4:
                    pe.wait_ge(k.norm_done.s, b_inv + n - 3)
                for c in range(4):
                    mm = pe.matmul(k.ps[:, n % 4, c * P:(c + 1) * P], spread(rt[:, 1, 4 * n + c:4 * n + c + 1], 1, P), ident,
                                   start=True, stop=True)
                mm.then_inc(k.hn_rows.s, 1)

        @block.scalar
        def _(act):
            for n in range(KT):
                if n >= 2:
                    act.wait_ge(k.sum_done.s, b_ss + n - 1)
                act.activation(sq[:, n % 2, :], pair(o, n), ACT.Square).then_inc(k.sq_done.s, 1)
            act.wait_ge(k.sum_done.s, b_ss + KT)
            act.activation(rt[:, 0, :], k.ps[:, 7, 0:2 * GH], ACT.Sqrt, scale=1.0 / P, bias=k.eps[:, 0:1])\
               .then_inc(k.root_done.s, 1)

        @block.vector
        def _(dve):
            dve.wait_ge(k.root_done.s, b_rt + 1)
            dve.reciprocal(rt[:, 1, :], rt[:, 0, :]).then_inc(k.hn_inv.s, 1)
            for n in range(KT):
                dve.wait_ge(k.hn_rows.s, n + 1)
                if n >= 4 and n % 2:
                    dve.wait_ge(k.hn_pool.s, n // 2 - 1)
                dve.scalar_tensor_tensor(inv[:, n % 4, :], pair(z, n), gain, k.ps[:, n % 4, :], ALU.mult, ALU.mult)\
                   .then_inc(k.norm_done.s, 1)
                if n % 2 == 0:
                    dve.wait_ge(k.norm_done.s, b_inv + n + 1)
                    dve.tensor_tensor(pair(o, n), pair(o, n), inv[:, n % 4, :], ALU.mult)

        @block.gpsimd
        def _(pool):
            for n in range(1, KT, 2):
                pool.wait_ge(k.norm_done.s, b_inv + n + 1)
                pool.tensor_tensor(pair(o, n), pair(o, n), inv[:, n % 4, :], ALU.mult).then_inc(k.hn_pool.s, 1)
    for s in (k.sq_done, k.sum_done, k.norm_done):
        s.n += KT
    k.root_done.n += 1


def delta_rule(k, col, qk, v):
    nc = k.nc
    HG = 4
    NG = GH // HG
    with ExitStack() as ctx:
        def sb(name, shape, dt=F32):
            return ctx.enter_context(nc.sbuf_tensor(name, shape, dt))
        ktok = sb("dr_ktok", [P, 2, 2, P])
        bv = sb("dr_bv", [P, 2, HG, P])
        E = sb("dr_e", [P, 2, HG, 2, P])
        kbg, kdec = E[:, :, :, 0, :], E[:, :, :, 1, :]
        AQ = sb("dr_aq", [P, 2, HG, 2, P])
        MT = sb("dr_mt", [P, 2, HG, P])
        X = sb("dr_x", [P, 2, HG, P])
        XT = sb("dr_xt", [P, 2, HG, P])
        Ps = sb("dr_ps", [P, 2, HG, P])
        u = sb("dr_u", [P, 2, HG, P])
        wT = sb("dr_wt", [P, 2, HG, P])
        qd = k.h[:, 0:HG, :]
        rx = k.h[:, HG:2 * HG, :]
        S = sb("dr_s", [P, 2, HG, P])
        Sd = k.rs[:, :, :].rearrange("p a n -> p (a n)").rearrange("p (h n) -> p h n", h=HG)
        g = Space()
        g.vt = k.sem("gdn_values_transposed")
        g.kt = k.sem("gdn_keys_transposed")
        g.gq = k.sem("gdn_products_and_rows")
        g.vc = k.sem("gdn_beta_values")
        g.kc = k.sem("gdn_keys_copied")
        g.re = k.sem("gdn_row_exp")
        g.t = k.sem("gdn_rows_masked")
        g.e = k.sem("gdn_decays")
        g.aq = k.sem("gdn_a_and_q")
        g.qd = k.sem("gdn_queries_decayed")
        g.kb = k.sem("gdn_keys_scaled")
        g.kd = k.sem("gdn_keys_scaled_for_state")
        g.mt = k.sem("gdn_level_part")
        g.p = k.sem("gdn_m_x")
        g.pc = k.sem("gdn_m_x_copied")
        g.px = k.sem("gdn_x_m_x")
        g.x = k.sem("gdn_x_updated")
        g.u = k.sem("gdn_u_in_psum")
        g.w = k.sem("gdn_w_in_psum")
        g.uc = k.sem("gdn_u_copied")
        g.wc = k.sem("gdn_w_copied")
        g.ws = k.sem("gdn_w_state")
        g.vn = k.sem("gdn_u_corrected")
        g.kv = k.sem("gdn_keys_u")
        g.o = k.sem("gdn_chunk_output")
        g.oc = k.sem("gdn_output_copied")
        g.s = k.sem("gdn_state")
        g.sd = k.sem("gdn_state_decayed")
        block = ctx.enter_context(nc.Block())
        ident, cum = const(k, "ident"), const(k, "cumulate")
        lmask = const(k, "levels").rearrange("p (l n) -> p l n", l=LEVELS)
        dmask = const(k, "decay_mask")
        levels = range(1, LEVELS + 1)

        def four(bank):
            return k.ps[:, bank, :].rearrange("p (h n) -> p h n", h=HG)

        def q_of(hg, kh):
            return qk[:, 2 * hg + kh, :]

        def k_of(hg, kh):
            return qk[:, KT + 2 * hg + kh, :]

        @block.tensor
        def _(pe):
            for hg in range(NG):
                U = 2 * hg
                for a in range(2):
                    rows = slice(a * P, (a + 1) * P)
                    if a == 0 and hg:
                        pe.wait_ge(g.oc, 4 * hg)
                    for kh in range(2):
                        for half, rhs in enumerate((k_of(hg, kh), q_of(hg, kh))):
                            pe.matmul(k.ps[:, a, (2 * kh + half) * P:(2 * kh + half + 1) * P], k_of(hg, kh)[:, rows], rhs[:, rows],
                                      start=True, stop=True)
                    for hh in range(HG):
                        h = HG * hg + hh
                        bank, c = 2 + 2 * a + hh // 2, hh % 2 * 2 * P
                        pe.matmul(k.ps[:, bank, c:c + 2 * P], spread(col[:, a, 4, h:h + 1], 1, P), cum, start=True, stop=True)
                        mm = pe.matmul(k.ps[:, bank, c:c + P], spread(col[:, a, 5, h:h + 1], 1, P), ident, start=False, stop=True,
                                       skip_group_check=True)
                    mm.then_inc(g.gq, 1)
                for a in range(2):
                    rows = slice(a * P, (a + 1) * P)
                    if a == 1:
                        pe.wait_ge(g.vc, U + 1)
                        pe.wait_ge(g.kc, U + 1)
                    elif hg:
                        pe.wait_ge(g.uc, U)
                        pe.wait_ge(g.wc, U)
                    for hh in range(HG):
                        mm = pe.transpose(k.ps[:, 6, hh * P:(hh + 1) * P], v[:, HG * hg + hh, rows], ident)
                    mm.then_inc(g.vt, 1)
                    for kh in range(2):
                        mm = pe.transpose(k.ps[:, 7, kh * P:(kh + 1) * P], k_of(hg, kh)[:, rows], ident)
                    mm.then_inc(g.kt, 1)
                for l in levels:
                    for a in range(2):
                        pe.wait_ge(g.mt, 12 * hg + 2 * (l - 1) + a + 1)
                        if l > 1:
                            pe.wait_ge(g.x, 12 * hg + 2 * (l - 2) + a + 1)
                        for hh in range(HG):
                            mm = pe.matmul(k.ps[:, a, hh * P:(hh + 1) * P], MT[:, a, hh, :], ident if l == 1 else X[:, a, hh, :],
                                           start=True, stop=True)
                        mm.then_inc(g.p, 1)
                    if l > 1:
                        for a in range(2):
                            pe.wait_ge(g.pc, 10 * hg + 2 * (l - 2) + a + 1)
                            if l == 2:
                                pe.wait_ge(g.re, U + a + 1)
                            for hh in range(HG):
                                cols = slice(hh * P, (hh + 1) * P)
                                if l < LEVELS:
                                    pe.matmul(k.ps[:, 2 + 2 * a, cols], XT[:, a, hh, :], Ps[:, a, hh, :], start=True, stop=True)
                                mm = pe.matmul(k.ps[:, 3 + 2 * a, cols], Ps[:, a, hh, :], XT[:, a, hh, :], start=True, stop=True)
                            mm.then_inc(g.px, 1)
                for a in range(2):
                    pe.wait_ge(g.x, 12 * hg + 2 * (LEVELS - 1) + a + 1)
                    pe.wait_ge(g.kb, U + a + 1)
                    if a == 0:
                        pe.wait_ge(g.vc, U + 2)
                        pe.wait_ge(g.kc, U + 2)
                    else:
                        pe.wait_ge(g.uc, U + 1)
                        pe.wait_ge(g.wc, U + 1)
                    for hh in range(HG):
                        mm = pe.matmul(k.ps[:, 6, hh * P:(hh + 1) * P], XT[:, a, hh, :], bv[:, a, hh, :], start=True, stop=True)
                    mm.then_inc(g.u, 1)
                    for hh in range(HG):
                        mm = pe.matmul(k.ps[:, 7, hh * P:(hh + 1) * P], kbg[:, a, hh, :], XT[:, a, hh, :], start=True, stop=True)
                    mm.then_inc(g.w, 1)
                for n in range(4):
                    a, p0 = n // 2, GC * (n % 2)
                    part = slice(p0, p0 + GC)
                    if n == 0:
                        pe.wait_ge(g.uc, U + 2)
                        pe.wait_ge(g.wc, U + 2)
                        pe.wait_ge(g.qd, U + 2)
                        pe.wait_ge(g.kd, U + 2)
                    else:
                        pe.wait_ge(g.s, 3 * hg + n)
                        for hh in range(HG):
                            mm = pe.matmul(k.ps[part, n % 2, hh * P:(hh + 1) * P], wT[:, a, hh, part], S[:, n % 2, hh, :],
                                           start=True, stop=True, tile_position=(0, p0))
                        mm.then_inc(g.ws, 1)
                        pe.wait_ge(g.vn, 3 * hg + n)
                    if n < 3:
                        for hh in range(HG):
                            mm = pe.matmul(k.ps[:, 4 + n % 2, hh * P:(hh + 1) * P], kdec[part, a, hh, :], u[part, a, hh, :],
                                           start=True, stop=True, tile_position=(p0, 0))
                        mm.then_inc(g.kv, 1)
                    if n >= 2:
                        pe.wait_ge(g.oc, 4 * hg + n - 1)
                    for hh in range(HG):
                        out = k.ps[:, 2 + n % 2, hh * GC:(hh + 1) * GC]
                        if n:
                            pe.matmul(out, S[:, n % 2, hh, :], qd[:, hh, n * GC:(n + 1) * GC], start=True, stop=False)
                        mm = pe.matmul(out, u[part, a, hh, :], AQ[part, a, hh, 1, part], start=(n == 0), stop=True,
                                       tile_position=(p0, 0))
                    mm.then_inc(g.o, 1)

        @block.scalar
        def _(act):
            for hg in range(NG):
                U = 2 * hg
                for a in range(2):
                    act.wait_ge(g.t, U + a + 1)
                    for hh in range(HG):
                        h = HG * hg + hh
                        ins = act.activation(E[:, a, hh, :, :], E[:, a, hh, :, :], ACT.Exp, bias=col[:, a, 1, h:h + 1])
                    ins.then_inc(g.e, 1)
                for a in range(2):
                    rows = slice(a * P, (a + 1) * P)
                    if hg:
                        act.wait_ge(g.qd, U)
                        act.wait_ge(g.sd, 2 * hg)
                    for b in range(2):
                        rows4 = k.ps[:, 2 + 2 * a + b, :].rearrange("p (h c n) -> p h c n", h=2, c=2)
                        ins = act.activation(rx[:, 2 * b:2 * b + 2, rows], rows4[:, :, 1, :], ACT.Exp)
                    ins.then_inc(g.re, 1)
                    act.wait_ge(g.vt, U + a + 1)
                    if hg:
                        act.wait_ge(g.u, U - 1 + a)
                    for hh in range(HG):
                        h = HG * hg + hh
                        ins = act.activation(bv[:, a, hh, :], k.ps[:, 6, hh * P:(hh + 1) * P], ACT.Copy, scale=col[:, a, 0, h:h + 1])
                    ins.then_inc(g.vc, 1)
                    act.wait_ge(g.kt, U + a + 1)
                    if hg:
                        act.wait_ge(g.kd, U - 1 + a)
                    act.activation(ktok[:, a, :, :], k.ps[:, 7, 0:2 * P].rearrange("p (h n) -> p h n", h=2), ACT.Copy).then_inc(g.kc, 1)
                for l in levels:
                    if l > 1:
                        for a in range(2):
                            act.wait_ge(g.p, 12 * hg + 2 * (l - 1) + a + 1)
                            if l > 2 or hg:
                                act.wait_ge(g.px, 10 * hg + 2 * (l - 3) + a + 1)
                            act.activation(Ps[:, a, :, :], four(a), ACT.Copy).then_inc(g.pc, 1)
                    if l in (2, 3):
                        a = l - 2
                        act.wait_ge(g.kc, U + a + 1)
                        act.wait_ge(g.aq, U + a + 1)
                        for hh in range(HG):
                            h = HG * hg + hh
                            ins = act.activation(kbg[:, a, hh, :], ktok[:, a, hh // 2, :], ACT.Copy, scale=col[:, a, 2, h:h + 1])
                        ins.then_inc(g.kb, 1)
                for a in range(2):
                    act.wait_ge(g.w, U + a + 1)
                    act.activation(wT[:, a, :, :], four(7), ACT.Copy).then_inc(g.wc, 1)
                for n in range(4):
                    act.wait_ge(g.o, 4 * hg + n + 1)
                    act.activation(v[:, HG * hg:HG * (hg + 1), n * GC:(n + 1) * GC],
                                   k.ps[:, 2 + n % 2, 0:HG * GC].rearrange("p (h n) -> p h n", h=HG), ACT.Copy).then_inc(g.oc, 1)

        @block.vector
        def _(dve):
            for hg in range(NG):
                U = 2 * hg
                for a in range(2):
                    dve.wait_ge(g.gq, U + a + 1)
                    if hg:
                        dve.wait_ge(g.o, 4 * hg)
                    for b in range(2):
                        ins = dve.tensor_tensor(E[:, a, 2 * b:2 * b + 2, :, :].rearrange("p h c n -> p h (c n)"),
                                                k.ps[:, 2 + 2 * a + b, :].rearrange("p (h n) -> p h n", h=2),
                                                spread(dmask.rearrange("p (o n) -> p o n", o=1), 1, 2), ALU.add)
                    ins.then_inc(g.t, 1)
                for a in range(2):
                    dve.wait_ge(g.e, U + a + 1)
                    if hg:
                        dve.wait_ge(g.o, 4 * hg)
                    for kh in range(2):
                        ins = dve.tensor_tensor(AQ[:, a, 2 * kh:2 * kh + 2, :, :].rearrange("p h c n -> p h (c n)"),
                                                E[:, a, 2 * kh:2 * kh + 2, :, :].rearrange("p h c n -> p h (c n)"),
                                                spread(k.ps[:, a, 2 * kh * P:(2 * kh + 2) * P].rearrange("p (o n) -> p o n", o=1), 1, 2),
                                                ALU.mult)
                    ins.then_inc(g.aq, 1)
                    dve.wait_ge(g.aq, U + a + 1)
                    dve.tensor_tensor(MT[:, a, :, :], AQ[:, a, :, 0, :], spread(lmask[:, 0:1, :], 1, HG), ALU.mult).then_inc(g.mt, 1)
                idb = spread(ident.rearrange("p (o n) -> p o n", o=1), 1, HG)
                for l in levels:
                    for a in range(2):
                        if l == 1:
                            dve.wait_ge(g.p, 12 * hg + a + 1)
                            dve.wait_ge(g.mt, 12 * hg + a + 1)
                            dve.tensor_tensor(X[:, a, :, :], idb, four(a), ALU.subtract)
                            dve.tensor_tensor(XT[:, a, :, :], idb, MT[:, a, :, :], ALU.subtract).then_inc(g.x, 1)
                        else:
                            dve.wait_ge(g.px, 10 * hg + 2 * (l - 2) + a + 1)
                            if l < LEVELS:
                                dve.tensor_tensor(X[:, a, :, :], X[:, a, :, :], four(2 + 2 * a), ALU.subtract)
                            dve.tensor_tensor(XT[:, a, :, :], XT[:, a, :, :], four(3 + 2 * a), ALU.subtract).then_inc(g.x, 1)
                for a in range(2):
                    dve.wait_ge(g.u, U + a + 1)
                    dve.tensor_copy(u[:, a, :, :], four(6)).then_inc(g.uc, 1)
                for n in range(4):
                    a, p0 = n // 2, GC * (n % 2)
                    part = slice(p0, p0 + GC)
                    if n:
                        dve.wait_ge(g.ws, 3 * hg + n)
                        dve.tensor_tensor(u[part, a, :, :], u[part, a, :, :], four(n % 2)[part, :, :], ALU.subtract).then_inc(g.vn, 1)
                    if n < 3:
                        dve.wait_ge(g.kv, 3 * hg + n + 1)
                        if n == 0:
                            if hg:
                                dve.wait_ge(g.o, 4 * hg)
                            dve.tensor_copy(S[:, 1, :, :], four(4)).then_inc(g.s, 1)
                        else:
                            dve.wait_ge(g.sd, 2 * hg + n)
                            if n == 2:
                                dve.wait_ge(g.o, 4 * hg + 2)
                            dve.tensor_tensor(S[:, (n + 1) % 2, :, :], Sd[:, :, :], four(4 + n % 2), ALU.add).then_inc(g.s, 1)

        @block.gpsimd
        def _(pool):
            for hg in range(NG):
                U = 2 * hg
                for l in levels[1:]:
                    for a in range(2):
                        pool.wait_ge(g.p, 12 * hg + 2 * (l - 2) + a + 1)
                        if l == 2:
                            pool.wait_ge(g.x, 12 * hg + a + 1)
                        pool.tensor_tensor(MT[:, a, :, :], AQ[:, a, :, 0, :], spread(lmask[:, l - 1:l, :], 1, HG), ALU.mult)\
                            .then_inc(g.mt, 1)
                    if l in (2, 3):
                        a = l - 2
                        pool.wait_ge(g.kc, U + a + 1)
                        pool.wait_ge(g.aq, U + a + 1)
                        if hg:
                            pool.wait_ge(g.o, 4 * hg)
                        for hh in range(HG):
                            h = HG * hg + hh
                            ins = pool.tensor_scalar(kdec[:, a, hh, :], ktok[:, a, hh // 2, :], col[:, a, 3, h:h + 1], None, ALU.mult)
                        ins.then_inc(g.kd, 1)
                    if l in (4, 5):
                        a = l - 4
                        rows = slice(a * P, (a + 1) * P)
                        pool.wait_ge(g.re, U + a + 1)
                        for kh in range(2):
                            ins = pool.tensor_tensor(qd[:, 2 * kh:2 * kh + 2, rows], rx[:, 2 * kh:2 * kh + 2, rows],
                                                     spread(q_of(hg, kh)[:, rows].rearrange("p (o n) -> p o n", o=1), 1, 2), ALU.mult)
                        ins.then_inc(g.qd, 1)
                for n in (1, 2):
                    pool.wait_ge(g.s, 3 * hg + n)
                    end = (n + 1) * GC
                    pool.tensor_tensor(Sd[:, :, :], S[:, n % 2, :, :], spread(rx[:, :, end - 1:end], 2, P), ALU.mult).then_inc(g.sd, 1)






def build(nc, ins, x_in, out, plan, n_items):
    k = Space()
    k.nc, k.ins, k.weights = nc, ins, ins["weights"]
    k.items = START + n_items
    k.used = START
    with ExitStack() as ctx:
        k.ctx = ctx

        def sb(name, shape, dt=F32):
            return ctx.enter_context(nc.sbuf_tensor(name, shape, dt))

        def sem(name):
            return ctx.enter_context(nc.semaphore(name))

        def counted(name, n=0):
            return Signal(sem(name), n)

        k.sem = sem
        k.ps = ctx.enter_context(nc.psum_tensor("ps", [P, 8, 512], F32))
        k.raw = sb("raw", [P, RAW, ITEM * P])
        k.hi = sb("hi", [P, CUT, ITEM * P], F32R)
        k.lo = sb("lo", [P, CUT, ITEM * P], F32R)
        k.x = sb("x", [P, KT, T])
        k.h = sb("h", [P, KT, T])
        k.hp = sb("h_high", [P, KT, T], F32R), sb("h_low", [P, KT, T], F32R)
        k.rs = sb("reciprocal_root", [P, 2, T])
        k.root = sb("root", [P, T])
        k.vec = sb("vec", [P, NVEC])
        k.consts = sb("consts", [P, ins["consts"].shape[1]])
        k.ones = sb("ones", [P, P])
        k.eps = sb("eps", [P, 1])
        k.zeros = sb("zeros", [P, 512], mybir.dt.bfloat16)
        k.item_here = [sem(f"item_here_{s}") for s in range(RAW)]
        k.item_rounded = sem("item_rounded")
        k.item_cut = sem("item_cut")
        k.item_used = sem("item_used")
        k.input_here = sem("input_here")
        k.setup_done = sem("setup_done")
        k.stored = sem("stored")
        k.sq_done = counted("squares_done")
        k.sum_done = counted("square_sum_done")
        k.root_done = counted("root_done")
        k.norm_done = counted("norm_done")
        k.act_done = counted("scalar_part_done")
        k.norm_out = counted("norm_tile")
        k.cut_round = counted("high_part")
        k.cut_low = counted("low_part")
        k.dft2_low = counted("token_dft_low_part")
        k.low_even = counted("low_part_even_tile")
        k.low_odd = counted("low_part_odd_tile")
        k.token_out = counted("token_major_first_half_out")
        k.silu_done = counted("silu_done")
        k.mul_done = counted("product_done")
        k.side_here = counted("side_inputs_here")
        k.dft1_done = counted("feature_dft_done")
        k.dft1_out = counted("feature_dft_copied")
        k.dft2_done = counted("token_dft_done")
        k.dft2_out = counted("token_dft_copied")
        k.s5v = counted("s5_vector_steps")
        k.s5a = counted("s5_scalar_steps")
        k.s5_bu = counted("s5_drive_in_psum")
        k.s5_y = counted("s5_output_terms")
        k.s5_ang = counted("s5_fraction_of_turn")
        k.s5_phase = counted("s5_angle_in_turns")
        k.s5_tab = counted("s5_cos_sin_done")
        k.s5_abs = counted("s5_fraction_abs")
        k.s5_free = counted("s5_drive_read")
        k.s5_bm = counted("s5_drive_turned")
        k.s5_scan = counted("s5_scans_done")
        k.s5_prod = counted("s5_products_done")
        k.s5_out = counted("s5_output_tile")
        k.at_sc = counted("attention_scores")
        k.at_max = counted("attention_scores_masked")
        k.at_neg = counted("attention_row_maximum")
        k.at_exp = counted("attention_probabilities")
        k.at_rd = counted("attention_inverse_sum")
        k.at_diag = counted("attention_inverse_sum_diagonal")
        k.at_tr = counted("attention_probabilities_transposed")
        k.at_cp = counted("attention_transposed_copied")
        k.at_pv = counted("attention_values_mixed")
        k.at_o = counted("attention_heads_out")
        k.at_fill = counted("attention_bias_filled")
        k.at_bias = [counted("attention_bias_0"), counted("attention_bias_1")]
        k.bias_ps = counted("bias_in_psum")
        k.bias_tab = counted("bias_table")
        k.bias_written = counted("bias_written")
        k.rg_xc = counted("rg_convolved")
        k.rg_gate = counted("rg_gates_in_psum")
        k.rg_sig = counted("rg_sigmoids")
        k.rg_at = counted("rg_decay")
        k.rg_q = counted("rg_quotient")
        k.rg_root = counted("rg_root")
        k.rg_fin = counted("rg_tile_done")
        k.rg_high = counted("rg_convolved_high_part")
        k.rg_tanh = counted("rg_tanh_done")
        k.rg_quotient = counted("rg_inverse_done")
        k.rg_input = counted("rg_gated_input")
        k.rg_scanned = counted("rg_scanned")
        k.rope_sw = counted("rope_halves_swapped")
        k.rope_out = counted("rope_products")
        k.gg_ba = counted("gdn_b_a_in_psum")
        k.gg_g = counted("gdn_g_done")
        k.gg_gc = counted("gdn_cumulated")
        k.cv_silu = counted("conv_silu_done")
        k.hn_inv = counted("head_norm_inverse")
        k.hn_rows = counted("head_norm_rows")
        k.hn_pool = counted("head_norm_scaled_by_pool")
        k.eps128 = sb("eps128", [P, 1])
        k.eps192 = sb("eps192", [P, 1])
        k.one_c = sb("one_c", [P, 1])
        k.eps64 = sb("eps64", [P, 1])
        k.half_pi = sb("half_pi", [P, 1])
        k.round_c = sb("round_c", [P, 1])
        k.out_done = counted("output_done", 8)
        k.hidden_done = counted("hidden_done", 8)

        with nc.Block() as block:
            @block.sync
            def _(sp):
                sp.dma_start(k.x[:, :, :], x_in).then_inc(k.input_here, 16)
                sp.dma_start(k.vec[:, :], ins["vec"]).then_inc(k.input_here, 16)
                sp.dma_start(k.consts[:, :], ins["consts"]).then_inc(k.input_here, 16)
                for s in range(RAW):
                    sp.dma_start(k.raw[:, s, :], k.weights[s, :, :]).then_inc(k.item_here[s], 16)
                sp.wait_ge(k.input_here, 48)

            @block.vector
            def _(dve):
                dve.memset(k.ones[:, :], 1.0)
                dve.memset(k.zeros[:, :], 0.0)
                dve.memset(k.eps[:, :], EPS)
                dve.memset(k.eps128[:, :], P * EPS)
                dve.memset(k.eps192[:, :], MLA_SCALE * EPS)
                dve.memset(k.one_c[:, :], 1.0)
                dve.memset(k.eps64[:, :], 64 * EPS)
                dve.memset(k.half_pi[:, :], math.pi / 2)
                dve.memset(k.round_c[:, :], ROUND)
                dve.sem_inc(k.out_done.s, 8)
                dve.sem_inc(k.hidden_done.s, 8)
                dve.sem_inc(k.item_used, START)
                dve.sem_inc(k.item_rounded, START)
                dve.sem_inc(k.item_cut, START)
        plan(k)
        assert k.used == k.items, (k.used, k.items)
        with nc.Block() as block:
            @block.sync
            def _(sp):
                sp.dma_start(out, k.x[:, :, :]).then_inc(k.stored, 16)
                sp.wait_ge(k.stored, 16)


def residual(k):
    def out(dve, n, ps):
        return dve.tensor_tensor(tile_of(k.x, n), tile_of(k.x, n), ps, ALU.add)
    return out


def ffn_first(k, layer):
    parts = norm(k, k.x, KT, VEC_AT["norm_ffn_g"] + KT * layer, k.h, D, pair=k.hp)
    swiglu(k, k.hp, residual(k), parts)


def tiles(w):
    kk, n = w.shape
    return w.reshape(kk // P, P, n // P, P).transpose(0, 2, 1, 3)


def as_items(t):
    return t.reshape(-1, ITEM, P, P).transpose(0, 2, 1, 3).reshape(-1, P, ITEM * P)


def by_output(w):
    t = tiles(w).transpose(1, 0, 2, 3)
    return as_items(t.reshape(-1, P, P))


def by_input(w):
    return as_items(tiles(w).reshape(-1, P, P))


def ffn_items(gate, up, down):
    g, u, d = by_output(gate), by_output(up), by_input(down)
    out = [g[0], u[0]]
    for j in range(FT):
        if j + 1 < FT:
            out += [g[j + 1], u[j + 1]]
        out.append(d[j])
    return np.stack(out)


def vectors(inp):
    cols = []
    for name, n in VECTORS:
        a = np.asarray(inp[name])
        if name in ("attn_q_gain", "attn_k_gain"):
            a = np.concatenate([a.reshape(3, 64), a.reshape(3, 64)], axis=1)
        cols.append(a.reshape(n, P))
    return np.ascontiguousarray(np.concatenate(cols).T)


def qkv_items(w):
    w = w.reshape(D, GROUPS, 3, D)
    parts = [by_output(w[:, g, 0]) for g in range(GROUPS)]
    parts += [by_output(w[:, g, 1]) for g in range(GROUPS)]
    parts += [by_input(w[:, g, 2]) for g in range(GROUPS)]
    return np.concatenate(parts)


def t5_bucket(rel):
    half, max_exact = 16, 8
    n = np.abs(rel)
    sign = (rel > 0).astype(np.int32) * half
    large = max_exact + (np.log(np.maximum(n, 1) / max_exact) / math.log(1024 / max_exact)
                         * (half - max_exact)).astype(np.int32)
    large = np.minimum(large, half - 1)
    return (sign + np.where(n < max_exact, n, large)).astype(np.int32)


def bias_tables():
    onehot = np.zeros((32, GROUPS, 512), np.float32)
    mask = np.full((AH, GROUPS, 512), NEG, np.float32)
    rel = np.arange(-255, 256)
    onehot[t5_bucket(rel), 0, np.arange(511)] = 1
    mask[:, 0, :511][:, np.abs(rel) <= 64] = 0
    step = np.arange(-63, 64)
    for g, stride in ((1, 1), (2, 4)):
        onehot[t5_bucket(4 * step), g, np.arange(127)] = 1
        mask[:, g, :127][:, step % stride == 0] = 0
    return onehot, mask


def hybrid_items(inp):
    w_in = inp["hy_w_in_2"][0]
    w_in = np.concatenate([w_in, w_in[:, -64:]], 1)
    gates = np.stack([inp["rg_gate_a_w_2"][0], inp["rg_gate_x_w_2"][0]], 1).reshape(-1, P, P)
    uq = inp["mla_w_uq_2"][0].reshape(QL * P, MH, 192)
    uq = np.concatenate([uq[:, :, :P].reshape(QL * P, -1), uq[:, :, P:].reshape(QL * P, -1)], 1)
    ukv = inp["mla_w_ukv_2"][0].reshape(KVL * P, MH, 2, P)
    return np.concatenate([by_output(w_in), as_items(gates), by_output(uq),
                           by_output(np.ascontiguousarray(ukv[:, :, 0]).reshape(KVL * P, D)),
                           by_input(np.ascontiguousarray(ukv[:, :, 1]).reshape(KVL * P, D)),
                           by_output(inp["hy_w_out_2"][0])])


def gdn_items(inp):
    w = inp["gdn_w_in_2"][0]
    return np.concatenate([by_output(w[:, :6 * D]), by_output(inp["gdn_w_out_2"][0])])


def gdn_ba(inp):
    return np.ascontiguousarray(inp["gdn_w_in_2"][0][:, 6 * D:].reshape(KT, P, 2 * GH).transpose(1, 0, 2).reshape(P, -1))


def s5_lam(inp):
    def lay(a):
        return a.reshape(2, SG // 2, 2, SN).transpose(2, 3, 0, 1).reshape(P, ST)
    dt = np.repeat(np.asarray(inp["s5_log_dt"])[0][:, :, None], SN, 2)
    return np.ascontiguousarray(np.stack([lay(inp["s5_lambda_re"][0]), lay(inp["s5_lambda_im"][0]), lay(dt)], 1))


def s5_b(inp):
    def lay(a):
        return a[0].reshape(2, KT, KT, SN, SP_).transpose(2, 4, 0, 1, 3).reshape(P, 2 * KT * SN)
    return np.ascontiguousarray(np.concatenate([lay(inp["s5_b_re"]), lay(inp["s5_b_im"])], 1))


def s5_c(inp):
    def lay(a):
        return a[0].reshape(2, SG // 2, 2, SP_, SN).transpose(2, 4, 0, 1, 3).reshape(P, ST * SP_)
    return np.ascontiguousarray(np.concatenate([lay(inp["s5_c_re"]), lay(inp["s5_c_im"])], 1))


def glu_items(w):
    v, g = by_output(w[:, :D]), by_output(w[:, D:])
    return np.stack([g, v], 1).reshape(-1, P, ITEM * P)


def constants():
    i = np.arange(P)
    parts = {}
    parts["ident"] = np.eye(P)
    ang = 2 * np.pi * np.outer(i, i) / P
    parts["dft_feature"] = np.concatenate([np.cos(ang), np.sin(ang)], 1) / math.sqrt(T * P)
    s = np.arange(T)
    angt = 2 * np.pi * (np.outer(s, s) % T) / T
    parts["dft_cos"] = np.cos(angt).reshape(2, P, T).transpose(1, 0, 2).reshape(P, 2 * T)
    parts["dft_nsin"] = -np.sin(angt).reshape(2, P, T).transpose(1, 0, 2).reshape(P, 2 * T)
    parts["time"] = np.broadcast_to(s, (P, T))
    parts["two_heads"] = i[:, None] // 64 == i[None, :] // 64
    parts["rope_swap"] = np.where(i[:, None] == (i[None, :] ^ 32), np.where(i[None, :] % 64 < 32, -1.0, 1.0), 0.0)
    inv = 1.0 / (np.float32(10000.0) ** (np.arange(0, 64, 2, dtype=np.float32) / np.float32(64)))
    parts["inv_freq"] = np.tile(inv.astype(np.float32), 4)[:, None]
    parts["causal"] = np.concatenate([np.zeros((P, P)), np.where(i[None, :] <= i[:, None], 0.0, NEG)], 1)
    chunk = i[:, None] // GC == i[None, :] // GC
    later = i[None, :] >= i[:, None]
    parts["cumulate"] = np.tile(chunk & later, (1, 2))
    parts["chunk_sum"] = chunk
    parts["decay_mask"] = np.where(np.concatenate([chunk & (i[None, :] > i[:, None]), chunk & later], 1), 0.0, NEG)
    parts["levels"] = np.concatenate([(i[:, None] >> l == i[None, :] >> l) & (i[:, None] >> (l - 1) != i[None, :] >> (l - 1))
                                      for l in range(1, LEVELS + 1)], 1)
    parts["b_half"] = np.stack([(i // SP_) % 2 == 0, (i // SP_) % 2 == 1], 1)
    parts["c_half"] = np.stack([i < SN, i >= SN], 1)
    return parts


CONST_AT = {}
_at = 0
for _name, _a in constants().items():
    CONST_AT[_name] = (_at, _at + _a.shape[1])
    _at += _a.shape[1]


def const(k, name):
    a, b = CONST_AT[name]
    return k.consts[:, a:b]


def whole_program(k):
    for layer in range(4):
        if layer in (0, 3):
            norm(k, k.x, KT, VEC_AT["norm_mix_g"] + KT * layer, k.h, D)
            fourier(k, first=layer == 0)
        elif layer == 1:
            s5(k)
        else:
            make_parts(k, norm(k, k.x, KT, VEC_AT["norm_mix_g"] + KT * layer, k.h, D, pair=k.hp))
            attention(k)
        ffn_first(k, layer)
    hybrid(k)
    ffn_second(k, 0)
    gdn(k)
    ffn_second(k, 1)


def all_items(inp):
    def first(layer):
        gu = inp["ffn_w_gate_up"][layer]
        return ffn_items(gu[:, :FF], gu[:, FF:], inp["ffn_w_down"][layer])

    def second(layer):
        return ffn_items(inp["ffn_w_gate_2"][layer], inp["ffn_w_up_2"][layer], inp["ffn_w_down_2"][layer])
    return np.concatenate([
        by_output(inp["fnet_w_out"][0]), first(0),
        glu_items(inp["s5_w_glu"][0]), first(1),
        qkv_items(inp["attn_w_qkv"][0]), by_output(inp["attn_w_o"][0]), first(2),
        by_output(inp["fnet_w_out"][1]), first(3),
        hybrid_items(inp), second(0),
        gdn_items(inp), second(1),
    ])


def kernel(**inputs):
    import concourse.bacc as bacc
    from concourse.bass_utils import run_bass_kernel_spmd

    inp = {name: np.asarray(a) for name, a in inputs.items()}
    onehot, mask = bias_tables()
    arrays = {
        "in_x": np.ascontiguousarray(inp["x"].reshape(T, KT, P).transpose(2, 1, 0)),
        "in_weights": all_items(inp),
        "in_vec": vectors(inp),
        "in_consts": np.concatenate(list(constants().values()), 1).astype(np.float32),
        "in_s5_lam": s5_lam(inp), "in_s5_b": s5_b(inp), "in_s5_c": s5_c(inp),
        "in_bias_onehot": onehot, "in_bias_mask": mask, "in_rel_bias": np.ascontiguousarray(inp["rel_bias"]),
        "in_positions": np.ascontiguousarray(inp["positions_2"]),
        "in_gdn_ba": gdn_ba(inp),
        "in_gdn_a_log": np.ascontiguousarray(inp["gdn_a_log_2"]),
        "in_gdn_dt_bias": np.ascontiguousarray(inp["gdn_dt_bias_2"]),
    }
    nc = bacc.Bacc("TRN2", target_bir_lowering=False, num_devices=1)
    ins = {name[3:]: nc.dram_tensor(name, a.shape, mybir.dt.from_np(a.dtype), kind="ExternalInput").ap()
           for name, a in arrays.items()}
    out = nc.dram_tensor("out", (P, KT, T), F32, kind="ExternalOutput").ap()
    build(nc, ins, ins["x"], out, whole_program, arrays["in_weights"].shape[0])
    r = run_bass_kernel_spmd(nc, [arrays], core_ids=[0])
    return np.ascontiguousarray(r.results[0]["out"].transpose(2, 1, 0)).reshape(1, T, D)
```
